# Optimizing a Trainium2 kernel written in Bass

```python
import jax, jax.numpy as jnp
from jax import lax
import numpy as np
import math

D_MODEL = 1024
BATCH = 1
SEQ = 512
DEPTH = 2

N_MIXERS = 2
EPS = 1e-6
NEG_INF = -1e30
HG_HEADS = 8
HG_DK = 128
HG_DV = D_MODEL // HG_HEADS
HG_CHUNK = 64
NSA_HEADS = 16
NSA_KV = 4
NSA_GROUP = NSA_HEADS // NSA_KV
NSA_HD = D_MODEL // NSA_HEADS
CMP_LEN = 32
CMP_STRIDE = 16
SEL_LEN = 64
SEL_TOPK = 16
WINDOW = 512
Q_BLOCK = 32
FORCED_SCORE = 1e4
D_FF = 2816
CONV_W = 3


def rmsnorm(x, g):
    xf = x.astype(jnp.float32)
    y = xf * lax.rsqrt(jnp.mean(xf * xf, axis=-1, keepdims=True) + EPS)
    return (y * g).astype(x.dtype)

def alibi_slopes(n):
    return jnp.asarray([2.0 ** (-8.0 * (h + 1) / n) for h in range(n)], jnp.float32)

def hgrn2_mixer(h, w_in, w_out, g_norm, lb):
    B, S, _ = h.shape
    fd = HG_HEADS * HG_DK
    proj = h @ w_in
    q, f_pre, i_in, g = jnp.split(proj, [fd, 2 * fd, 2 * fd + D_MODEL], axis=-1)
    f_pre = f_pre.astype(jnp.float32)
    log_f = jnp.log(lb + (1.0 - lb) * jax.nn.sigmoid(f_pre))
    k = (1.0 - lb) * jax.nn.sigmoid(-f_pre)
    n = S // HG_CHUNK

    def chunks(t, d):
        return t.astype(jnp.float32).reshape(B, n, HG_CHUNK, HG_HEADS, d).transpose(1, 0, 3, 2, 4)

    xs = (chunks(q, HG_DK), chunks(k, HG_DK), chunks(i_in, HG_DV), chunks(log_f, HG_DK))
    causal = jnp.tril(jnp.ones((HG_CHUNK, HG_CHUNK), bool))[:, :, None]

    def step(state, inp):
        qc, kc, vc, lfc = inp
        b = jnp.cumsum(lfc, axis=2)
        o_inter = jnp.einsum('bhtk,bhkv->bhtv', qc * jnp.exp(b), state)
        diff = b[:, :, :, None, :] - b[:, :, None, :, :]
        decay = jnp.exp(jnp.where(causal, diff, NEG_INF))
        scores = jnp.einsum('bhtk,bhsk,bhtsk->bhts', qc, kc, decay)
        o_intra = jnp.einsum('bhts,bhsv->bhtv', scores, vc)
        b_last = b[:, :, -1:, :]
        state = state * jnp.exp(b_last[:, :, 0, :, None]) + jnp.einsum(
            'bhsk,bhsv->bhkv', kc * jnp.exp(b_last - b), vc)
        return state, o_inter + o_intra

    s0 = jnp.zeros((B, HG_HEADS, HG_DK, HG_DV), jnp.float32)
    _, o = lax.scan(step, s0, xs)
    o = o.transpose(1, 0, 3, 2, 4).reshape(B, S, HG_HEADS, HG_DV)
    o = rmsnorm(o, g_norm).reshape(B, S, D_MODEL)
    o = o * jax.nn.silu(g.astype(jnp.float32))
    return o.astype(h.dtype) @ w_out

def nsa_mixer(h, w_in, w_out, cmp_pe, cmp_w1, cmp_w2):
    B, S, _ = h.shape
    G, HPG, HD = NSA_KV, NSA_GROUP, NSA_HD
    nc = (S - CMP_LEN) // CMP_STRIDE + 1
    ns = S // SEL_LEN
    k_sel_n = min(SEL_TOPK, ns)
    kvd = G * HD
    split_at = [D_MODEL + j * kvd for j in range(7)]
    q, k_c, v_c, k_s, v_s, k_w, v_w, gate = jnp.split(h @ w_in, split_at, axis=-1)
    q = q.reshape(B, S, G, HPG, HD)
    gate = jax.nn.sigmoid(gate.astype(jnp.float32)).reshape(B, S, G, HPG, 3)

    def kv(t):
        return t.reshape(B, S, G, HD)

    cidx = (np.arange(nc) * CMP_STRIDE)[:, None] + np.arange(CMP_LEN)[None, :]

    def compress(t, pe, w1, w2):
        blocks = kv(t)[:, cidx] + pe[None, None, :, None, :]
        blocks = blocks.transpose(0, 1, 3, 2, 4).reshape(B, nc, G, CMP_LEN * HD)
        return jax.nn.silu(blocks @ w1) @ w2

    kc = compress(k_c, cmp_pe[0], cmp_w1[0], cmp_w2[0])
    vc = compress(v_c, cmp_pe[1], cmp_w1[1], cmp_w2[1])
    cmp_end = jnp.asarray(np.arange(nc) * CMP_STRIDE + CMP_LEN - 1, jnp.int32)
    cmp_mid = jnp.asarray(np.arange(nc) * CMP_STRIDE + (CMP_LEN - 1) / 2.0, jnp.float32)
    ci = np.arange(nc)[:, None] * CMP_STRIDE
    sj = np.arange(ns)[None, :] * SEL_LEN
    overlap = jnp.asarray((ci <= sj + SEL_LEN - 1) & (ci + CMP_LEN - 1 >= sj), jnp.float32)

    ks_blk = kv(k_s).reshape(B, ns, SEL_LEN, G, HD).transpose(0, 3, 1, 2, 4)
    vs_blk = kv(v_s).reshape(B, ns, SEL_LEN, G, HD).transpose(0, 3, 1, 2, 4)
    pad = ((0, 0), (WINDOW, 0), (0, 0), (0, 0))
    kw_pad = jnp.pad(kv(k_w), pad)
    vw_pad = jnp.pad(kv(v_w), pad)

    slopes = alibi_slopes(NSA_HEADS).reshape(G, HPG)
    scale = HD ** -0.5
    blk_ids = jnp.arange(ns)
    bi = jnp.arange(B)[:, None, None, None]
    gi = jnp.arange(G)[None, :, None, None]

    def block(i):
        q0 = i * Q_BLOCK
        t = q0 + jnp.arange(Q_BLOCK)
        qb = lax.dynamic_slice_in_dim(q, q0, Q_BLOCK, axis=1)
        gb = lax.dynamic_slice_in_dim(gate, q0, Q_BLOCK, axis=1)
        s_c = jnp.einsum('bqghd,bngd->bghqn', qb, kc, preferred_element_type=jnp.float32) * scale
        dist_c = t[:, None].astype(jnp.float32) - cmp_mid[None, :]
        s_c = s_c - slopes[None, :, :, None, None] * dist_c
        valid_c = cmp_end[None, :] <= t[:, None]
        p_c = jax.nn.softmax(jnp.where(valid_c, s_c, NEG_INF), axis=-1)
        p_c = p_c * (t >= CMP_LEN - 1).astype(jnp.float32)[None, None, None, :, None]
        o_c = jnp.einsum('bghqn,bngd->bqghd', p_c, vc)
        imp = jnp.einsum('bghqn,nj->bgqj', p_c, overlap)
        cur = t // SEL_LEN
        valid_s = blk_ids[None, :] * SEL_LEN <= t[:, None]
        forced = ((blk_ids[None, :] == 0) | (blk_ids[None, :] == cur[:, None])
                  | (blk_ids[None, :] == cur[:, None] - 1)) & valid_s
        score = jnp.where(forced, FORCED_SCORE, jnp.where(valid_s, imp, -1.0))
        _, idx = lax.top_k(score, k_sel_n)
        k_sel = ks_blk[bi, gi, idx]
        v_sel = vs_blk[bi, gi, idx].reshape(B, G, Q_BLOCK, k_sel_n * SEL_LEN, HD)
        pos = idx[..., None] * SEL_LEN + jnp.arange(SEL_LEN)
        s_s = jnp.einsum('bqghd,bgqkld->bghqkl', qb, k_sel, preferred_element_type=jnp.float32) * scale
        dist_s = (t[None, None, :, None, None] - pos).astype(jnp.float32)
        s_s = s_s - slopes[None, :, :, None, None, None] * dist_s[:, :, None]
        mask_s = (pos <= t[None, None, :, None, None])[:, :, None]
        s_s = jnp.where(mask_s, s_s, NEG_INF).reshape(B, G, HPG, Q_BLOCK, k_sel_n * SEL_LEN)
        o_s = jnp.einsum('bghqm,bgqmd->bqghd', jax.nn.softmax(s_s, axis=-1), v_sel)
        kw = lax.dynamic_slice_in_dim(kw_pad, q0, Q_BLOCK + WINDOW, axis=1)
        vw = lax.dynamic_slice_in_dim(vw_pad, q0, Q_BLOCK + WINDOW, axis=1)
        s_pos = q0 - WINDOW + jnp.arange(Q_BLOCK + WINDOW)
        s_w = jnp.einsum('bqghd,bsgd->bghqs', qb, kw, preferred_element_type=jnp.float32) * scale
        s_w = s_w - slopes[None, :, :, None, None] * (t[:, None] - s_pos[None, :]).astype(jnp.float32)
        mask_w = (s_pos[None, :] <= t[:, None]) & (s_pos[None, :] > t[:, None] - WINDOW) & (s_pos[None, :] >= 0)
        o_w = jnp.einsum('bghqs,bsgd->bqghd', jax.nn.softmax(jnp.where(mask_w, s_w, NEG_INF), axis=-1), vw)
        return gb[..., 0, None] * o_c + gb[..., 1, None] * o_s + gb[..., 2, None] * o_w

    o = lax.map(block, jnp.arange(S // Q_BLOCK))
    o = o.transpose(1, 0, 2, 3, 4, 5).reshape(B, S, D_MODEL)
    return o.astype(h.dtype) @ w_out

def conv_ffn(h, w_up, conv_w, conv_b, w_down):
    a, v = jnp.split(h @ w_up, 2, axis=-1)
    a = lax.conv_general_dilated(a, conv_w[:, None, :].astype(a.dtype), window_strides=(1,),
                                 padding=[(CONV_W - 1, 0)], dimension_numbers=('NWC', 'WIO', 'NWC'),
                                 feature_group_count=D_FF) + conv_b
    return (jax.nn.silu(a) * v) @ w_down

def first_inputs(seed: int = 0) -> dict:
    key = jax.random.key(seed)
    ks = jax.random.split(key, 24)
    n_a = (DEPTH + 1) // 2
    n_b = DEPTH // 2
    D = D_MODEL
    nsa_in = D + 6 * NSA_KV * NSA_HD + 3 * NSA_HEADS

    def nrm(k, shape, s):
        return jax.random.normal(k, shape, jnp.float32) * s

    return {
        'x': nrm(ks[0], (BATCH, SEQ, D), 1.0),
        'c': nrm(ks[1], (BATCH, D), 1.0),
        'ada_w': nrm(ks[2], (DEPTH, D, 6 * D), 0.5 * D ** -0.5),
        'ada_b': nrm(ks[3], (DEPTH, 6 * D), 0.02),
        'norm_mix': 1.0 + nrm(ks[4], (DEPTH, D), 0.02),
        'norm_ffn': 1.0 + nrm(ks[5], (DEPTH, D), 0.02),
        'final_norm': 1.0 + nrm(ks[6], (D,), 0.02),
        'hg_w_in': nrm(ks[7], (n_a, D, 2 * HG_HEADS * HG_DK + 2 * D), D ** -0.5),
        'hg_w_out': nrm(ks[8], (n_a, D, D), D ** -0.5),
        'hg_gnorm': 1.0 + nrm(ks[9], (n_a, HG_DV), 0.02),
        'hg_lb': nrm(ks[10], (n_a + 1, HG_HEADS * HG_DK), 0.5),
        'nsa_w_in': nrm(ks[11], (n_b, D, nsa_in), D ** -0.5),
        'nsa_w_out': nrm(ks[12], (n_b, D, D), D ** -0.5),
        'nsa_cmp_pe': nrm(ks[13], (n_b, 2, CMP_LEN, NSA_HD), 0.1),
        'nsa_cmp_w1': nrm(ks[14], (n_b, 2, CMP_LEN * NSA_HD, NSA_HD), (CMP_LEN * NSA_HD) ** -0.5),
        'nsa_cmp_w2': nrm(ks[15], (n_b, 2, NSA_HD, NSA_HD), NSA_HD ** -0.5),
        'ffn_w_up': nrm(ks[16], (DEPTH, D, 2 * D_FF), D ** -0.5),
        'ffn_conv_w': nrm(ks[17], (DEPTH, CONV_W, D_FF), CONV_W ** -0.5),
        'ffn_conv_b': nrm(ks[18], (DEPTH, D_FF), 0.02),
        'ffn_w_down': nrm(ks[19], (DEPTH, D_FF, D), D_FF ** -0.5),
    }

def first_block(x, c, ada_w, ada_b, norm_mix, norm_ffn, final_norm, hg_w_in, hg_w_out, hg_gnorm, hg_lb,
              nsa_w_in, nsa_w_out, nsa_cmp_pe, nsa_cmp_w1, nsa_cmp_w2, ffn_w_up, ffn_conv_w, ffn_conv_b,
              ffn_w_down):
    lb_all = jnp.cumsum(jax.nn.softmax(hg_lb.astype(jnp.float32), axis=0), axis=0)
    c_act = jax.nn.silu(c)
    for layer in range(DEPTH):
        mod = c_act @ ada_w[layer] + ada_b[layer]
        sh1, sc1, g1, sh2, sc2, g2 = [m[:, None, :] for m in jnp.split(mod, 6, axis=-1)]
        hmix = rmsnorm(x, norm_mix[layer]) * (1.0 + sc1) + sh1
        j = layer // N_MIXERS
        if layer % N_MIXERS == 0:
            y = hgrn2_mixer(hmix, hg_w_in[j], hg_w_out[j], hg_gnorm[j], lb_all[j])
        else:
            y = nsa_mixer(hmix, nsa_w_in[j], nsa_w_out[j], nsa_cmp_pe[j], nsa_cmp_w1[j], nsa_cmp_w2[j])
        x = x + g1 * y
        hffn = rmsnorm(x, norm_ffn[layer]) * (1.0 + sc2) + sh2
        x = x + g2 * conv_ffn(hffn, ffn_w_up[layer], ffn_conv_w[layer], ffn_conv_b[layer], ffn_w_down[layer])
    return rmsnorm(x, final_norm)


DEPTH_2 = 1

D_MIX = D_MODEL
ATT_WIDTH = D_MIX // 2
POOL_WIDTH = D_MIX - ATT_WIDTH
HEAD_DIM = 64
N_HEADS = ATT_WIDTH // HEAD_DIM
IDX_HEADS = 4
IDX_DIM = 64
IDX_ROPE_DIM = 32
INDEX_TOPK = 256
POOL_WINDOWS = (2, 4, 8, 16)
N_POOL_GROUPS = len(POOL_WINDOWS)
POOL_CH = POOL_WIDTH // N_POOL_GROUPS
ROPE_THETA = 10000.0
NORM_EPS = 1e-6
Q_BLOCK_2 = 128
IN_SPLITS = (ATT_WIDTH, ATT_WIDTH, ATT_WIDTH, IDX_HEADS * IDX_DIM, IDX_DIM, IDX_HEADS, POOL_WIDTH)
IN_COLS = sum(IN_SPLITS)


def rms_norm(x, g):
    xf = x.astype(jnp.float32)
    y = xf * lax.rsqrt(jnp.mean(xf * xf, axis=-1, keepdims=True) + NORM_EPS)
    return (y * g.astype(jnp.float32)).astype(x.dtype)

def rope(x, pos, rot_dim):
    half = rot_dim // 2
    inv = ROPE_THETA ** (-jnp.arange(half, dtype=jnp.float32) / half)
    ang = pos.astype(jnp.float32)[:, None] * inv[None, :]
    cos = jnp.cos(ang)[:, None, :]
    sin = jnp.sin(ang)[:, None, :]
    xr = x[..., :rot_dim].astype(jnp.float32)
    x1, x2 = xr[..., :half], xr[..., half:]
    rot = jnp.concatenate([x1 * cos - x2 * sin, x2 * cos + x1 * sin], axis=-1).astype(x.dtype)
    return jnp.concatenate([rot, x[..., rot_dim:]], axis=-1)

def swiglu(x, w_gate, w_up, w_down):
    return (jax.nn.silu(x @ w_gate) * (x @ w_up)) @ w_down

def dsa_attention(q, k, v, q_idx, k_idx, w_idx, top_k):
    B, S, H, Dh = q.shape
    nb = S // Q_BLOCK_2
    key_pos = jnp.arange(S)
    scale = Dh ** -0.5

    def to_blocks(a):
        return a.reshape((B, nb, Q_BLOCK_2) + a.shape[2:]).swapaxes(0, 1)

    def block(args):
        qb, qib, wb, posb = args
        rel = jax.nn.relu(jnp.einsum('bthd,bsd->bths', qib, k_idx).astype(jnp.float32))
        score = jnp.einsum('bth,bths->bts', wb.astype(jnp.float32), rel)
        causal = key_pos[None, :] <= posb[:, None]
        score = jnp.where(causal[None], score, -jnp.inf)
        _, idx = lax.top_k(score, top_k)
        valid = idx <= posb[None, :, None]
        k_sel = jax.vmap(lambda kk, ii: kk[ii])(k, idx)
        v_sel = jax.vmap(lambda vv, ii: vv[ii])(v, idx)
        logits = jnp.einsum('bthd,btkhd->bhtk', qb, k_sel).astype(jnp.float32) * scale
        logits = jnp.where(valid[:, None], logits, -jnp.inf)
        p = jax.nn.softmax(logits, axis=-1).astype(v.dtype)
        return jnp.einsum('bhtk,btkhd->bthd', p, v_sel)

    pos_blocks = jnp.arange(S).reshape(nb, Q_BLOCK_2)
    out = lax.map(block, (to_blocks(q), to_blocks(q_idx), to_blocks(w_idx), pos_blocks))
    return out.swapaxes(0, 1).reshape(B, S, H * Dh)

def multiscale_pool(u):
    B, S, _ = u.shape
    uf = u.astype(jnp.float32).reshape(B, S, N_POOL_GROUPS, POOL_CH)
    c = jnp.concatenate([jnp.zeros((B, 1, N_POOL_GROUPS, POOL_CH), jnp.float32),
                         jnp.cumsum(uf, axis=1)], axis=1)
    t = jnp.arange(S)
    outs = []
    for g, w in enumerate(POOL_WINDOWS):
        cg = c[:, :, g]
        c_lo = jnp.concatenate([jnp.zeros((B, w - 1, POOL_CH), jnp.float32), cg[:, :S + 1 - w]], axis=1)
        count = jnp.minimum(t + 1, w).astype(jnp.float32)[None, :, None]
        outs.append((cg[:, 1:] - c_lo) / count - uf[:, :, g])
    return jnp.stack(outs, axis=2).astype(u.dtype)

def second_inputs(seed: int = 0) -> dict:
    key = jax.random.key(seed)
    ks = jax.random.split(key, 20)
    f32 = jnp.float32

    def nrm(k, shape, fan_in):
        return jax.random.normal(k, shape, f32) * fan_in ** -0.5

    def gain(k, shape):
        return 1.0 + 0.02 * jax.random.normal(k, shape, f32)

    L = DEPTH_2
    return {
        "x": jax.random.normal(ks[0], (BATCH, SEQ, D_MODEL), f32),
        "ffn1_norm": gain(ks[1], (L, D_MODEL)),
        "ffn1_w_gate": nrm(ks[2], (L, D_MODEL, D_FF), D_MODEL),
        "ffn1_w_up": nrm(ks[3], (L, D_MODEL, D_FF), D_MODEL),
        "ffn1_w_down": nrm(ks[4], (L, D_FF, D_MODEL), D_FF),
        "mix_norm": gain(ks[5], (L, D_MODEL)),
        "w_in": nrm(ks[6], (L, D_MODEL, IN_COLS), D_MODEL),
        "q_norm": gain(ks[7], (L, HEAD_DIM)),
        "k_norm": gain(ks[8], (L, HEAD_DIM)),
        "pool_w": nrm(ks[9], (L, N_POOL_GROUPS, POOL_CH, POOL_CH), POOL_CH),
        "pool_scale": 0.5 + 0.05 * jax.random.normal(ks[10], (L, POOL_WIDTH), f32),
        "w_out": nrm(ks[11], (L, D_MIX, D_MODEL), D_MIX),
        "ffn2_norm": gain(ks[12], (L, D_MODEL)),
        "ffn2_w_gate": nrm(ks[13], (L, D_MODEL, D_FF), D_MODEL),
        "ffn2_w_up": nrm(ks[14], (L, D_MODEL, D_FF), D_MODEL),
        "ffn2_w_down": nrm(ks[15], (L, D_FF, D_MODEL), D_FF),
    }

def second_block(x, ffn1_norm, ffn1_w_gate, ffn1_w_up, ffn1_w_down, mix_norm, w_in,
              q_norm, k_norm, pool_w, pool_scale, w_out,
              ffn2_norm, ffn2_w_gate, ffn2_w_up, ffn2_w_down):
    B, S, _ = x.shape
    top_k = min(INDEX_TOPK, S // 4)
    pos = jnp.arange(S)
    split_points = list(np.cumsum(IN_SPLITS)[:-1])
    idx_scale = (IDX_HEADS ** -0.5) * (IDX_DIM ** -0.5)

    for l in range(DEPTH_2):
        x = x + 0.5 * swiglu(rms_norm(x, ffn1_norm[l]), ffn1_w_gate[l], ffn1_w_up[l], ffn1_w_down[l])

        h = rms_norm(x, mix_norm[l])
        proj = h @ w_in[l]
        q, k, v, qi, ki, wi, u = jnp.split(proj, split_points, axis=-1)
        q = rope(rms_norm(q.reshape(B, S, N_HEADS, HEAD_DIM), q_norm[l]), pos, HEAD_DIM)
        k = rope(rms_norm(k.reshape(B, S, N_HEADS, HEAD_DIM), k_norm[l]), pos, HEAD_DIM)
        v = v.reshape(B, S, N_HEADS, HEAD_DIM)
        qi = rope(qi.reshape(B, S, IDX_HEADS, IDX_DIM), pos, IDX_ROPE_DIM)
        ki = rope(ki.reshape(B, S, 1, IDX_DIM), pos, IDX_ROPE_DIM)[:, :, 0]
        wi = wi * idx_scale

        attn = dsa_attention(q, k, v, qi, ki, wi, top_k)

        pooled = jnp.einsum('bsgc,gcd->bsgd', multiscale_pool(u), pool_w[l])
        pooled = pooled.reshape(B, S, POOL_WIDTH) * pool_scale[l]

        x = x + jnp.concatenate([attn, pooled], axis=-1) @ w_out[l]

        x = x + 0.5 * swiglu(rms_norm(x, ffn2_norm[l]), ffn2_w_gate[l], ffn2_w_up[l], ffn2_w_down[l])
    return x


def setup_inputs(seed=0):
    out = dict(first_inputs(seed))
    for name, value in second_inputs(seed + 1).items():
        if name != "x":
            out[name + "_2"] = value
    return out


def reference(
    x, c, ada_w, ada_b, norm_mix, norm_ffn, final_norm, hg_w_in, hg_w_out, hg_gnorm, hg_lb,
    nsa_w_in, nsa_w_out, nsa_cmp_pe, nsa_cmp_w1, nsa_cmp_w2, ffn_w_up, ffn_conv_w, ffn_conv_b,
    ffn_w_down, ffn1_norm_2, ffn1_w_gate_2, ffn1_w_up_2, ffn1_w_down_2, mix_norm_2, w_in_2,
    q_norm_2, k_norm_2, pool_w_2, pool_scale_2, w_out_2, ffn2_norm_2, ffn2_w_gate_2,
    ffn2_w_up_2, ffn2_w_down_2,
):
    x = first_block(
        x, c, ada_w, ada_b, norm_mix, norm_ffn, final_norm, hg_w_in, hg_w_out, hg_gnorm, hg_lb,
        nsa_w_in, nsa_w_out, nsa_cmp_pe, nsa_cmp_w1, nsa_cmp_w2, ffn_w_up, ffn_conv_w,
        ffn_conv_b, ffn_w_down,
    )
    return second_block(
        x, ffn1_norm_2, ffn1_w_gate_2, ffn1_w_up_2, ffn1_w_down_2, mix_norm_2, w_in_2, q_norm_2,
        k_norm_2, pool_w_2, pool_scale_2, w_out_2, ffn2_norm_2, ffn2_w_gate_2, ffn2_w_up_2,
        ffn2_w_down_2,
    )


_drawn_inputs = setup_inputs


def setup_inputs(seed=0):
    import zlib

    import numpy as np

    out = dict(_drawn_inputs(seed))
    spreads = {}
    factors = {'norm_mix': 4.153,
     'norm_ffn': 4.608,
     'hg_gnorm': 6.855,
     'nsa_cmp_pe': 4.018,
     'ffn_conv_b': 6.146,
     'ffn1_norm_2': 4.722,
     'mix_norm_2': 4.058,
     'q_norm_2': 8.0,
     'k_norm_2': 8.0,
     'ffn2_norm_2': 7.487,
     'pool_scale_2': 2.713}
    for name, (base, spread) in spreads.items():
        noise = np.random.default_rng([zlib.crc32(name.encode()), seed]).standard_normal(out[name].shape)
        drawn = base * np.exp(spread * noise) if base else spread * noise
        out[name] = __import__('jax').numpy.asarray(drawn.astype(out[name].dtype))
    for name, factor in factors.items():
        out[name] = (out[name] * factor).astype(out[name].dtype)
    return out
```

```python
import numpy as np

import concourse.bass as bass
import concourse.mybir as mybir

F32 = mybir.dt.float32
F32R = mybir.dt.float32r
I32 = mybir.dt.int32
ALU = mybir.AluOpType
ACT = mybir.ActivationFunctionType
AX = mybir.AxisListType

P = 128
S = 512
D = 1024
KD = D // P
TT = S // P
FF = 2816
KF = FF // P
EPS = 1e-6
NEG = -1e30
RAW = 4
SPL = 2
STOP = 99


class Event:
    def __init__(self, eng, const, loop=None):
        self.eng, self.const, self.loop = eng, const, loop


class Engine:
    def __init__(self, prog, name, raw):
        self.prog, self.name, self.e = prog, name, raw
        self.sem = prog.nc.alloc_semaphore("done_" + name)
        self.n = 0
        self.seen = {}

    def did(self, instruction, name=None):
        instruction.then_inc(self.sem, 1)
        self.n += 1
        if name is not None:
            self.prog.events[name] = Event(self, self.n, self.prog.loop)
        return instruction

    def wait(self, *names):
        for name in names:
            self.prog.wait(self, name)

    def reach(self, sem, const, step=0):
        loop = self.prog.loop
        if loop is None or step == 0:
            if const > 0:
                self.e.wait_ge(sem, const)
        else:
            assert const > 0, const
            self.e.wait_ge(sem, loop["i"] * step + const)
            self.settle()

    def settle(self, always=False):
        if (always or self.name in ("scalar", "gpsimd")) and self.prog.loop is not None:
            self.e.sem_inc(self.prog.settled[self.name], 1)


class Program:
    def __init__(self, nc, per_loop):
        self.nc = nc
        self.per_loop = per_loop
        self.learned = {}
        self.events = {}
        self.loop = None
        self.v = Engine(self, "vector", nc.vector)
        self.a = Engine(self, "scalar", nc.scalar)
        self.g = Engine(self, "gpsimd", nc.gpsimd)
        self.p = Engine(self, "tensor", nc.tensor)
        self.s = Engine(self, "sync", nc.sync)
        self.settled = {n: nc.alloc_semaphore("settled_" + n) for n in ("scalar", "gpsimd", "vector", "tensor")}
        self.engines = [self.v, self.a, self.g, self.p, self.s]

    def wait(self, eng, name):
        loop = self.loop
        ev = self.events.get(name)
        here = ev is not None and loop is not None and ev.loop is loop
        if not here:
            if ev is not None:
                const = ev.const
                if ev.loop is not None:
                    L = ev.loop
                    const += (L["count"] - 1) * L["per"][ev.eng.name]
                key = (ev.eng.name, None)
                if eng.seen.get(key, 0) < const:
                    eng.e.wait_ge(ev.eng.sem, const)
                    eng.seen[key] = const
            if loop is not None and name in loop["last"]:
                producer, k = loop["last"][name]
                src = next(x for x in self.engines if x.name == producer)
                self.wait_iter(eng, src, loop["base"][producer] + k - loop["per"][producer])
            return
        self.wait_iter(eng, ev.eng, ev.const)

    def wait_iter(self, eng, src, const):
        loop = self.loop
        key = (src.name, loop["name"])
        if eng.seen.get(key, -10**9) >= const:
            return
        eng.seen[key] = const
        per = loop["per"][src.name]
        if per:
            assert const > 0, (loop["name"], const)
            eng.e.wait_ge(src.sem, loop["i"] * per + const)
            eng.settle()
        elif const > 0:
            eng.e.wait_ge(src.sem, const)

    def run_loop(self, name, count, body):
        base = {e.name: e.n for e in self.engines}
        per, last = self.per_loop.get(name, ({e.name: 0 for e in self.engines}, {}))
        with self.nc.Fori(0, count) as i:
            L = dict(name=name, i=i, count=count, base=base, per=per, last=last)
            self.loop = L
            body(i)
            self.loop = None
        made = {e.name: e.n - base[e.name] for e in self.engines}
        self.learned[name] = (made, {n: (ev.eng.name, ev.const - base[ev.eng.name])
                                     for n, ev in self.events.items() if ev.loop is L})
        L["per"] = made
        for e in self.engines:
            for src in self.engines:
                const = e.seen.pop((src.name, name), None)
                if const is not None:
                    whole = const + (count - 1) * made[src.name]
                    e.seen[(src.name, None)] = max(whole, e.seen.get((src.name, None), 0))
            e.n = base[e.name] + count * made[e.name]


def constants():
    p = np.arange(P)[:, None]
    cols, at = [], {}

    def put(name, a):
        a = np.asarray(a, np.float32).reshape(P, -1)
        at[name] = (sum(c.shape[1] for c in cols), a.shape[1])
        cols.append(a)

    put("ident", np.eye(P))
    put("ones", np.ones((P, P)))
    f = np.arange(P)[None, :]
    for m in range(7):
        hs = 1 << m
        own = (p // (2 * hs) == f // (2 * hs)) & (p // hs % 2 == 0) & (f // hs % 2 == 1)
        put(f"level{m}", own.astype(np.int32).view(np.float32))
    put("level7", (p == f).astype(np.int32).view(np.float32))
    t = np.arange(S)[None, :]
    put("restart", np.broadcast_to((t % P != 0), (P, S)))
    u = np.arange(S)[None, :]
    put("dist", np.where(u <= p + 3 * P, -(p + 3 * P - u).astype(np.float64), NEG))
    n = np.arange(32)[None, None, :]
    tok = (np.arange(TT)[None, :, None] * P + p[:, :, None])
    put("dist_c", np.where((n < 31) & (n * 16 + 31 <= tok), -(tok - (n * 16 + 15.5)), NEG))
    put("slope", np.broadcast_to(2.0 ** (-8.0 * (np.arange(16)[None, :] + 1) / 16), (P, 16)))
    put("seen", np.broadcast_to(tok >= 31, (P, TT, 4)))
    for tag, half in (("", 32), ("_i", 16)):
        inv = np.float32(10000.0) ** (-np.arange(half, dtype=np.float32) / np.float32(half))
        ang = tok[:, :, 0:1].astype(np.float32) * inv[None, None, :].astype(np.float32)
        put("cos" + tag, np.cos(ang))
        put("sin" + tag, np.sin(ang))
    put("tri", np.where(f <= p, 0.0, NEG))
    t16 = np.arange(16) + 1.0
    put("corr", np.broadcast_to(np.stack([w / np.minimum(t16, w) for w in (2, 4, 8, 16)]), (P, 4, 16)))
    return np.concatenate(cols, 1), at


class Kernel:
    def __init__(self, nc, io, const_at, per_loop):
        self.nc, self.io, self.const_at = nc, io, const_at
        self.pr = Program(nc, per_loop)
        self.v, self.a, self.g, self.p, self.s = self.pr.engines
        nc_alloc = nc.alloc_sbuf_tensor_at
        self.at = (nc.sbuf_base + 31) // 32 * 32
        self.used = 0

        def sb(name, shape, dt=F32, at=None):
            size = int(np.prod(shape[1:])) * 4
            if at is None:
                at = self.at
                self.at += (size + 31) // 32 * 32
            assert at + size <= nc.sbuf_usable_end, (name, at + size)
            return nc_alloc(name, shape, dt, offset=at)
        self.sb = sb
        width = const_at['ones'][0] + P
        self.const = sb("const", [P, width])
        self.xT = sb("xT", [P, KD, S])
        self.h_at = self.at
        self.h_hi = sb("h_hi", [P, KD, S], F32R)
        self.h_lo = sb("h_lo", [P, KD, S], F32R)
        self.w_raw = [sb(f"w_raw{i}", [P, 1024]) for i in range(RAW)]
        self.w_hi = [sb(f"w_hi{i}", [P, 1024], F32R) for i in range(SPL)]
        self.w_lo = [sb(f"w_lo{i}", [P, 1024], F32R) for i in range(SPL)]
        self.m_raw = [sb(f"m_raw{i}", [P, 1024]) for i in range(2)]
        self.m_acc = sb("m_acc", [P, 5, 1024])
        self.mod = sb("mod", [P, 2, 6, KD])
        self.cvec = sb("cvec", [P, KD])
        self.vecs = sb("vecs", [P, 4, P])
        self.small = sb("small", [P, 256])
        self.scr_at = self.at
        self.arena = self.at
        self.ps = nc.alloc_psum_tensor("ps", [P, 8, S], F32)
        sem = nc.alloc_semaphore
        self.s_raw = [sem(f"raw_landed{i}") for i in range(RAW)]
        self.s_hi = sem("weights_high")
        self.s_lo = sem("weights_low")
        self.s_mm = sem("unit_multiplied")
        self.s_m = [sem(f"mod_landed{i}") for i in range(2)]
        self.s_mac = sem("mod_unit_added")
        self.s_const = sem("constants_landed")
        self.s_out = sem("output_stored")
        self.n_const = 0
        self.U = 0
        self.US = 0
        self.M = 0

    def c(self, name):
        o, w = self.const_at[name]
        return self.const[:, o:o + w]

    def load_const(self, dst, src):
        self.nc.scalar.dma_start(dst, src).then_inc(self.s_const, 16)
        self.n_const += 16

    def load_unit(self, halves, k=0, step=0):
        u = self.U + k
        slot = u % RAW
        assert step % RAW == 0
        self.s.reach(self.s_lo, u + 1, step)
        for dst, src in halves(self.w_raw[slot]):
            self.nc.sync.dma_start(dst, src).then_inc(self.s_raw[slot], 16)

    def split_unit(self, cols=1024, k=0, step=0, view=None):
        u = self.U + k
        if u >= self.pr.per_loop.get("units", 10**9):
            return
        raw, hi, lo = self.w_raw[u % RAW], self.w_hi[u % SPL], self.w_lo[u % SPL]
        pick = view or (lambda t: t[:, 0:cols])
        for e in (self.a, self.v):
            e.reach(self.s_raw[u % RAW], 32 * (u // RAW + 1), 32 * step // RAW)
            e.reach(self.s_mm, u + 1, step)
        self.nc.scalar.activation(pick(hi), pick(raw), ACT.Copy).then_inc(self.s_hi, 1)
        self.v.reach(self.s_hi, u + 1, step)
        self.nc.vector.tensor_tensor(pick(lo), pick(raw), pick(hi).bitcast(F32),
                                     ALU.subtract).then_inc(self.s_lo, 1)

    def multiply_unit(self, products, k=0, step=0):
        u = self.U + k
        self.p.reach(self.s_lo, u + 1 + RAW, step)
        for out, lhsT, rhs, start, stop in products(self.w_hi[u % SPL], self.w_lo[u % SPL]):
            last = self.nc.tensor.matmul(out, lhsT, rhs, start=start, stop=stop)
        last.then_inc(self.s_mm, 1)

    def group_done(self, eng, k, step=0):
        eng.reach(self.s_mm, self.U + k + 1 + SPL, step)

    def mod_unit(self, layer, part, kt, acc, k, step=0):
        m = self.M + k
        raw = self.m_raw[m % 2]
        if m >= 2:
            self.g.reach(self.s_mac, m - 1, step)
        cols = bass.ds(part * D, D) if not isinstance(part, int) else slice(part * D, (part + 1) * D)
        self.nc.gpsimd.dma_start(raw[:, :], self.io["ada_w"][layer, kt * P:(kt + 1) * P, cols]) \
            .then_inc(self.s_m[m % 2], 16)
        self.v.reach(self.s_m[m % 2], 16 * (m // 2 + 1), 8 * step)
        if m >= 1:
            self.v.reach(self.s_mac, m, step)
        if kt == 0:
            ins = self.nc.vector.tensor_scalar(acc, raw[:, :], self.cvec[:, kt:kt + 1], None, ALU.mult)
        else:
            ins = self.nc.vector.scalar_tensor_tensor(acc, raw[:, :], self.cvec[:, kt:kt + 1], acc,
                                                      ALU.mult, ALU.add)
        ins.then_inc(self.s_mac, 1)

    def mod_finish(self, layer, part, slot, bank):
        self.p.reach(self.s_mac, self.M)
        self.p.wait(f"bank{bank}")
        for n in range(KD):
            ins = self.nc.tensor.matmul(self.ps[:, bank, n:n + 1], self.m_acc[:, slot, n * P:(n + 1) * P],
                                        self.c("ones")[:, 0:1], start=True, stop=True)
        self.p.did(ins, "mod_sum")
        self.v.wait("mod_sum")
        self.v.did(self.nc.vector.tensor_tensor(self.mod[:, layer, part, :], self.ps[:, bank, 0:KD],
                                                self.mod_b[:, layer, part, :], ALU.add), f"bank{bank}")
        self.pr.events[f"mod{layer}{part}"] = self.pr.events[f"bank{bank}"]

    def group_load(self, k, step, pieces):
        for u in range(4):
            def halves(raw, u=u):
                two = raw[:, :].rearrange("p (kk c) -> p kk c", kk=2)
                for (kk, cols), src in pieces(u):
                    yield two[:, kk, cols], src
            self.load_unit(halves, k + u, step)

    @staticmethod
    def k_tiles(w, u, cols):
        for kk in range(2):
            kt = 2 * u + kk
            width = cols.stop - cols.start if isinstance(cols, slice) else 512
            yield (kk, slice(0, width)), w[kt * P:(kt + 1) * P, cols]

    def feature_products(self, u, banks):
        def products(hi, lo):
            for kk in range(2):
                kt = 2 * u + kk
                for n, b in enumerate(banks):
                    c = kk * 512 + n * P
                    out = self.ps[:, b, :]
                    yield out, hi[:, c:c + P], self.h_hi[:, kt, :], kt == 0, False
                    yield out, hi[:, c:c + P], self.h_lo[:, kt, :], False, False
                    yield out, lo[:, c:c + P], self.h_hi[:, kt, :], False, kt == KD - 1
        return products

    def token_products(self, u, banks, width=512):
        def products(hi, lo):
            for kk in range(2):
                kt = 2 * u + kk
                for t, b in enumerate(banks):
                    out = self.ps[:, b, 0:width]
                    w = slice(kk * 512, kk * 512 + width)
                    tok = slice(t * P, (t + 1) * P)
                    yield out, self.h_hi[:, kt, tok], hi[:, w], kt == 0, False
                    yield out, self.h_lo[:, kt, tok], hi[:, w], False, False
                    yield out, self.h_hi[:, kt, tok], lo[:, w], False, kt == KD - 1
        return products

    def group(self, k, step, banks, pieces, kind="feature", width=512, next_width=None, extra=None):
        self.group_load(k, step, pieces)
        for u in range(4):
            self.p.wait(*([f"h{2 * u}", f"h{2 * u + 1}"]))
            if u == 0:
                self.p.wait(*[f"bank{b}" for b in banks])
            if kind == "feature":
                self.multiply_unit(self.feature_products(u, banks), k + u, step)
            else:
                self.multiply_unit(self.token_products(u, banks, width), k + u, step)
            w = width if u < 2 else (next_width or 512)
            view = None if w == 512 else (lambda t, w=w: t[:, :].rearrange("p (a b) -> p a b", a=2)[:, :, 0:w])
            self.split_unit(k=k + u + 2, step=step, view=view)
            if extra:
                extra(u)

    def square_sum(self, kt, bank=7):
        self.a.wait(f"x{kt}", f"sq_used{kt % 2}")
        sq = self.sq[kt % 2]
        self.a.did(self.nc.scalar.activation(sq[:, :], self.xT[:, kt, :], ACT.Square), f"sq{kt % 2}")
        self.p.wait(f"sq{kt % 2}")
        if kt == 0:
            self.p.wait(f"bank{bank}")
        ins = self.nc.tensor.matmul(self.ps[:, bank, :], self.c("ones"), sq[:, :],
                                    start=kt == 0, stop=kt == KD - 1)
        self.p.did(ins, f"sq_used{kt % 2}")

    def norm(self, scale, bias, need, bank=7, into_x=False):
        nc = self.nc
        for kt in range(KD):
            self.square_sum(kt, bank)
        self.a.wait(f"sq_used{(KD - 1) % 2}")
        self.a.did(nc.scalar.activation(self.rstd[:, :], self.ps[:, bank, :], ACT.Ln, bias=self.eps,
                                        scale=1.0 / D), f"bank{bank}")
        self.a.wait(f"bank{bank}")
        self.a.did(nc.scalar.activation(self.rstd[:, :], self.rstd[:, :], ACT.Exp, scale=-0.5), "rstd")
        self.a.wait(*need)
        self.v.wait("rstd", *need)
        for kt in range(KD):
            t, full = self.nt[kt % 2], self.nh[kt % 2]
            self.v.wait(f"normed{kt % 2}")
            if into_x:
                self.v.did(nc.vector.scalar_tensor_tensor(self.xT[:, kt, :], self.xT[:, kt, :], scale(kt),
                                                          self.rstd[:, :], ALU.mult, ALU.mult), f"x{kt}")
                continue
            self.v.did(nc.vector.scalar_tensor_tensor(t[:, :], self.xT[:, kt, :], scale(kt),
                                                      self.rstd[:, :], ALU.mult, ALU.mult), f"nt{kt % 2}")
            self.a.wait(f"nt{kt % 2}", f"h{kt}")
            b = bias(kt) if bias else 0.0
            self.a.did(nc.scalar.activation(full[:, :], t[:, :], ACT.Identity, bias=b) if bias else
                       nc.scalar.activation(full[:, :], t[:, :], ACT.Copy), f"normed{kt % 2}")
            self.a.wait(f"normed{kt % 2}")
            self.a.did(nc.scalar.activation(self.h_hi[:, kt, :], full[:, :], ACT.Copy), f"hh{kt % 2}")
            self.v.wait(f"hh{kt % 2}")
            self.v.did(nc.vector.tensor_tensor(self.h_lo[:, kt, :], full[:, :],
                                               self.h_hi[:, kt, :].bitcast(F32), ALU.subtract), f"h{kt}")

    def norm_scratch(self, base):
        n = next(self.names)
        self.sq = [self.sb(f"sq{n}_{i}", [P, S], at=base + i * 2048) for i in range(2)]
        self.nt = [self.sb(f"nt{n}_{i}", [P, S], at=base + (2 + i) * 2048) for i in range(2)]
        self.nh = [self.sb(f"nh{n}_{i}", [P, S], at=base + (4 + i) * 2048) for i in range(2)]
        self.rstd = self.sb(f"rstd{n}", [P, S], at=base + 6 * 2048)

    def start(self):
        nc, io = self.nc, self.io
        nc.vector.sem_inc(self.s_lo, RAW)
        nc.tensor.sem_inc(self.s_mm, SPL)
        nc.vector.sem_inc(self.v.sem, 8); self.v.n = 8
        nc.scalar.sem_inc(self.a.sem, 8); self.a.n = 8
        nc.gpsimd.sem_inc(self.g.sem, 8); self.g.n = 8
        nc.tensor.sem_inc(self.p.sem, 8); self.p.n = 8
        xin = self.sb("xin", [P, TT, D], at=self.arena)
        self.load_const(self.const[:, :], io["const"])
        self.load_const(xin[:, :, :], io["x"].rearrange("b (t p) d -> p (b t) d", p=P))
        rows = self.sb("vec_rows", [P, 4, P], at=self.arena + 16384)
        at = {}

        def vec(tile, name, src, n):
            lo = sum(k for (t, k) in at.values() if t == tile)
            at[name] = (tile, n)
            self.load_const(rows[lo:lo + n, tile, :], src)
            return self.vecs[:, tile, lo:lo + n]
        self.mod_b = vec(0, "ada_b", io["ada_b"].rearrange("l (r p) -> (l r) p", p=P), 96) \
            .rearrange("p (l a k) -> p l a k", l=2, a=6)
        self.c_in = vec(0, "c", io["c"].rearrange("b (k p) -> (b k) p", p=P), KD)
        self.lbp = vec(0, "hg_lb", io["hg_lb"].rearrange("a (k p) -> (a k) p", p=P), 16) \
            .rearrange("p (a k) -> p a k", a=2)
        self.gn = vec(0, "hg_gnorm", io["hg_gnorm"], 1)
        self.norms = {}
        for name in ("norm_mix", "norm_ffn", "final_norm", "ffn1_norm_2", "mix_norm_2", "ffn2_norm_2"):
            src = io[name]
            src = src.rearrange("(k p) -> k p", p=P) if name == "final_norm" else \
                src.rearrange("l (k p) -> (l k) p", p=P)
            self.norms[name] = vec(1, name, src, src.shape[0])
        self.pool_scale = vec(1, "pool_scale", io["pool_scale_2"].rearrange("l (k p) -> (l k) p", p=P), 4)
        self.conv = []
        for layer in range(2):
            w = vec(2 + layer, f"conv_w{layer}", io["ffn_conv_w"][layer].rearrange("w (k p) -> (w k) p", p=P), 3 * KF)
            bias = vec(2 + layer, f"conv_b{layer}", io["ffn_conv_b"][layer].rearrange("(k p) -> k p", p=P), KF)
            self.conv.append((w.rearrange("p (w k) -> p w k", w=3), bias))
        n_rows = [sum(k for (t, k) in at.values() if t == tile) for tile in range(4)]
        small = self.small
        self.eps, self.lb, self.oml = small[:, 0:1], small[:, 8:16], small[:, 16:24]
        for e in (self.v, self.a, self.p, self.g):
            e.reach(self.s_const, self.n_const)
        self.v.did(nc.vector.memset(self.eps, EPS), "eps")
        self.a.wait("eps")
        for tile, n in enumerate(n_rows):
            ins = nc.tensor.transpose(self.ps[:, 4 + tile, 0:n], rows[0:n, tile, :], self.c("ident")[0:n, 0:n])
            self.p.did(ins, "vec_t")
            self.v.wait("vec_t")
            self.v.did(nc.vector.tensor_copy(self.vecs[:, tile, 0:n], self.ps[:, 4 + tile, 0:n]), f"bank{4 + tile}")
        self.a.wait("bank7")
        self.a.did(nc.scalar.activation(self.cvec[:, :], self.c_in, ACT.Silu), "c_act")
        self.v.wait("c_act")
        for kt in range(KD):
            b = kt % 4
            if kt >= 4:
                self.p.wait(f"bank{b}")
            for t in range(TT):
                ins = nc.tensor.transpose(self.ps[:, b, t * P:(t + 1) * P], xin[:, t, kt * P:(kt + 1) * P],
                                          self.c("ident"))
            self.p.did(ins, "xt")
            self.a.wait("xt")
            self.a.did(nc.scalar.activation(self.xT[:, kt, :], self.ps[:, b, :], ACT.Copy), f"bank{b}")
            self.pr.events[f"x{kt}"] = self.pr.events[f"bank{b}"]
        for part in range(2):
            self.v.wait("mod_sum") if part else None
            for kt in range(KD):
                self.mod_unit(0, part, kt, self.m_acc[:, part, :], kt)
            self.M += KD
            self.mod_finish(0, part, part, 4 + part)
        self.split_unit_later = 2

    def lower_bounds(self):
        nc, v, a = self.nc, self.v, self.a
        sc = self.small
        mx, e0, e1 = sc[:, 40:48], sc[:, 48:56], sc[:, 56:64]
        l0, l1 = self.lbp[:, 0, :], self.lbp[:, 1, :]
        v.did(nc.vector.tensor_tensor(mx, l0, l1, ALU.max), "lb_t"); v.wait("lb_t")
        v.did(nc.vector.tensor_tensor(e0, l0, mx, ALU.subtract), "lb_t")
        v.did(nc.vector.tensor_tensor(e1, l1, mx, ALU.subtract), "lb_t")
        a.wait("lb_t")
        a.did(nc.scalar.activation(sc[:, 48:64], sc[:, 48:64], ACT.Exp), "lb_e")
        v.wait("lb_e")
        v.did(nc.vector.tensor_tensor(mx, e0, e1, ALU.add), "lb_t"); v.wait("lb_t")
        v.did(nc.vector.reciprocal(mx, mx), "lb_t"); v.wait("lb_t")
        v.did(nc.vector.tensor_tensor(self.lb, e0, mx, ALU.mult), "lb_t")
        v.did(nc.vector.tensor_tensor(self.oml, e1, mx, ALU.mult), "lb")

    def modulation_scales(self, layer):
        nc, v = self.nc, self.v
        for part, gain in ((1, "norm_mix"), (4, "norm_ffn")):
            if f"mod{layer}{part}" not in self.pr.events or f"ms{layer}{part}" in self.pr.events:
                continue
            dst = self.mod[:, layer, part, :]
            v.wait(f"mod{layer}{part}")
            v.did(nc.vector.scalar_tensor_tensor(dst, dst, 1.0, self.norms[gain][:, layer * KD:(layer + 1) * KD],
                                                         ALU.add, ALU.mult),
                  f"ms{layer}{part}")

    def prologue(self):
        for k in range(2):
            self.split_unit(k=k)

    def hgrn_in(self):
        nc, w = self.nc, self.io["hg_w_in"]
        self.proj = self.sb("proj", [P, 4 * KD, S], at=self.arena)

        def body(i):
            for gi in range(2):
                banks = range(4 * gi, 4 * gi + 4)
                cols = bass.ds(i * 1024 + gi * 512, 512)
                self.group(4 * gi, 8, banks,
                           lambda u: self.k_tiles(w[0], u, cols),
                           extra=lambda u, gi=gi: self.mod_unit(0, bass_part(i + 2), 4 * gi + u,
                                                                self.m_acc[:, bass.ds(i, 1), :], 4 * gi + u, 8))
                for e, n in ((self.a, 0), (self.v, 1), (self.a, 2), (self.v, 3)):
                    if n < 2:
                        self.group_done(e, 4 * gi + 3, 8)
                    dst = self.proj[:, bass.ds(i * 8 + gi * 4 + n, 1), :]
                    src = self.ps[:, banks[n]:banks[n] + 1, :]
                    if e is self.a:
                        e.did(nc.scalar.activation(dst, src, ACT.Copy), f"bank{banks[n]}")
                    else:
                        e.did(nc.vector.tensor_copy(dst, src), f"bank{banks[n]}")
        self.pr.run_loop("hgrn_in", 4, body)
        self.U += 32
        self.M += 32

    def hgrn_mix(self):
        nc, v, a, g, p = self.nc, self.v, self.a, self.g, self.p
        pr = self.proj
        at = [self.h_at]

        def tmp(name, shape, dt=F32):
            t = self.sb(name, shape, dt, at=at[0])
            at[0] += int(np.prod(shape[1:])) * 4
            assert at[0] <= self.h_at + 32768
            return t
        kk = self.sb("hg_k", [P, KD, S], at=self.arena + 65536)
        diff = [tmp(f"hg_d{j}", [P, S]) for j in range(2)]
        G = [tmp(f"hg_g{j}", [P, S]) for j in range(2)]
        scT, qe, kd, kdT, vs, vT = (tmp("hg_" + n, [P, S]) for n in ("scT", "qe", "kd", "kdT", "vs", "vT"))
        osq, rst, oo = (tmp("hg_" + n, [P, S]) for n in ("osq", "rst", "oo"))
        state = tmp("hg_state", [P, 3, P])
        ebl = tmp("hg_ebl", [P, TT])
        a.wait("bank7"); v.wait("bank6")
        a.wait("lb")

        def gates(i):
            f, k, gt = pr[:, bass.ds(i + 8, 1), :], kk[:, bass.ds(i, 1), :], pr[:, bass.ds(i + 24, 1), :]
            a.did(nc.scalar.activation(k, f, ACT.Sigmoid, scale=-1.0), "k0")
            a.wait("k0")
            a.did(nc.scalar.activation(f, f, ACT.Sigmoid), "sf")
            v.wait("k0")
            v.did(nc.vector.tensor_scalar(k, k, self.oml[:, bass.ds(i, 1)], None, ALU.mult), "k1")
        v.wait("bank7")
        a.wait("bank1", "bank3", "bank5")
        self.pr.run_loop("hg_gates", KD, gates)

        def silu(i):
            gt = pr[:, bass.ds(i + 24, 1), :]
            a.did(nc.scalar.activation(gt, gt, ACT.Silu), "sg")
        self.pr.run_loop("hg_silu", KD, silu)

        def logs(i):
            f = pr[:, bass.ds(i + 8, 1), :]
            if True:
                a.did(nc.scalar.activation(f, f, ACT.Ln, bias=self.lb[:, bass.ds(i, 1)],
                                           scale=self.oml[:, bass.ds(i, 1)]), "logf")
            v.wait("logf")
            v.did(nc.vector.tensor_tensor_scan(pr[:, bass.ds(i + 8, 1), :].rearrange("p a t -> p (a t)"),
                                               self.c2["restart"], f.rearrange("p a t -> p (a t)"), 0.0,
                                               ALU.mult, ALU.add), "b")
        a.wait("sf")
        v.reach(self.s_c2, self.n_c2)
        self.pr.run_loop("hg_logs", KD, logs)
        g.wait("b", "k1")
        v.did(nc.vector.memset(scT[:, :], 0.0), "scT0")

        def head(i):
            q = pr[:, bass.ds(i, 1), :].rearrange("p a t -> p (a t)")
            b = pr[:, bass.ds(i + 8, 1), :].rearrange("p a t -> p (a t)")
            vv = pr[:, bass.ds(i + 16, 1), :].rearrange("p a t -> p (a t)")
            gt = pr[:, bass.ds(i + 24, 1), :].rearrange("p a t -> p (a t)")
            k = kk[:, bass.ds(i, 1), :].rearrange("p a t -> p (a t)")

            a.wait("vT_used")
            a.did(nc.scalar.activation(vs[:, :], vv, ACT.Copy), "vs")
            p.wait("vs", "bank4")
            for c in range(TT):
                ins = nc.tensor.transpose(self.ps[:, 4, c * P:(c + 1) * P], vs[:, c * P:(c + 1) * P], self.c("ident"))
            p.did(ins, "vTp")
            a.wait("vTp", "o_done")
            a.did(nc.scalar.activation(vT[:, :], self.ps[:, 4, :], ACT.Copy), "bank4")

            d0, d1 = diff
            b3 = b.rearrange("p (c t) -> p c t", c=TT)
            last = b3[:, :, P - 1:P]
            v.wait("e_used0")
            v.did(nc.vector.tensor_tensor(d0[:, :].rearrange("p (c t) -> p c t", c=TT),
                                          last.to_broadcast([P, TT, P]), b3, ALU.subtract), "d0")
            a.wait("d0", "kd_used")
            a.did(nc.scalar.activation(kd[:, :], d0[:, :], ACT.Exp), "ekd")
            a.wait("state_done")
            a.did(nc.scalar.activation(ebl[:, :], last.rearrange("p c t -> p (c t)"), ACT.Exp), "ebl")
            a.wait("o_done")
            a.did(nc.scalar.activation(qe[:, :], b, ACT.Exp), "eqe")
            g.wait("eqe")
            g.did(nc.gpsimd.tensor_tensor(qe[:, :], qe[:, :], q, ALU.mult), "qe")
            g.wait("ekd")
            g.did(nc.gpsimd.tensor_tensor(kd[:, :], kd[:, :], k, ALU.mult), "kd")
            self.pr.events["e_used0"] = self.pr.events["ekd"]
            p.wait("kd", "bank5")
            for c in range(TT):
                ins = nc.tensor.transpose(self.ps[:, 5, c * P:(c + 1) * P], kd[:, c * P:(c + 1) * P], self.c("ident"))
            p.did(ins, "kd_used")
            a.wait("kd_used", "state_done")
            a.did(nc.scalar.activation(kdT[:, :], self.ps[:, 5, :], ACT.Copy), "bank5")

            for m in range(8):
                j = m % 2
                if m < 7:
                    hs = 1 << m
                    bb = b.rearrange("p (n a t) -> p n a t", a=2, t=hs)
                    dd = diff[j][:, :].rearrange("p (n a t) -> p n a t", a=2, t=hs)
                    gg = G[j][:, :].rearrange("p (n a t) -> p n a t", a=2, t=hs)
                    qq = q.rearrange("p (n a t) -> p n a t", a=2, t=hs)
                    kq = k.rearrange("p (n a t) -> p n a t", a=2, t=hs)
                    nb = S // (2 * hs)
                    ref = bb[:, :, 0, hs - 1:hs].to_broadcast([P, nb, hs])
                    v.wait(f"G{j}")
                    if j == 0 and m == 0:
                        v.wait("e_used0")
                    v.did(nc.vector.tensor_tensor(dd[:, :, 1, :], bb[:, :, 1, :], ref, ALU.subtract))
                    v.did(nc.vector.tensor_tensor(dd[:, :, 0, :], ref, bb[:, :, 0, :], ALU.subtract), f"d{j}")
                    a.wait(f"d{j}")
                    a.did(nc.scalar.activation(diff[j][:, :], diff[j][:, :], ACT.Exp), f"e{j}")
                    g.wait(f"e{j}", f"S{j}")
                    g.did(nc.gpsimd.tensor_tensor(gg[:, :, 1, :], qq[:, :, 1, :], dd[:, :, 1, :], ALU.mult))
                    g.did(nc.gpsimd.tensor_tensor(gg[:, :, 0, :], kq[:, :, 0, :], dd[:, :, 0, :], ALU.mult), f"G{j}")
                else:
                    g.wait(f"S{j}")
                    g.did(nc.gpsimd.tensor_tensor(G[j][:, :], q, k, ALU.mult), f"G{j}")
                p.wait(f"G{j}", f"bank{m % 4}")
                for c in range(TT):
                    gc = G[j][:, c * P:(c + 1) * P]
                    ins = nc.tensor.matmul(self.ps[:, m % 4, c * P:(c + 1) * P], gc,
                                           gc if m < 7 else self.c("ones"), start=True, stop=True)
                p.did(ins, f"S{j}")
                v.wait(f"S{j}")
                if m == 0:
                    v.wait("o_done")
                mask = self.c2[f"level{m}"].bitcast(I32).unsqueeze(1).broadcast_to([P, TT, P])
                if m > 0:
                    v.wait("sc")
                v.settle(True)
                v.did(nc.vector.copy_predicated(scT[:, :].rearrange("p (c t) -> p c t", c=TT), mask,
                                                self.ps[:, m % 4, :].rearrange("p (c t) -> p c t", c=TT)), "sc")
                self.pr.events[f"bank{m % 4}"] = self.pr.events["sc"]

            for c in range(3):
                p.wait("bank4", "bank5", "bank7")
                p.did(nc.tensor.matmul(self.ps[:, 7, 0:P], kdT[:, c * P:(c + 1) * P], vT[:, c * P:(c + 1) * P],
                                       start=True, stop=True), "st")
                v.wait("st")
                if c == 0:
                    v.wait("o_done")
                    v.did(nc.vector.tensor_copy(state[:, 0, :], self.ps[:, 7, 0:P]), "state_done")
                else:
                    v.wait("state_done", "ebl")
                    v.did(nc.vector.scalar_tensor_tensor(state[:, c, :], state[:, c - 1, :], ebl[:, c:c + 1],
                                                         self.ps[:, 7, 0:P], ALU.mult, ALU.add), "state_done")
                self.pr.events["bank7"] = self.pr.events["state_done"]
            p.wait("sc", "state_done", "qe", "bank6")
            for c in range(TT):
                w = slice(c * P, (c + 1) * P)
                ins = nc.tensor.matmul(self.ps[:, 6, w], vT[:, w], scT[:, w], start=True, stop=c == 0)
                if c:
                    ins = nc.tensor.matmul(self.ps[:, 6, w], state[:, c - 1, :], qe[:, w], start=False, stop=True)
            p.did(ins, "o_done")
            self.pr.events["vT_used"] = self.pr.events["o_done"]
            a.wait("o_done", "osum")
            a.did(nc.scalar.activation(osq[:, :], self.ps[:, 6, :], ACT.Square), "osq")
            p.wait("osq", "bank7")
            p.did(nc.tensor.matmul(self.ps[:, 7, :], self.c("ones"), osq[:, :], start=True, stop=True), "osum")
            a.wait("osum", "oo")
            a.did(nc.scalar.activation(rst[:, :], self.ps[:, 7, :], ACT.Ln, bias=self.eps, scale=1.0 / P), "bank7")
            a.wait("bank7")
            a.did(nc.scalar.activation(rst[:, :], rst[:, :], ACT.Exp, scale=-0.5), "rst")
            v.wait("rst", "o_gated")
            v.did(nc.vector.scalar_tensor_tensor(oo[:, :], self.ps[:, 6, :], self.gn, rst[:, :],
                                                 ALU.mult, ALU.mult), "oo")
            self.pr.events["bank6"] = self.pr.events["oo"]
            g.wait("oo")
            g.did(nc.gpsimd.tensor_tensor(q, oo[:, :], gt, ALU.mult), "o_gated")
        for n in ("S0", "S1", "G0", "G1", "e_used0", "o_done", "osum", "oo", "o_gated", "kd_used", "state_done", "vT_used"):
            self.pr.events.pop(n, None)
        for n in (4, 5, 6, 7):
            a.wait(f"bank{n}"); v.wait(f"bank{n}"); p.wait(f"bank{n}")
        g.wait("sg"); a.wait("b"); v.wait("scT0")
        p.wait("scT0")
        self.pr.run_loop("hg_head", KD, head)
        self.split_h(lambda kt: self.proj[:, kt, :], ("o_gated", "G0", "G1", "S0", "S1", "oo", "sc", "bank4", "bank5", "bank7"))

    def split_h(self, src, need):
        nc = self.nc
        self.a.wait(*need)
        self.v.wait(*need)
        for kt in range(KD):
            self.a.did(nc.scalar.activation(self.h_hi[:, kt, :], src(kt), ACT.Copy), f"hh{kt % 2}")
            self.v.wait(f"hh{kt % 2}")
            self.v.did(nc.vector.tensor_tensor(self.h_lo[:, kt, :], src(kt), self.h_hi[:, kt, :].bitcast(F32),
                                               ALU.subtract), f"h{kt}")

    def out_proj(self, w, gain, need, extra=None):
        nc = self.nc
        for gi in range(2):
            banks = range(4 * gi, 4 * gi + 4)
            self.group(0, 0, banks, lambda u: self.k_tiles(w, u, slice(gi * 512, (gi + 1) * 512)),
                       extra=(lambda u, gi=gi: extra(4 * gi + u)) if extra else None)
            self.group_done(self.v, 3)
            self.v.wait(*need)
            for n in range(4):
                kt = gi * 4 + n
                self.add_to_x(kt, banks[n], gain)
            self.U += 4

    def add_to_x(self, kt, bank, gain):
        x = self.xT[:, kt, :]
        self.v.did(self.nc.vector.scalar_tensor_tensor(x, self.ps[:, bank, :], gain(kt), x, ALU.mult, ALU.add),
                   f"bank{bank}")
        self.pr.events[f"x{kt}"] = self.pr.events[f"bank{bank}"]

    def ffn(self, name, gate_w, up_w, down_w, gain, conv=None, need=(), extra=None, after_up=None):
        nc, v, a, p = self.nc, self.v, self.a, self.p
        hid_hi = self.sb(f"hid_hi_{name}", [P, KF, S], F32R, at=self.arena)
        hid_lo = self.sb(f"hid_lo_{name}", [P, KF, S], F32R, at=self.arena + KF * 2048)
        cb = [self.sb(f"cb{j}_{name}", [P, S], at=self.arena + (2 * KF + j) * 2048) for j in range(2)]
        hd = [self.sb(f"hd_{name}", [P, S], at=self.arena + (2 * KF + 2) * 2048)] * 2

        def up_group(f0, k, step, banks, ex=None):
            def pieces(u):
                cols = bass.ds(f0 * P, 256) if not isinstance(f0, int) else slice(f0 * P, f0 * P + 256)
                for half, w in enumerate((gate_w, up_w)):
                    yield (slice(0, 2), slice(half * 256, half * 256 + 256)), \
                        w[2 * u * P:(2 * u + 2) * P, cols].rearrange("(kk p) c -> p kk c", p=P)
            self.group(k, step, banks, pieces, extra=ex)
            self.group_done(a, k + 3, step)
            self.group_done(v, k + 3, step)
            for j in range(2):
                pa, pv = self.ps[:, banks[j], :], self.ps[:, banks[2 + j], :]
                f = f0 + j
                if conv:
                    wt, bias = conv

                    def tap(n):
                        return wt[:, n, bass.ds(f, 1)] if not isinstance(f, int) else wt[:, n, f:f + 1]
                    bc = bias[:, bass.ds(f, 1)] if not isinstance(f, int) else bias[:, f:f + 1]
                    v.wait(f"hd{j}")
                    v.did(nc.vector.tensor_scalar(cb[j][:, :], pa, tap(2), bc, ALU.mult, ALU.add), "cv")
                    v.wait("cv")
                    v.did(nc.vector.scalar_tensor_tensor(cb[j][:, 1:S], pa[:, 0:S - 1], tap(1), cb[j][:, 1:S],
                                                         ALU.mult, ALU.add), "cv")
                    v.wait("cv")
                    v.did(nc.vector.scalar_tensor_tensor(cb[j][:, 2:S], pa[:, 0:S - 2], tap(0), cb[j][:, 2:S],
                                                         ALU.mult, ALU.add), "cv")
                    self.pr.events[f"bank{banks[j]}"] = self.pr.events["cv"]
                    a.wait("cv")
                    a.did(nc.scalar.activation(cb[j][:, :], cb[j][:, :], ACT.Silu), f"silu{j}")
                else:
                    a.wait(f"hd{j}")
                    a.did(nc.scalar.activation(cb[j][:, :], pa, ACT.Silu), f"silu{j}")
                    self.pr.events[f"bank{banks[j]}"] = self.pr.events[f"silu{j}"]
                v.wait(f"silu{j}", f"hid{1 - j}")
                v.did(nc.vector.tensor_tensor(hd[j][:, :], cb[j][:, :], pv, ALU.mult), f"hd{j}")
                self.pr.events[f"bank{banks[2 + j]}"] = self.pr.events[f"hd{j}"]
                dst_hi = hid_hi[:, bass.ds(f, 1), :] if not isinstance(f, int) else hid_hi[:, f:f + 1, :]
                dst_lo = hid_lo[:, bass.ds(f, 1), :] if not isinstance(f, int) else hid_lo[:, f:f + 1, :]
                src = hd[j][:, :].unsqueeze(1)
                a.wait(f"hd{j}")
                a.did(nc.scalar.activation(dst_hi, src, ACT.Copy), f"hid_hi{j}")
                v.wait(f"hid_hi{j}")
                v.did(nc.vector.tensor_tensor(dst_lo, src, dst_hi.bitcast(F32), ALU.subtract), f"hid{j}")

        def body(i):
            for gi in range(2):
                up_group(4 * i + 2 * gi, 4 * gi, 8, range(4 * gi, 4 * gi + 4),
                         (lambda u, gi=gi: extra(i, 4 * gi + u)) if extra else None)
        for n in ("hd0", "hd1"):
            self.pr.events.pop(n, None)
        self.pr.run_loop(name, KF // 4, body)
        self.U += 8 * (KF // 4)
        if extra:
            self.M += 8 * (KF // 4)
        up_group(KF - 2, 0, 0, range(0, 4))
        self.U += 4

        def down_unit(kt, k, step, start, stop):
            rows = bass.ds(kt * P, P) if not isinstance(kt, int) else slice(kt * P, (kt + 1) * P)

            def halves(raw):
                for c in range(2):
                    yield raw[:, c * 512:(c + 1) * 512], down_w[rows, c * 512:(c + 1) * 512]

            def products(hi, lo):
                for n in range(KD):
                    out = self.ps[:, n, :]
                    ht = hid_hi[:, bass.ds(kt, 1), :] if not isinstance(kt, int) else hid_hi[:, kt, :]
                    lt = hid_lo[:, bass.ds(kt, 1), :] if not isinstance(kt, int) else hid_lo[:, kt, :]
                    yield out, hi[:, n * P:(n + 1) * P], ht, start, False
                    yield out, hi[:, n * P:(n + 1) * P], lt, False, False
                    yield out, lo[:, n * P:(n + 1) * P], ht, False, stop
            self.load_unit(halves, k, step)
            self.multiply_unit(products, k, step)
            self.split_unit(k=k + 2, step=step)
        if after_up:
            after_up()
        p.wait("hid0", "hid1", *[f"bank{b}" for b in range(8)])
        for kt in range(2):
            down_unit(kt, 0, 0, kt == 0, False)
            self.U += 1

        def down_body(i):
            for j in range(4):
                down_unit(4 * i + 2 + j, j, 4, False, False)
        n = (KF - 2) // 4 - 1
        self.pr.run_loop(name + "_down", n, down_body)
        self.U += 4 * n
        for kt in range(4 * n + 2, KF):
            down_unit(kt, 0, 0, False, kt == KF - 1)
            self.U += 1
        self.v.reach(self.s_mm, self.U + SPL)
        self.v.wait(*need)
        for n in range(KD):
            self.add_to_x(n, n, gain)

    def finish_early(self):
        self.store_x()
        self.pr.learned["units"] = self.U
        return self.pr.learned

    def attend(self, n, q, k, bias, values, out, mx, rs, first):
        nc, v, a, p = self.nc, self.v, self.a, self.p
        j = self.blk % 2
        self.blk += 1
        w = n * P
        sc, prob, probT = self.at_s[j], self.at_p[j], self.at_t[j]
        p.wait(f"bank{j}")
        p.settle(True)
        p.did(nc.tensor.matmul(self.ps[:, j, 0:w], q, k, start=True, stop=True), f"qk{j}")
        v.wait(f"qk{j}", f"exp{j}")
        v.settle(True)
        v.did(nc.vector.tensor_tensor_reduce(sc[:, 0:w], self.ps[:, j, 0:w], bias, 1.0, -3e38,
                                             ALU.add, ALU.max, mx), f"bank{j}")
        v.wait(f"bank{j}")
        v.did(nc.vector.tensor_scalar(mx, mx, -1.0, None, ALU.mult), f"mx{j}")
        a.wait(f"mx{j}", f"pt{j}")
        a.did(nc.scalar.activation(prob[:, 0:w], sc[:, 0:w], ACT.Exp, bias=mx, accum_out=rs), f"exp{j}")
        p.wait(f"exp{j}", f"bank{2 + j}")
        for s in range(n):
            ins = nc.tensor.transpose(self.ps[:, 2 + j, s * P:(s + 1) * P], prob[:, s * P:(s + 1) * P],
                                      self.c("ident"))
        p.did(ins, f"pt{j}")
        e = v if j else a
        e.wait(f"pt{j}", f"pv{j}")
        if j:
            v.did(nc.vector.tensor_copy(probT[:, 0:w], self.ps[:, 2 + j, 0:w]), f"bank{2 + j}")
        else:
            a.did(nc.scalar.activation(probT[:, 0:w], self.ps[:, 2 + j, 0:w], ACT.Copy), f"bank{2 + j}")
        pend = (n, probT, values, out, j, f"bank{2 + j}", first)
        return pend

    def attend_values(self, pend):
        n, probT, values, out, j, ready, first = pend
        self.p.wait(ready, *first)
        for s in range(n):
            ins = self.nc.tensor.matmul(out, probT[:, s * P:(s + 1) * P], values(s), start=s == 0, stop=s == n - 1)
        self.p.did(ins, f"pv{j}")

    def attention_scratch(self, tag, at):
        self.at_s = [self.sb(f"at_s{j}{tag}", [P, S], at=at + j * 2048) for j in range(2)]
        self.at_p = [self.sb(f"at_p{j}{tag}", [P, S], at=at + (2 + j) * 2048) for j in range(2)]
        self.at_t = [self.sb(f"at_t{j}{tag}", [P, S], at=at + (4 + j) * 2048) for j in range(2)]
        return at + 6 * 2048

    def forget(self, *names):
        for n in names:
            self.pr.events.pop(n, None)

    def nsa_weights(self):
        nc, io = self.nc, self.io
        self.w1 = self.sb("nsa_w1", [64, 2, 32, 64], at=self.arena + 74752)
        self.w2 = self.small[0:64, 64:192].rearrange("p (a b) -> p a b", a=2)
        self.pe_rows = self.small[0:64, 192:256]
        for kv in range(2):
            nc.scalar.dma_start(self.w1[:, kv, :, :], io["nsa_cmp_w1"][0, kv].rearrange("(l d) h -> d l h", d=64)) \
                .then_inc(self.s_c2, 16)
            nc.scalar.dma_start(self.w2[:, kv, :], io["nsa_cmp_w2"][0, kv]).then_inc(self.s_c2, 16)
        nc.scalar.dma_start(self.pe_rows, io["nsa_cmp_pe"][0].rearrange("a l d -> (a l) d")).then_inc(self.s_c2, 16)
        self.n_c2 += 5 * 16

    def nsa_in(self):
        nc, v, a, w = self.nc, self.v, self.a, self.io["nsa_w_in"][0]
        ar = self.arena
        self.nq = self.sb("nsa_q", [64, 16, S], at=ar)
        self.nk = self.sb("nsa_k", [64, 8, S], at=ar + 32768)
        self.nc_kv = self.sb("nsa_ckv", [64, 8, S], at=ar + 49152)
        self.nv = self.sb("nsa_v", [P, TT, S], at=ar + 65536)
        self.gate = self.sb("nsa_gate", [P, TT, 48], at=ar + 73728)

        def cols(a0, n=512):
            return slice(a0, a0 + n)

        def strided(off):
            def pieces(u):
                for kk in range(2):
                    kt = 2 * u + kk
                    src = w[kt * P:(kt + 1) * P, 1536:2560].rearrange("p (b c) -> p b c", b=2)[:, :, off:off + 256]
                    yield (kk, slice(0, 512)), src
            return pieces

        groups = [("feature", lambda u: self.k_tiles(w, u, cols(0)), [(self.nq, n) for n in range(4)]),
                  ("feature", lambda u: self.k_tiles(w, u, cols(512)), [(self.nq, n) for n in range(4, 8)]),
                  ("feature", lambda u: self.k_tiles(w, u, cols(1024)), [(self.nc_kv, n) for n in range(4)]),
                  ("feature", strided(0), [(self.nk, n) for n in range(4)]),
                  ("token", strided(256), None),
                  ("token", lambda u: self.k_tiles(w, u, cols(2560, 48)), None)]
        for gi, (kind, pieces, dsts) in enumerate(groups):
            banks = range(4 * (gi % 2), 4 * (gi % 2) + 4)
            self.group(0, 0, banks, pieces, kind=kind, width=48 if gi == 5 else 512)
            self.group_done(a, 3)
            self.group_done(v, 3)
            for n, b in enumerate(banks):
                if kind == "feature":
                    dst, tile = dsts[n]
                    s = 0.125 if dst is self.nq else 1.0
                    a.did(nc.scalar.activation(dst[:, 2 * tile, :], self.ps[0:64, b, :], ACT.Copy, scale=s), f"half{b}")
                    v.wait(f"half{b}")
                    v.did(nc.vector.tensor_scalar(dst[:, 2 * tile + 1, :], self.ps[64:128, b, :], s, None,
                                                  ALU.mult), f"bank{b}")
                elif gi == 4:
                    v.did(nc.vector.tensor_copy(self.nv[:, n, :], self.ps[:, b, :]), f"bank{b}")
                else:
                    a.did(nc.scalar.activation(self.gate[:, n, :], self.ps[:, b, 0:48], ACT.Sigmoid), f"bank{b}")
            self.U += 4

    def nsa_compress(self):
        nc, v, a, p, g = self.nc, self.v, self.a, self.p, self.g
        hs = self.tmp("c_hs", [64, 2, 4, 31])
        self.kc = self.tmp("c_kc", [64, 4, 32])
        self.vbd = self.tmp("c_vbd", [P, 4, 4, 64])
        peT, bias = self.tmp("c_peT", [64, 64]), self.tmp("c_bias", [64, 2])
        v.did(nc.vector.memset(self.kc[:, :, :], 0.0), "kc0")
        v.did(nc.vector.memset(self.vbd[:, :, :, :], 0.0), "vbd0")
        for e in (p, v, a):
            e.reach(self.s_c2, self.n_c2)
        p.wait("bank0")
        p.did(nc.tensor.transpose(self.ps[0:64, 0, 0:64], self.pe_rows[:, :], self.c("ident")[0:64, 0:64]), "peT")
        v.wait("peT")
        v.did(nc.vector.tensor_copy(peT[:, :], self.ps[0:64, 0, 0:64]), "bank0")
        for kv in range(2):
            p.wait(f"bank{1 + kv}", "bank0", f"bank{3 + kv}")
            for l in range(32):
                nc.tensor.matmul(self.ps[0:64, 1 + kv, 0:124], self.w1[:, kv, l, :],
                                 self.nc_kv[:, 4 * kv:4 * kv + 4, l:l + 16 * 30 + 1:16],
                                 start=l == 0, stop=l == 31)
            for l in range(32):
                ins = nc.tensor.matmul(self.ps[0:64, 3 + kv, 0:1], self.w1[:, kv, l, :],
                                       peT[:, kv * 32 + l:kv * 32 + l + 1], start=l == 0, stop=l == 31)
            p.did(ins, f"hid_c{kv}")
            v.wait(f"hid_c{kv}")
            v.did(nc.vector.tensor_copy(bias[:, kv:kv + 1], self.ps[0:64, 3 + kv, 0:1]), f"bank{3 + kv}")
            a.wait(f"bank{3 + kv}")
            a.did(nc.scalar.activation(hs[:, kv, :, :], self.ps[0:64, 1 + kv, 0:124].rearrange("p (a b) -> p a b", a=4),
                                       ACT.Silu, bias=bias[:, kv:kv + 1]), f"bank{1 + kv}")
        p.wait("bank1", "bank2", "bank5", "bank6")
        ins = nc.tensor.matmul(self.ps[0:64, 5, 0:124], self.w2[:, 0, :], hs[:, 0, :, :], start=True, stop=True)
        p.did(ins, "kc_p")
        v.wait("kc_p", "kc0")
        v.did(nc.vector.tensor_copy(self.kc[:, :, 0:31], self.ps[0:64, 5, 0:124].rearrange("p (a b) -> p a b", a=4)), "bank5")
        for j in range(4):
            for gr in range(4):
                ins = nc.tensor.matmul(self.ps[32 * j:32 * j + 31, 6, gr * 64:(gr + 1) * 64], hs[:, 1, gr, :],
                                       self.w2[:, 1, :], start=True, stop=True)
        p.did(ins, "vc_p")
        v.wait("vc_p", "vbd0")
        for j in range(4):
            v.did(nc.vector.tensor_copy(self.vbd[32 * j:32 * j + 31, :, j, :],
                                        self.ps[32 * j:32 * j + 31, 6, 0:256].rearrange("p (g d) -> p g d", g=4)), "bank6")

    def nsa_mix(self):
        nc, v, a, p, g = self.nc, self.v, self.a, self.p, self.g
        at = [self.h_at]

        def tmp(name, shape, dt=F32):
            t = self.sb(name, shape, dt, at=at[0])
            at[0] += (int(np.prod(shape[1:])) * 4 + 31) // 32 * 32
            assert at[0] <= self.h_at + 32768
            return t
        self.tmp = tmp
        for e in (a, v):
            e.wait("bank0", "bank4", "bank5", "bank6", "bank7")
        self.nsa_compress()
        at[0] = self.attention_scratch("n", at[0])
        qst = tmp("n_q", [64, 4, S])
        bs = [tmp(f"n_b{j}", [P, S]) for j in range(2)]
        o_tok = self.sb("o_tok", [P, TT, D], at=self.arena + 74752)
        base = self.arena + 49152
        spc, self_bc, pT, ot1 = (self.sb(f"n_x{i}", [P, S], at=base + i * 2048) for i in range(4))
        st = self.sb("n_stat", [P, 8, 16], at=base + 8192)
        cm, rc, fc = st[:, 0, :], st[:, 1, :], st[:, 2, :]
        mxs = self.sb("n_mx", [P, 8], at=base + 8192 + 512)
        rs = self.sb("n_rs", [P, 2, 4, 2], at=base + 8192 + 576)
        fac = self.sb("n_fac", [P, 2, 4, 2], at=base + 8192 + 640)
        C, Cc, slope, ok = self.c2["dist"], self.c2["dist_c"], self.c2["slope"], self.c2["seen"]
        O = [4, 5]
        self.blk = 0
        self.forget("pt0", "pt1", "pv0", "pv1", "exp0", "exp1", "qk0", "qk1", "mx0", "mx1", "qst", "b_used0", "b_used1")
        for e in (a, v, p, g):
            for n in range(8):
                e.wait(f"bank{n}")

        def body(i):
            a.wait("qk0", "qk1", "cs")
            a.did(nc.scalar.activation(qst[:, :, :], self.nq[:, bass.ds(4 * i, 4), :], ACT.Copy), "qst")
            p.wait("qst", "bank6")
            p.settle(True)
            for t in range(TT):
                for j in range(4):
                    c0 = (t * 4 + j) * 32
                    ins = nc.tensor.matmul(self.ps[:, 6, c0:c0 + 32], qst[:, j, t * P:(t + 1) * P],
                                           self.kc[:, bass.ds(i, 1), :], start=True, stop=True)
            p.did(ins, "cs")
            v.wait("cT")
            for j in range(4):
                dst = self_bc[:, :].rearrange("p (t j n) -> p t j n", t=TT, j=4)[:, :, j, :]
                v.did(nc.vector.tensor_scalar(dst, Cc.rearrange("p (t n) -> p t n", t=TT),
                                              slope[:, bass.ds(4 * i + j, 1)], None, ALU.mult), "bc")
            v.wait("bc", "cs")
            v.did(nc.vector.tensor_tensor(spc[:, :], self.ps[:, 6, :], self_bc[:, :], ALU.add), "bank6")
            v.wait("bank6")
            s3 = spc[:, :].rearrange("p (r n) -> p r n", n=32)
            v.did(nc.vector.tensor_reduce(cm, s3, AX.X, ALU.max), "cm")
            v.wait("cm")
            v.did(nc.vector.tensor_tensor(s3, s3, cm.unsqueeze(2).broadcast_to([P, 16, 32]), ALU.subtract), "cm")
            a.wait("cm")
            a.did(nc.scalar.activation(spc[:, :], spc[:, :], ACT.Exp), "ce")
            v.wait("ce")
            v.did(nc.vector.tensor_reduce(rc, s3, AX.X, ALU.add), "cm")
            v.wait("cm")
            v.did(nc.vector.reciprocal(rc, rc), "cm")
            v.wait("cm")
            v.did(nc.vector.tensor_tensor(rc, rc, ok, ALU.mult), "cm")
            v.wait("cm")
            gt = self.gate[:, :, bass.ds(12 * i, 12)].rearrange("p t (j b) -> p t j b", b=3)
            v.did(nc.vector.tensor_tensor(fc.rearrange("p (t j) -> p t j", t=TT), rc.rearrange("p (t j) -> p t j", t=TT),
                                          gt[:, :, :, 0], ALU.mult), "fc")
            p.wait("ce", "bank7")
            for t in range(TT):
                ins = nc.tensor.transpose(self.ps[:, 7, t * P:(t + 1) * P], spc[:, t * P:(t + 1) * P], self.c("ident"))
            p.did(ins, "cT")
            a.wait("cT", "cv")
            a.did(nc.scalar.activation(pT[:, :], self.ps[:, 7, :], ACT.Copy), "bank7")
            p.wait("bank7", "bank6")
            for t in range(TT):
                b = 7 if t < 2 else 6
                ins = nc.tensor.matmul(self.ps[:, b, (t % 2) * 256:(t % 2) * 256 + 256], pT[:, t * P:(t + 1) * P],
                                       self.vbd[:, bass.ds(i, 1), :, :], start=True, stop=True)
            p.did(ins, "cv")
            v.wait("cv", "fc")
            for half in range(2):
                dst = o_tok[:, 2 * half:2 * half + 2, bass.ds(256 * i, 256)].rearrange("p t (j d) -> p t j d", j=4)
                src = self.ps[:, 7 - half, :].rearrange("p (t j d) -> p t j d", t=2, j=4)
                f = fc.rearrange("p (t j) -> p t j", t=TT)[:, 2 * half:2 * half + 2, :].unsqueeze(3).broadcast_to([P, 2, 4, 64])
                v.did(nc.vector.tensor_tensor(dst, src, f, ALU.mult), f"bank{7 - half}")
            pend = []
            for j in range(4):
                jb = j % 2
                v.wait(f"b_used{jb}")
                v.did(nc.vector.tensor_scalar(bs[jb][:, :], C, slope[:, bass.ds(4 * i + j, 1)], None, ALU.mult), f"bias{jb}")
                v.wait(f"bias{jb}")
                for br in range(2):
                    for t in range(TT):
                        m = t * 2 + br
                        kT = self.nk[:, bass.ds(i + 4 * br, 1), 0:(t + 1) * P]
                        item = self.attend(
                            t + 1, qst[:, j, t * P:(t + 1) * P], kT, bs[jb][:, (3 - t) * P:S],
                            lambda s, br=br: self.nv[:, s, bass.ds(64 * i + 256 * br, 64)],
                            self.ps[:, O[jb], (t * 2 + br) * 64:(t * 2 + br) * 64 + 64],
                            mxs[:, self.blk % 2:self.blk % 2 + 1], rs[:, jb, t, br:br + 1], (f"bank{O[jb]}",))
                        pend.append(item)
                        if len(pend) > 1:
                            self.attend_values(pend.pop(0))
                self.pr.events[f"b_used{jb}"] = self.pr.events[f"bank{(self.blk - 1) % 2}"]
                self.attend_values(pend.pop(0))
                v.wait("exp0", "exp1")
                v.did(nc.vector.reciprocal(fac[:, jb, :, :], rs[:, jb, :, :]), "fac")
                v.wait("fac")
                gj = self.gate[:, :, bass.ds(12 * i + 3 * j + 1, 2)]
                v.did(nc.vector.tensor_tensor(fac[:, jb, :, :], fac[:, jb, :, :], gj, ALU.mult), "fac")
                v.wait("fac", "pv0", "pv1")
                for br in range(2):
                    src = self.ps[:, O[jb], :].rearrange("p (t b d) -> p t b d", t=TT, b=2)[:, :, br, :]
                    f = fac[:, jb, :, br:br + 1].broadcast_to([P, TT, 64])
                    t3 = ot1[:, br * 256:(br + 1) * 256].rearrange("p (t d) -> p t d", t=TT)
                    v.did(nc.vector.tensor_tensor(t3, src, f, ALU.mult), f"ot{br}")
                    self.pr.events[f"bank{O[jb]}"] = self.pr.events[f"ot{br}"]
                    o = o_tok[:, :, bass.ds(256 * i + 64 * j, 64)]
                    v.wait(f"ot{br}", "bank6")
                    if br:
                        v.wait("osum2")
                    v.did(nc.vector.tensor_tensor(o, o, t3, ALU.add), "osum2")
        self.pr.run_loop("nsa_heads", 4, body)
        for e in (a, v, p):
            e.wait("osum2", "qst", "pv0", "pv1")
        self.token_to_h(o_tok, 0, KD)

    def token_to_h(self, src, first, count):
        nc = self.nc
        for n in range(count):
            kt, b = first + n, n % 4
            self.p.wait(f"bank{b}")
            for t in range(TT):
                ins = nc.tensor.transpose(self.ps[:, b, t * P:(t + 1) * P], src[:, t, n * P:(n + 1) * P], self.c("ident"))
            self.p.did(ins, f"oT{b}")
            self.a.wait(f"oT{b}")
            self.a.did(nc.scalar.activation(self.h_hi[:, kt, :], self.ps[:, b, :], ACT.Copy), f"hh{b}")
            self.v.wait(f"hh{b}")
            self.v.did(nc.vector.tensor_tensor(self.h_lo[:, kt, :], self.ps[:, b, :], self.h_hi[:, kt, :].bitcast(F32),
                                               ALU.subtract), f"h{kt}")
            self.pr.events[f"bank{b}"] = self.pr.events[f"h{kt}"]

    def dsa_weights(self):
        nc, io, at = self.nc, self.io, self.arena + 89344
        self.pool_w = self.sb("pool_w", [P, 4, P], at=at)
        self.qk_gain = self.sb("qk_gain", [P, 2, 64], at=at + 2048)
        nc.scalar.dma_start(self.pool_w[:, :, :], io["pool_w_2"][0].rearrange("g c d -> c g d")).then_inc(self.s_c2, 16)
        for n, name in enumerate(("q_norm_2", "k_norm_2")):
            nc.scalar.dma_start(self.qk_gain[:, n, :], io[name].partition_broadcast(P)
                                if len(io[name].shape) == 1 else io[name][0].partition_broadcast(P)) \
                .then_inc(self.s_c2, 16)
        self.n_c2 += 48

    def dsa_in(self):
        nc, v, a, w, ar = self.nc, self.v, self.a, self.io["w_in_2"][0], self.arena
        self.tq = self.sb("dsa_q", [P, TT, S], at=ar)
        self.tk = self.sb("dsa_k", [P, TT, S], at=ar + 8192)
        self.tv = self.sb("dsa_v", [P, TT, S], at=ar + 16384)
        self.ti = self.sb("dsa_i", [P, TT, 324], at=ar + 24576)
        self.mask = self.sb("dsa_mask", [P, 10 * P], at=ar + 29760)
        self.qT = self.sb("dsa_qT", [64, 8, S], at=ar + 34880)
        self.kT = self.sb("dsa_kT", [64, 8, S], at=ar + 51264)
        self.iT = self.sb("dsa_iT", [64, 5, S], at=ar + 67648)
        self.u = self.sb("dsa_u", [P, 4, S], at=ar + 77888)
        groups = [("token", 1536, 324, self.ti), ("token", 0, 512, self.tq), ("token", 512, 512, self.tk),
                  ("token", 1024, 512, self.tv), ("feature", 1860, 512, self.u)]
        for gi, (kind, c0, width, dst) in enumerate(groups):
            banks = range(4 * (gi % 2), 4 * (gi % 2) + 4)
            self.group(0, 0, banks, lambda u: self.k_tiles(w, u, slice(c0, c0 + width)), kind=kind, width=width)
            for n, b in enumerate(banks):
                e = (a, v)[n % 2]
                if n < 2:
                    self.group_done(e, 3)
                src = self.ps[:, b, 0:width]
                e.did(nc.scalar.activation(dst[:, n, :], src, ACT.Copy) if e is a
                      else nc.vector.tensor_copy(dst[:, n, :], src), f"bank{b}")
                self.pr.events[f"g{gi}_{n}"] = self.pr.events[f"bank{b}"]
            self.U += 4

    def rotate(self, x, heads, half, cs, sn, tables=None):
        nc, v = self.nc, self.v
        x1, x2 = x[:, :, :, 0:half], x[:, :, :, half:2 * half]
        t = [b[:, 0:TT * heads * half].rearrange("p (t h d) -> p t h d", t=TT, h=heads) for b in self.rt]
        c1, s2, c2, s1 = tables or (cs, sn, cs, sn)

        def wide(tb):
            return tb.rearrange("p (t d) -> p t d", t=TT).unsqueeze(2).broadcast_to([P, TT, heads, half])
        v.wait("rot")
        v.did(nc.vector.tensor_tensor(t[0], x1, wide(c1), ALU.mult))
        v.did(nc.vector.tensor_tensor(t[1], x2, wide(s2), ALU.mult))
        v.did(nc.vector.tensor_tensor(t[2], x2, wide(c2), ALU.mult))
        v.did(nc.vector.tensor_tensor(t[3], x1, wide(s1), ALU.mult), "rot")
        v.wait("rot")
        v.did(nc.vector.tensor_tensor(x1, t[0], t[1], ALU.subtract))
        v.did(nc.vector.tensor_tensor(x2, t[2], t[3], ALU.add), "rot")

    def heads_out(self, x, heads, dst, scale, base):
        for h in range(heads):
            b = base + h % 2
            self.p.wait(f"bank{b}", "rot")
            for t in range(TT):
                ins = self.nc.tensor.transpose(self.ps[0:64, b, t * P:(t + 1) * P], x[:, t, h * 64:(h + 1) * 64],
                                               self.c("ident"))
            self.p.did(ins, f"ho{b}")
            self.a.wait(f"ho{b}")
            self.a.did(self.nc.scalar.activation(dst[:, h, :], self.ps[0:64, b, :], ACT.Copy, scale=scale), f"bank{b}")
            self.pr.events["heads"] = self.pr.events[f"bank{b}"]

    def dsa_mix(self):
        nc, v, a, p, g = self.nc, self.v, self.a, self.p, self.g
        hb = self.h_at
        self.rt = [self.sb(f"rt{j}", [P, 1024], at=hb + j * 4096) for j in range(4)]
        sm = self.sb("dsa_small", [P, 256], at=hb + 16384 - 1024)
        cs, sn, ci, si = (self.c2[n] for n in ("cos", "sin", "cos_i", "sin_i"))
        for e in (v, p, a, g):
            e.reach(self.s_c2, self.n_c2)
            e.wait(*[f"bank{n}" for n in range(8)])
        v.did(nc.vector.tensor_scalar(self.ti[:, :, 320:324], self.ti[:, :, 320:324], (4 ** -0.5) * (64 ** -0.5),
                                      None, ALU.mult), "wi")
        i4 = self.ti[:, :, 0:320].rearrange("p t (h d) -> p t h d", d=64)
        self.rotate(i4, 5, 16, ci, si)
        self.heads_out(self.ti, 5, self.iT, 1.0, 0)
        off = [0, P, 3 * P, 6 * P]
        rl = [self.sb(f"relu{j}", [P, S], at=hb + 16384 + j * 2048) for j in range(2)]
        n = 0
        v.did(nc.vector.tensor_copy(self.mask[:, 0:P], self.c2["tri"]), "sc0")
        for t in range(1, TT):
            w = (t + 1) * P
            m = self.mask[:, off[t]:off[t] + w]
            for h in range(4):
                j = n % 2
                n += 1
                p.wait("heads", f"bank{2 + j}")
                p.did(nc.tensor.matmul(self.ps[:, 2 + j, 0:w], self.iT[:, h, t * P:(t + 1) * P], self.iT[:, 4, 0:w],
                                       start=True, stop=True), f"is{j}")
                a.wait(f"is{j}", f"relu_used{j}")
                a.did(nc.scalar.activation(rl[j][:, 0:w], self.ps[:, 2 + j, 0:w], ACT.Relu), f"bank{2 + j}")
                v.wait(f"bank{2 + j}", "wi")
                wc = self.ti[:, t, 320 + h:321 + h]
                if h == 0:
                    v.did(nc.vector.tensor_scalar(m, rl[j][:, 0:w], wc, None, ALU.mult), "acc")
                else:
                    v.wait("acc")
                    v.did(nc.vector.scalar_tensor_tensor(m, rl[j][:, 0:w], wc, m, ALU.mult, ALU.add), "acc")
                self.pr.events[f"relu_used{j}"] = self.pr.events["acc"]
            v.wait("acc")
            v.did(nc.vector.tensor_tensor(m[:, t * P:w], m[:, t * P:w], self.c2["tri"], ALU.add), f"sc{t}")
        sq = self.sb("dsa_sq", [P, TT, S], at=self.arena + 51264)
        ss, tabs = self.sb("dsa_ss", [P, 32], at=hb + 24576), self.sb("dsa_tab", [P, 4, P], at=hb + 24576 + 128)
        for n, (x, dst, scale) in enumerate(((self.tq, self.qT, 0.125), (self.tk, self.kT, 1.0))):
            gain = self.qk_gain[:, n, :]
            x4 = x[:, :, :].rearrange("p t (h d) -> p (t h) d", d=64)
            a.wait("ssum", f"g{n + 1}_0", f"g{n + 1}_1", f"g{n + 1}_3")
            v.wait(f"g{n + 1}_0", f"g{n + 1}_2", "rot")
            a.did(nc.scalar.activation(sq[:, :, :], x[:, :, :], ACT.Square), "qsq")
            v.wait("qsq")
            v.did(nc.vector.tensor_reduce(ss[:, :], sq[:, :, :].rearrange("p t (h d) -> p (t h) d", d=64), AX.X, ALU.add), "ssum")
            a.wait("ssum")
            a.did(nc.scalar.activation(ss[:, :], ss[:, :], ACT.Ln, bias=self.eps, scale=1.0 / 64), "sln")
            a.wait("sln")
            a.did(nc.scalar.activation(ss[:, :], ss[:, :], ACT.Exp, scale=-0.5), "sln")
            for k, (tb, off_g) in enumerate(((cs, 0), (sn, 32), (cs, 32), (sn, 0))):
                v.did(nc.vector.tensor_tensor(tabs[:, k, :].rearrange("p (t d) -> p t d", t=TT),
                                              tb.rearrange("p (t d) -> p t d", t=TT),
                                              gain[:, off_g:off_g + 32].unsqueeze(1).broadcast_to([P, TT, 32]),
                                              ALU.mult), "tab")
            v.wait("sln", "tab")
            v.did(nc.vector.tensor_tensor(x4, x4, ss[:, :].unsqueeze(2).broadcast_to([P, 32, 64]), ALU.mult), "rot")
            self.rotate(x[:, :, :].rearrange("p t (h d) -> p t h d", d=64), 8, 32, None, None,
                        tables=[tabs[:, k, :] for k in range(4)])
            if n == 0:
                self.heads_out(x, 8, dst, scale, 0)
        bufs = [self.sb(f"pool{j}", [P, 4, S], at=hb + 16384 + j * 8192) for j in range(2)]
        mx8 = self.small[:, 192:200]
        for t in range(1, TT):
            w = (t + 1) * P
            m = self.mask[:, off[t]:off[t] + w]

            def rounds(i, m=m, t=t):
                v.wait("mr", f"sc{t}")
                v.did(nc.vector.max(mx8, m), "m8")
                v.wait("m8")
                v.settle(True)
                v.did(nc.vector.match_replace(m, mx8, m, -3.3e38), "mr")
            for i in range(P // 8):
                rounds(i)
            v.wait("mr")
            v.did(nc.vector.tensor_scalar(m, m, -3.2e38, NEG, ALU.is_gt, ALU.mult), "mask")
        self.heads_out(self.tk, 8, self.kT, 1.0, 0)
        a.wait("heads")
        g.wait("acc", "rot", "heads")
        src = self.u
        for step in range(4):
            sh, dst = 1 << step, bufs[step % 2]
            g.wait("pl")
            g.did(nc.gpsimd.tensor_tensor(dst[:, step:4, sh:S], src[:, step:4, sh:S], src[:, step:4, 0:S - sh], ALU.add))
            g.did(nc.gpsimd.tensor_copy(dst[:, step:4, 0:sh], src[:, step:4, 0:sh]), "pl")
            d, uu = dst[:, step, :], self.u[:, step, :]
            v.wait("pl")
            corr = self.c2["corr"][:, step * 16:(step + 1) * 16]
            v.did(nc.vector.tensor_tensor(d[:, 0:16], d[:, 0:16], corr, ALU.mult), "pc")
            v.wait("pc")
            v.did(nc.vector.scalar_tensor_tensor(uu, d, 1.0 / (2 * sh), uu, ALU.mult, ALU.subtract), f"pooled{step}")
            self.pr.events["pooled"] = self.pr.events[f"pooled{step}"]
            g.wait(f"pooled{step}")
            src = dst
        self.attention_scratch("d", hb)
        qst = [self.sb(f"d_q{j}", [64, S], at=hb + 12288 + j * 2048) for j in range(2)]
        o_tok = self.sb("d_o", [P, TT, S], at=self.arena)
        st = self.sb("d_st", [P, 32], at=self.arena + 8192)
        mxs, rs, fac = st[:, 0:2], st[:, 8:16].rearrange("p (j t) -> p j t", j=2), \
            st[:, 16:24].rearrange("p (j t) -> p j t", j=2)
        self.blk = 0
        self.forget("pt0", "pt1", "pv0", "pv1", "exp0", "exp1", "qk0", "qk1", "mx0", "mx1", "qst0", "qst1")
        for e in (a, v, p):
            e.wait("mask", "rot", "heads", "pooled", "relu_used0", "relu_used1", *[f"bank{n}" for n in range(8)])

        def body(i):
            pend = []
            for j in range(2):
                a.wait(f"q_used{j}")
                a.did(nc.scalar.activation(qst[j][:, :].unsqueeze(1), self.qT[:, bass.ds(2 * i + j, 1), :], ACT.Copy), f"qst{j}")
                p.wait(f"qst{j}")
                for t in range(TT):
                    item = self.attend(
                        t + 1, qst[j][:, t * P:(t + 1) * P], self.kT[:, bass.ds(2 * i + j, 1), 0:(t + 1) * P],
                        self.mask[:, off[t]:off[t] + (t + 1) * P],
                        lambda s, j=j: self.tv[:, s, bass.ds(128 * i + 64 * j, 64)],
                        self.ps[:, 4 + j, t * 64:t * 64 + 64], mxs[:, self.blk % 2:self.blk % 2 + 1],
                        rs[:, j, t:t + 1], (f"bank{4 + j}",))
                    pend.append(item)
                    if len(pend) > 1:
                        self.attend_values(pend.pop(0))
                self.pr.events[f"q_used{j}"] = self.pr.events[f"qk{(self.blk - 1) % 2}"]
                self.attend_values(pend.pop(0))
                v.wait("exp0", "exp1")
                v.did(nc.vector.reciprocal(fac[:, j, :], rs[:, j, :]), "fac")
                v.wait("fac", "pv0", "pv1")
                v.did(nc.vector.tensor_tensor(o_tok[:, :, bass.ds(128 * i + 64 * j, 64)],
                                              self.ps[:, 4 + j, 0:256].rearrange("p (t d) -> p t d", t=TT),
                                              fac[:, j, :].unsqueeze(2).broadcast_to([P, TT, 64]), ALU.mult), f"bank{4 + j}")
        self.pr.run_loop("dsa_heads", 4, body)
        for e in (a, v, p):
            e.wait("bank4", "bank5", "qst0", "qst1", "pv0", "pv1")
        self.token_to_h(o_tok, 0, 4)
        for n in range(4):
            b = 4 + n
            p.wait(f"bank{b}")
            p.did(nc.tensor.matmul(self.ps[:, b, :], self.pool_w[:, n, :], self.u[:, n, :], start=True, stop=True), f"pw{n}")
            v.wait(f"pw{n}")
            v.did(nc.vector.tensor_scalar(self.u[:, n, :], self.ps[:, b, :], self.pool_scale[:, n:n + 1], None,
                                          ALU.mult), f"bank{b}")
            a.wait(f"bank{b}")
            a.did(nc.scalar.activation(self.h_hi[:, 4 + n, :], self.u[:, n, :], ACT.Copy), f"hh{n}")
            v.wait(f"hh{n}")
            v.did(nc.vector.tensor_tensor(self.h_lo[:, 4 + n, :], self.u[:, n, :], self.h_hi[:, 4 + n, :].bitcast(F32),
                                          ALU.subtract), f"h{4 + n}")

    def store_x(self):
        nc = self.nc
        ot = self.sb("out_tok", [P, TT, D], at=self.arena)
        out = self.io["out"].rearrange("b (t p) d -> p (b t) d", p=P)
        for t in range(TT):
            for half in range(2):
                b = (2 * t + half) % 8
                self.p.wait(f"bank{b}", *[f"x{n}" for n in range(KD)])
                for j in range(4):
                    kt = half * 4 + j
                    ins = nc.tensor.transpose(self.ps[:, b, j * P:(j + 1) * P], self.xT[:, kt, t * P:(t + 1) * P],
                                              self.c("ident"))
                self.p.did(ins, "xo")
                self.v.wait("xo")
                self.v.did(nc.vector.tensor_copy(ot[:, t, half * 512:(half + 1) * 512], self.ps[:, b, :]), "ot")
            self.s.wait("ot")
            nc.sync.dma_start(out[:, t:t + 1, :], ot[:, t:t + 1, :]).then_inc(self.s_out, 16)
        nc.sync.wait_ge(self.s_out, 16 * TT)


def bass_part(i):
    return i



def program(nc, io, const_at, per_loop):
    K = Kernel(nc, io, const_at, per_loop)
    K.names = iter(range(100))
    K.s_c2 = nc.alloc_semaphore("phase_constants_landed")
    K.n_c2 = 0

    def phase_constants(base, names):
        K.c2 = {}
        for n in names:
            o, w = K.const_at[n]
            t = K.sb(f"c2_{n}", [P, w], at=base)
            base += w * 4
            nc.scalar.dma_start(t[:, :], K.io["const2"][:, o:o + w]).then_inc(K.s_c2, 16)
            K.n_c2 += 16
            K.c2[n] = t[:, :]
    K.phase_constants = phase_constants
    K.start()
    K.lower_bounds()
    K.norm_scratch(K.arena)
    phase_constants(K.arena + 81920, [f"level{m}" for m in range(8)] + ["restart"])
    K.prologue()
    K.modulation_scales(0)
    K.norm(lambda kt: K.mod[:, 0, 1, kt:kt + 1], lambda kt: K.mod[:, 0, 0, kt:kt + 1], ("ms01", "mod00"))
    K.hgrn_in()
    for j, part in enumerate(range(2, 6)):
        K.mod_finish(0, part, j, j)
    K.modulation_scales(0)
    K.hgrn_mix()
    K.v.wait("mod_sum")
    K.out_proj(K.io["hg_w_out"][0], lambda kt: K.mod[:, 0, 2, kt:kt + 1], ("mod02",),
               extra=lambda u: K.mod_unit(1, 5, u, K.m_acc[:, 0, :], u))
    if STOP < 2:
        return K.finish_early()
    K.M += 8
    K.norm_scratch(K.arena)
    K.norm(lambda kt: K.mod[:, 0, 4, kt:kt + 1], lambda kt: K.mod[:, 0, 3, kt:kt + 1], ("ms04", "mod03"))
    K.mod_finish(1, 5, 0, 0)
    K.v.wait("mod_sum")
    K.ffn("ffn_a", K.io["ffn_w_up"][0][:, 0:FF], K.io["ffn_w_up"][0][:, FF:2 * FF], K.io["ffn_w_down"][0],
          lambda kt: K.mod[:, 0, 5, kt:kt + 1], conv=K.conv[0], need=("mod05",),
          extra=lambda i, m: K.mod_unit(1, i, m, K.m_acc[:, bass.ds(i, 1), :], m, 8))
    for part in range(5):
        K.mod_finish(1, part, part, part)
    K.modulation_scales(1)
    if STOP < 3:
        return K.finish_early()
    K.norm_scratch(K.arena)
    K.a.wait("x7")
    phase_constants(K.arena + 91136, ["dist", "dist_c", "slope", "seen"])
    K.nsa_weights()
    K.norm(lambda kt: K.mod[:, 1, 1, kt:kt + 1], lambda kt: K.mod[:, 1, 0, kt:kt + 1], ("ms11", "mod10"))
    K.nsa_in()
    K.nsa_mix()
    K.out_proj(K.io["nsa_w_out"][0], lambda kt: K.mod[:, 1, 2, kt:kt + 1], ("mod12",))
    if STOP < 4:
        return K.finish_early()
    K.norm_scratch(K.arena)
    K.norm(lambda kt: K.mod[:, 1, 4, kt:kt + 1], lambda kt: K.mod[:, 1, 3, kt:kt + 1], ("ms14", "mod13"))
    K.ffn("ffn_b", K.io["ffn_w_up"][1][:, 0:FF], K.io["ffn_w_up"][1][:, FF:2 * FF], K.io["ffn_w_down"][1],
          lambda kt: K.mod[:, 1, 5, kt:kt + 1], conv=K.conv[1], need=("mod15",))
    if STOP < 5:
        return K.finish_early()
    K.norm_scratch(K.arena)
    K.norm(lambda kt: K.norms["final_norm"][:, kt:kt + 1], None, (), into_x=True)
    K.norm(lambda kt: K.norms["ffn1_norm_2"][:, kt:kt + 1], None, ())
    K.ffn("ffn_c", K.io["ffn1_w_gate_2"][0], K.io["ffn1_w_up_2"][0], K.io["ffn1_w_down_2"][0], lambda kt: 0.5)
    if STOP < 6:
        return K.finish_early()
    K.norm_scratch(K.arena)
    K.a.wait("x7")
    phase_constants(K.arena + 91904, ["cos", "sin", "cos_i", "sin_i", "tri", "corr"])
    K.dsa_weights()
    K.norm(lambda kt: K.norms["mix_norm_2"][:, kt:kt + 1], None, ())
    K.dsa_in()
    K.dsa_mix()
    K.out_proj(K.io["w_out_2"][0], lambda kt: 1.0, ())
    K.norm_scratch(K.arena)
    K.norm(lambda kt: K.norms["ffn2_norm_2"][:, kt:kt + 1], None, ())
    K.ffn("ffn_d", K.io["ffn2_w_gate_2"][0], K.io["ffn2_w_up_2"][0], K.io["ffn2_w_down_2"][0], lambda kt: 0.5)
    return K.finish_early()


_OUT = (1, S, D)


def kernel(**inputs):
    import concourse.bacc as bacc
    from concourse.bass_utils import run_bass_kernel_spmd
    table, const_at = constants()
    small = const_at["ones"][0] + P
    arrays = {"const": np.ascontiguousarray(table[:, :small]), "const2": table}
    arrays.update({n: np.ascontiguousarray(a) for n, a in inputs.items()})

    def build(per_loop):
        nc = bacc.Bacc("TRN2", target_bir_lowering=False, num_devices=1)
        io = {}
        for n, a in arrays.items():
            io[n] = nc.dram_tensor("in_" + n, a.shape, mybir.dt.from_np(a.dtype), kind="ExternalInput").ap()
        io["out"] = nc.dram_tensor("out", _OUT, F32, kind="ExternalOutput").ap()
        return nc, program(nc, io, const_at, per_loop)
    _, counts = build({})
    nc, _ = build(counts)
    r = run_bass_kernel_spmd(nc, [{"in_" + n: a for n, a in arrays.items()}], core_ids=[0])
    return r.results[0]["out"]
```

```python
import numpy as np

import concourse.bass as bass
import concourse.mybir as mybir

F32 = mybir.dt.float32
F32R = mybir.dt.float32r
I32 = mybir.dt.int32
ALU = mybir.AluOpType
ACT = mybir.ActivationFunctionType
AX = mybir.AxisListType

P = 128
S = 512
D = 1024
KD = D // P
TT = S // P
FF = 2816
KF = FF // P
EPS = 1e-6
NEG = -1e30
RAW = 4
SPL = 2
STOP = 99


class Event:
    def __init__(self, eng, const, loop=None):
        self.eng, self.const, self.loop = eng, const, loop


class Engine:
    def __init__(self, prog, name, raw):
        self.prog, self.name, self.e = prog, name, raw
        self.sem = prog.nc.alloc_semaphore("done_" + name)
        self.n = 0
        self.seen = {}

    def did(self, instruction, name=None):
        instruction.then_inc(self.sem, 1)
        self.n += 1
        if name is not None:
            self.prog.events[name] = Event(self, self.n, self.prog.loop)
        return instruction

    def wait(self, *names):
        for name in names:
            self.prog.wait(self, name)

    def reach(self, sem, const, step=0):
        loop = self.prog.loop
        if loop is None or step == 0:
            if const > 0:
                self.e.wait_ge(sem, const)
        else:
            assert const > 0, const
            self.e.wait_ge(sem, loop["i"] * step + const)
            self.settle()

    def settle(self, always=False):
        if (always or self.name in ("scalar", "gpsimd")) and self.prog.loop is not None:
            self.e.sem_inc(self.prog.settled[self.name], 1)


class Program:
    def __init__(self, nc, per_loop):
        self.nc = nc
        self.per_loop = per_loop
        self.learned = {}
        self.events = {}
        self.loop = None
        self.v = Engine(self, "vector", nc.vector)
        self.a = Engine(self, "scalar", nc.scalar)
        self.g = Engine(self, "gpsimd", nc.gpsimd)
        self.p = Engine(self, "tensor", nc.tensor)
        self.s = Engine(self, "sync", nc.sync)
        self.settled = {n: nc.alloc_semaphore("settled_" + n) for n in ("scalar", "gpsimd", "vector", "tensor")}
        self.engines = [self.v, self.a, self.g, self.p, self.s]

    def wait(self, eng, name):
        loop = self.loop
        ev = self.events.get(name)
        here = ev is not None and loop is not None and ev.loop is loop
        if not here:
            if ev is not None:
                const = ev.const
                if ev.loop is not None:
                    L = ev.loop
                    const += (L["count"] - 1) * L["per"][ev.eng.name]
                key = (ev.eng.name, None)
                if eng.seen.get(key, 0) < const:
                    eng.e.wait_ge(ev.eng.sem, const)
                    eng.seen[key] = const
            if loop is not None and name in loop["last"]:
                producer, k = loop["last"][name]
                src = next(x for x in self.engines if x.name == producer)
                self.wait_iter(eng, src, loop["base"][producer] + k - loop["per"][producer])
            return
        self.wait_iter(eng, ev.eng, ev.const)

    def wait_iter(self, eng, src, const):
        loop = self.loop
        key = (src.name, loop["name"])
        if eng.seen.get(key, -10**9) >= const:
            return
        eng.seen[key] = const
        per = loop["per"][src.name]
        if per:
            assert const > 0, (loop["name"], const)
            eng.e.wait_ge(src.sem, loop["i"] * per + const)
            eng.settle()
        elif const > 0:
            eng.e.wait_ge(src.sem, const)

    def run_loop(self, name, count, body):
        base = {e.name: e.n for e in self.engines}
        per, last = self.per_loop.get(name, ({e.name: 0 for e in self.engines}, {}))
        with self.nc.Fori(0, count) as i:
            L = dict(name=name, i=i, count=count, base=base, per=per, last=last)
            self.loop = L
            body(i)
            self.loop = None
        made = {e.name: e.n - base[e.name] for e in self.engines}
        self.learned[name] = (made, {n: (ev.eng.name, ev.const - base[ev.eng.name])
                                     for n, ev in self.events.items() if ev.loop is L})
        L["per"] = made
        for e in self.engines:
            for src in self.engines:
                const = e.seen.pop((src.name, name), None)
                if const is not None:
                    whole = const + (count - 1) * made[src.name]
                    e.seen[(src.name, None)] = max(whole, e.seen.get((src.name, None), 0))
            e.n = base[e.name] + count * made[e.name]


def constants():
    p = np.arange(P)[:, None]
    cols, at = [], {}

    def put(name, a):
        a = np.asarray(a, np.float32).reshape(P, -1)
        at[name] = (sum(c.shape[1] for c in cols), a.shape[1])
        cols.append(a)

    put("ident", np.eye(P))
    put("ones", np.ones((P, P)))
    f = np.arange(P)[None, :]
    for m in range(7):
        hs = 1 << m
        own = (p // (2 * hs) == f // (2 * hs)) & (p // hs % 2 == 0) & (f // hs % 2 == 1)
        put(f"level{m}", own.astype(np.int32).view(np.float32))
    put("level7", (p == f).astype(np.int32).view(np.float32))
    t = np.arange(S)[None, :]
    put("restart", np.broadcast_to((t % P != 0), (P, S)))
    u = np.arange(S)[None, :]
    put("dist", np.where(u <= p + 3 * P, -(p + 3 * P - u).astype(np.float64), NEG))
    n = np.arange(32)[None, None, :]
    tok = (np.arange(TT)[None, :, None] * P + p[:, :, None])
    put("dist_c", np.where((n < 31) & (n * 16 + 31 <= tok), -(tok - (n * 16 + 15.5)), NEG))
    put("slope", np.broadcast_to(2.0 ** (-8.0 * (np.arange(16)[None, :] + 1) / 16), (P, 16)))
    put("seen", np.broadcast_to(tok >= 31, (P, TT, 4)))
    for tag, half in (("", 32), ("_i", 16)):
        inv = np.float32(10000.0) ** (-np.arange(half, dtype=np.float32) / np.float32(half))
        ang = tok[:, :, 0:1].astype(np.float32) * inv[None, None, :].astype(np.float32)
        put("cos" + tag, np.cos(ang))
        put("sin" + tag, np.sin(ang))
    put("tri", np.where(f <= p, 0.0, NEG))
    t16 = np.arange(16) + 1.0
    put("corr", np.broadcast_to(np.stack([w / np.minimum(t16, w) for w in (2, 4, 8, 16)]), (P, 4, 16)))
    return np.concatenate(cols, 1), at


class Kernel:
    def __init__(self, nc, io, const_at, per_loop):
        self.nc, self.io, self.const_at = nc, io, const_at
        self.pr = Program(nc, per_loop)
        self.v, self.a, self.g, self.p, self.s = self.pr.engines
        nc_alloc = nc.alloc_sbuf_tensor_at
        self.at = (nc.sbuf_base + 31) // 32 * 32
        self.used = 0

        def sb(name, shape, dt=F32, at=None):
            size = int(np.prod(shape[1:])) * 4
            if at is None:
                at = self.at
                self.at += (size + 31) // 32 * 32
            assert at + size <= nc.sbuf_usable_end, (name, at + size)
            return nc_alloc(name, shape, dt, offset=at)
        self.sb = sb
        width = const_at['ones'][0] + P
        self.const = sb("const", [P, width])
        self.xT = sb("xT", [P, KD, S])
        self.h_at = self.at
        self.h_hi = sb("h_hi", [P, KD, S], F32R)
        self.h_lo = sb("h_lo", [P, KD, S], F32R)
        self.w_raw = [sb(f"w_raw{i}", [P, 1024]) for i in range(RAW)]
        self.w_hi = [sb(f"w_hi{i}", [P, 1024], F32R) for i in range(SPL)]
        self.w_lo = [sb(f"w_lo{i}", [P, 1024], F32R) for i in range(SPL)]
        self.m_raw = [sb(f"m_raw{i}", [P, 1024]) for i in range(2)]
        self.m_acc = sb("m_acc", [P, 5, 1024])
        self.mod = sb("mod", [P, 2, 6, KD])
        self.cvec = sb("cvec", [P, KD])
        self.vecs = sb("vecs", [P, 4, P])
        self.small = sb("small", [P, 256])
        self.scr_at = self.at
        self.arena = self.at
        self.ps = nc.alloc_psum_tensor("ps", [P, 8, S], F32)
        sem = nc.alloc_semaphore
        self.s_raw = [sem(f"raw_landed{i}") for i in range(RAW)]
        self.s_hi = sem("weights_high")
        self.s_lo = sem("weights_low")
        self.s_mm = sem("unit_multiplied")
        self.s_m = [sem(f"mod_landed{i}") for i in range(2)]
        self.s_mac = sem("mod_unit_added")
        self.s_const = sem("constants_landed")
        self.s_out = sem("output_stored")
        self.n_const = 0
        self.U = 0
        self.US = 0
        self.M = 0

    def c(self, name):
        o, w = self.const_at[name]
        return self.const[:, o:o + w]

    def load_const(self, dst, src):
        self.nc.scalar.dma_start(dst, src).then_inc(self.s_const, 16)
        self.n_const += 16

    def load_unit(self, halves, k=0, step=0):
        u = self.U + k
        slot = u % RAW
        assert step % RAW == 0
        self.s.reach(self.s_lo, u + 1, step)
        for dst, src in halves(self.w_raw[slot]):
            self.nc.sync.dma_start(dst, src).then_inc(self.s_raw[slot], 16)

    def split_unit(self, cols=1024, k=0, step=0, view=None):
        u = self.U + k
        if u >= self.pr.per_loop.get("units", 10**9):
            return
        raw, hi, lo = self.w_raw[u % RAW], self.w_hi[u % SPL], self.w_lo[u % SPL]
        pick = view or (lambda t: t[:, 0:cols])
        for e in (self.a, self.v):
            e.reach(self.s_raw[u % RAW], 32 * (u // RAW + 1), 32 * step // RAW)
            e.reach(self.s_mm, u + 1, step)
        self.nc.scalar.activation(pick(hi), pick(raw), ACT.Copy).then_inc(self.s_hi, 1)
        self.v.reach(self.s_hi, u + 1, step)
        self.nc.vector.tensor_tensor(pick(lo), pick(raw), pick(hi).bitcast(F32),
                                     ALU.subtract).then_inc(self.s_lo, 1)

    def multiply_unit(self, products, k=0, step=0, mark=None):
        u = self.U + k
        self.p.reach(self.s_lo, u + 1 + RAW, step)
        for out, lhsT, rhs, start, stop in products(self.w_hi[u % SPL], self.w_lo[u % SPL]):
            last = self.nc.tensor.matmul(out, lhsT, rhs, start=start, stop=stop)
            if mark is not None and stop and len(mark) < KD - 1:
                self.p.did(last, f"sum{len(mark)}")
                mark.append(last)
        last.then_inc(self.s_mm, 1)

    def group_done(self, eng, k, step=0):
        eng.reach(self.s_mm, self.U + k + 1 + SPL, step)

    def mod_unit(self, layer, part, kt, acc, k, step=0):
        m = self.M + k
        raw = self.m_raw[m % 2]
        if m >= 2:
            self.g.reach(self.s_mac, m - 1, step)
        cols = bass.ds(part * D, D) if not isinstance(part, int) else slice(part * D, (part + 1) * D)
        self.nc.gpsimd.dma_start(raw[:, :], self.io["ada_w"][layer, kt * P:(kt + 1) * P, cols]) \
            .then_inc(self.s_m[m % 2], 16)
        self.v.reach(self.s_m[m % 2], 16 * (m // 2 + 1), 8 * step)
        if m >= 1:
            self.v.reach(self.s_mac, m, step)
        if kt == 0:
            ins = self.nc.vector.tensor_scalar(acc, raw[:, :], self.cvec[:, kt:kt + 1], None, ALU.mult)
        else:
            ins = self.nc.vector.scalar_tensor_tensor(acc, raw[:, :], self.cvec[:, kt:kt + 1], acc,
                                                      ALU.mult, ALU.add)
        ins.then_inc(self.s_mac, 1)

    def mod_finish(self, layer, part, slot, bank):
        self.p.reach(self.s_mac, self.M)
        self.p.wait(f"bank{bank}")
        for n in range(KD):
            ins = self.nc.tensor.matmul(self.ps[:, bank, n:n + 1], self.m_acc[:, slot, n * P:(n + 1) * P],
                                        self.c("ones")[:, 0:1], start=True, stop=True)
        self.p.did(ins, "mod_sum")
        self.v.wait("mod_sum")
        self.v.did(self.nc.vector.tensor_tensor(self.mod[:, layer, part, :], self.ps[:, bank, 0:KD],
                                                self.mod_b[:, layer, part, :], ALU.add), f"bank{bank}")
        self.pr.events[f"mod{layer}{part}"] = self.pr.events[f"bank{bank}"]

    def group_load(self, k, step, pieces):
        for u in range(4):
            def halves(raw, u=u):
                two = raw[:, :].rearrange("p (kk c) -> p kk c", kk=2)
                for (kk, cols), src in pieces(u):
                    yield two[:, kk, cols], src
            self.load_unit(halves, k + u, step)

    @staticmethod
    def k_tiles(w, u, cols):
        for kk in range(2):
            kt = 2 * u + kk
            width = cols.stop - cols.start if isinstance(cols, slice) else 512
            yield (kk, slice(0, width)), w[kt * P:(kt + 1) * P, cols]

    def feature_products(self, u, banks):
        def products(hi, lo):
            for kk in range(2):
                kt = 2 * u + kk
                for n, b in enumerate(banks):
                    c = kk * 512 + n * P
                    out = self.ps[:, b, :]
                    yield out, hi[:, c:c + P], self.h_hi[:, kt, :], kt == 0, False
                    yield out, hi[:, c:c + P], self.h_lo[:, kt, :], False, False
                    yield out, lo[:, c:c + P], self.h_hi[:, kt, :], False, kt == KD - 1
        return products

    def token_products(self, u, banks, width=512):
        def products(hi, lo):
            for kk in range(2):
                kt = 2 * u + kk
                for t, b in enumerate(banks):
                    out = self.ps[:, b, 0:width]
                    w = slice(kk * 512, kk * 512 + width)
                    tok = slice(t * P, (t + 1) * P)
                    yield out, self.h_hi[:, kt, tok], hi[:, w], kt == 0, False
                    yield out, self.h_lo[:, kt, tok], hi[:, w], False, False
                    yield out, self.h_hi[:, kt, tok], lo[:, w], False, kt == KD - 1
        return products

    def group(self, k, step, banks, pieces, kind="feature", width=512, next_width=None, extra=None):
        self.group_load(k, step, pieces)
        for u in range(4):
            self.p.wait(*([f"h{2 * u}", f"h{2 * u + 1}"]))
            if u == 0:
                self.p.wait(*[f"bank{b}" for b in banks])
            if kind == "feature":
                self.multiply_unit(self.feature_products(u, banks), k + u, step)
            else:
                self.multiply_unit(self.token_products(u, banks, width), k + u, step)
            w = width if u < 2 else (next_width or 512)
            view = None if w == 512 else (lambda t, w=w: t[:, :].rearrange("p (a b) -> p a b", a=2)[:, :, 0:w])
            self.split_unit(k=k + u + 2, step=step, view=view)
            if extra:
                extra(u)

    def square_sum(self, kt, bank=7):
        self.a.wait(f"x{kt}", f"sq_used{kt % 2}")
        sq = self.sq[kt % 2]
        self.a.did(self.nc.scalar.activation(sq[:, :], self.xT[:, kt, :], ACT.Square), f"sq{kt % 2}")
        self.p.wait(f"sq{kt % 2}")
        if kt == 0:
            self.p.wait(f"bank{bank}")
        ins = self.nc.tensor.matmul(self.ps[:, bank, :], self.c("ones"), sq[:, :],
                                    start=kt == 0, stop=kt == KD - 1)
        self.p.did(ins, f"sq_used{kt % 2}")

    def warm_ln(self):
        self.a.did(self.nc.scalar.activation(self.small[:, 2:3], self.eps, ACT.Ln))

    def norm(self, scale, bias, need, bank=7, into_x=False):
        nc = self.nc
        for kt in range(KD):
            self.square_sum(kt, bank)
        self.a.wait(f"sq_used{(KD - 1) % 2}")
        self.a.did(nc.scalar.activation(self.rstd[:, :], self.ps[:, bank, :], ACT.Ln, bias=self.eps,
                                        scale=1.0 / D), f"bank{bank}")
        self.a.wait(f"bank{bank}")
        self.a.did(nc.scalar.activation(self.rstd[:, :], self.rstd[:, :], ACT.Exp, scale=-0.5), "rstd")
        self.a.wait(*need)
        self.v.wait("rstd", *need)
        for kt in range(KD):
            t = self.nt[kt % 4]
            if into_x:
                self.v.did(nc.vector.scalar_tensor_tensor(self.xT[:, kt, :], self.xT[:, kt, :], scale(kt),
                                                          self.rstd[:, :], ALU.mult, ALU.mult), f"x{kt}")
                continue
            self.v.did(nc.vector.scalar_tensor_tensor(t[:, :], self.xT[:, kt, :], scale(kt),
                                                      self.rstd[:, :], ALU.mult, ALU.mult), f"nt{kt % 4}")
            self.a.wait(f"nt{kt % 4}")
            hi = self.h_hi[:, kt, :]
            self.a.did(nc.scalar.activation(hi, t[:, :], ACT.Identity, bias=bias(kt)) if bias else
                       nc.scalar.activation(hi, t[:, :], ACT.Copy), f"hh{kt % 2}")
            if kt:
                self.low_part(kt - 1, bias)
        if not into_x:
            self.low_part(KD - 1, bias)

    def low_part(self, kt, bias):
        nc, t, hi, lo = self.nc, self.nt[kt % 4], self.h_hi[:, kt, :].bitcast(F32), self.h_lo[:, kt, :]
        self.v.wait(f"hh{kt % 2}")
        self.v.did(nc.vector.scalar_tensor_tensor(lo, t[:, :], bias(kt), hi, ALU.add, ALU.subtract) if bias else
                   nc.vector.tensor_tensor(lo, t[:, :], hi, ALU.subtract), f"h{kt}")

    def norm_scratch(self, base):
        n = next(self.names)
        self.sq = [self.sb(f"sq{n}_{i}", [P, S], at=base + i * 2048) for i in range(2)]
        self.nt = [self.sb(f"nt{n}_{i}", [P, S], at=base + (2 + i) * 2048) for i in range(4)]
        self.rstd = self.sb(f"rstd{n}", [P, S], at=base + 6 * 2048)

    def start(self):
        nc, io = self.nc, self.io
        nc.vector.sem_inc(self.s_lo, RAW)
        nc.tensor.sem_inc(self.s_mm, SPL)
        nc.vector.sem_inc(self.v.sem, 8); self.v.n = 8
        nc.scalar.sem_inc(self.a.sem, 8); self.a.n = 8
        nc.gpsimd.sem_inc(self.g.sem, 8); self.g.n = 8
        nc.tensor.sem_inc(self.p.sem, 8); self.p.n = 8
        xin = self.sb("xin", [P, TT, D], at=self.arena)
        self.load_const(self.const[:, :], io["const"])
        self.load_const(xin[:, :, :], io["x"].rearrange("b (t p) d -> p (b t) d", p=P))
        rows = self.sb("vec_rows", [P, 4, P], at=self.arena + 16384)
        at = {}

        def vec(tile, name, src, n):
            lo = sum(k for (t, k) in at.values() if t == tile)
            at[name] = (tile, n)
            self.load_const(rows[lo:lo + n, tile, :], src)
            return self.vecs[:, tile, lo:lo + n]
        self.mod_b = vec(0, "ada_b", io["ada_b"].rearrange("l (r p) -> (l r) p", p=P), 96) \
            .rearrange("p (l a k) -> p l a k", l=2, a=6)
        self.c_in = vec(0, "c", io["c"].rearrange("b (k p) -> (b k) p", p=P), KD)
        self.lbp = vec(0, "hg_lb", io["hg_lb"].rearrange("a (k p) -> (a k) p", p=P), 16) \
            .rearrange("p (a k) -> p a k", a=2)
        self.gn = vec(0, "hg_gnorm", io["hg_gnorm"], 1)
        self.norms = {}
        for name in ("norm_mix", "norm_ffn", "final_norm", "ffn1_norm_2", "mix_norm_2", "ffn2_norm_2"):
            src = io[name]
            src = src.rearrange("(k p) -> k p", p=P) if name == "final_norm" else \
                src.rearrange("l (k p) -> (l k) p", p=P)
            self.norms[name] = vec(1, name, src, src.shape[0])
        self.pool_scale = vec(1, "pool_scale", io["pool_scale_2"].rearrange("l (k p) -> (l k) p", p=P), 4)
        self.conv = []
        for layer in range(2):
            w = vec(2 + layer, f"conv_w{layer}", io["ffn_conv_w"][layer].rearrange("w (k p) -> (w k) p", p=P), 3 * KF)
            bias = vec(2 + layer, f"conv_b{layer}", io["ffn_conv_b"][layer].rearrange("(k p) -> k p", p=P), KF)
            self.conv.append((w.rearrange("p (w k) -> p w k", w=3), bias))
        n_rows = [sum(k for (t, k) in at.values() if t == tile) for tile in range(4)]
        small = self.small
        self.eps, self.lb, self.oml = small[:, 0:1], small[:, 8:16], small[:, 16:24]
        for e in (self.v, self.a, self.p, self.g):
            e.reach(self.s_const, self.n_const)
        self.v.did(nc.vector.memset(self.eps, EPS), "eps")
        self.a.wait("eps")
        for tile, n in enumerate(n_rows):
            ins = nc.tensor.transpose(self.ps[:, 4 + tile, 0:n], rows[0:n, tile, :], self.c("ident")[0:n, 0:n])
            self.p.did(ins, "vec_t")
            self.v.wait("vec_t")
            self.v.did(nc.vector.tensor_copy(self.vecs[:, tile, 0:n], self.ps[:, 4 + tile, 0:n]), f"bank{4 + tile}")
        self.a.wait("bank7")
        self.a.did(nc.scalar.activation(self.cvec[:, :], self.c_in, ACT.Silu), "c_act")
        self.v.wait("c_act")
        for kt in range(KD):
            b = kt % 4
            if kt >= 4:
                self.p.wait(f"bank{b}")
            for t in range(TT):
                ins = nc.tensor.transpose(self.ps[:, b, t * P:(t + 1) * P], xin[:, t, kt * P:(kt + 1) * P],
                                          self.c("ident"))
            self.p.did(ins, "xt")
            self.a.wait("xt")
            self.a.did(nc.scalar.activation(self.xT[:, kt, :], self.ps[:, b, :], ACT.Copy), f"bank{b}")
            self.pr.events[f"x{kt}"] = self.pr.events[f"bank{b}"]
        for part in range(2):
            self.v.wait("mod_sum") if part else None
            for kt in range(KD):
                self.mod_unit(0, part, kt, self.m_acc[:, part, :], kt)
            self.M += KD
            self.mod_finish(0, part, part, 4 + part)
        self.split_unit_later = 2

    def lower_bounds(self):
        nc, v, a = self.nc, self.v, self.a
        sc = self.small
        mx, e0, e1 = sc[:, 40:48], sc[:, 48:56], sc[:, 56:64]
        l0, l1 = self.lbp[:, 0, :], self.lbp[:, 1, :]
        v.did(nc.vector.tensor_tensor(mx, l0, l1, ALU.max), "lb_t"); v.wait("lb_t")
        v.did(nc.vector.tensor_tensor(e0, l0, mx, ALU.subtract), "lb_t")
        v.did(nc.vector.tensor_tensor(e1, l1, mx, ALU.subtract), "lb_t")
        a.wait("lb_t")
        a.did(nc.scalar.activation(sc[:, 48:64], sc[:, 48:64], ACT.Exp), "lb_e")
        v.wait("lb_e")
        v.did(nc.vector.tensor_tensor(mx, e0, e1, ALU.add), "lb_t"); v.wait("lb_t")
        v.did(nc.vector.reciprocal(mx, mx), "lb_t"); v.wait("lb_t")
        v.did(nc.vector.tensor_tensor(self.lb, e0, mx, ALU.mult), "lb_t")
        v.did(nc.vector.tensor_tensor(self.oml, e1, mx, ALU.mult), "lb")

    def modulation_scales(self, layer):
        nc, v = self.nc, self.v
        for part, gain in ((1, "norm_mix"), (4, "norm_ffn")):
            if f"mod{layer}{part}" not in self.pr.events or f"ms{layer}{part}" in self.pr.events:
                continue
            dst = self.mod[:, layer, part, :]
            v.wait(f"mod{layer}{part}")
            v.did(nc.vector.scalar_tensor_tensor(dst, dst, 1.0, self.norms[gain][:, layer * KD:(layer + 1) * KD],
                                                         ALU.add, ALU.mult),
                  f"ms{layer}{part}")

    def prologue(self):
        for k in range(2):
            self.split_unit(k=k)

    def hgrn_in(self):
        nc, w = self.nc, self.io["hg_w_in"]
        self.proj = self.sb("proj", [P, 4 * KD, S], at=self.arena)

        def body(i):
            for gi in range(2):
                banks = range(4 * gi, 4 * gi + 4)
                cols = bass.ds(i * 1024 + gi * 512, 512)
                self.group(4 * gi, 8, banks,
                           lambda u: self.k_tiles(w[0], u, cols),
                           extra=lambda u, gi=gi: self.mod_unit(0, bass_part(i + 2), 4 * gi + u,
                                                                self.m_acc[:, bass.ds(i, 1), :], 4 * gi + u, 8))
                for e, n in ((self.a, 0), (self.v, 1), (self.a, 2), (self.v, 3)):
                    if n < 2:
                        self.group_done(e, 4 * gi + 3, 8)
                    dst = self.proj[:, bass.ds(i * 8 + gi * 4 + n, 1), :]
                    src = self.ps[:, banks[n]:banks[n] + 1, :]
                    if e is self.a:
                        e.did(nc.scalar.activation(dst, src, ACT.Copy), f"bank{banks[n]}")
                    else:
                        e.did(nc.vector.tensor_copy(dst, src), f"bank{banks[n]}")
        self.pr.run_loop("hgrn_in", 4, body)
        self.U += 32
        self.M += 32

    def hgrn_mix(self):
        nc, v, a, g, p = self.nc, self.v, self.a, self.g, self.p
        pr = self.proj
        def place(base, end):
            at = [base]

            def tmp(name, shape, dt=F32):
                t = self.sb(name, shape, dt, at=at[0])
                at[0] += (int(np.prod(shape[1:])) * 4 + 31) // 32 * 32
                assert at[0] <= end
                return t
            return tmp
        tmp = place(self.h_at, self.h_at + 32768)
        kk = self.sb("hg_k", [P, KD, S], at=self.arena + 65536)
        diff = [tmp(f"hg_d{j}", [P, S]) for j in range(3)]
        G = [tmp(f"hg_g{j}", [P, S]) for j in range(3)]
        scT, qe, kdT, vT = ([tmp(f"hg_{n}{j}", [P, S]) for j in range(2)] for n in ("scT", "qe", "kdT", "vT"))
        kd, vs = tmp("hg_kd", [P, S]), tmp("hg_vs", [P, S])
        tmp = place(self.arena + 88064, self.arena + 94208)
        state = [tmp(f"hg_state{j}", [P, 3, P]) for j in range(2)]
        ebl = [tmp(f"hg_ebl{j}", [P, TT]) for j in range(2)]
        kdiff = tmp("hg_kdiff", [P, S])
        a.wait("bank7"); v.wait("bank6")
        a.wait("lb")

        def gates(i):
            f, k, gt = pr[:, bass.ds(i + 8, 1), :], kk[:, bass.ds(i, 1), :], pr[:, bass.ds(i + 24, 1), :]
            a.did(nc.scalar.activation(k, f, ACT.Sigmoid, scale=-1.0), "k0")
            a.wait("k0")
            a.did(nc.scalar.activation(f, f, ACT.Sigmoid), "sf")
            v.wait("k0")
            v.did(nc.vector.tensor_scalar(k, k, self.oml[:, bass.ds(i, 1)], None, ALU.mult), "k1")
        v.wait("bank7")
        a.wait("bank1", "bank3", "bank5")
        self.pr.run_loop("hg_gates", KD, gates)

        def silu(i):
            gt = pr[:, bass.ds(i + 24, 1), :]
            a.did(nc.scalar.activation(gt, gt, ACT.Silu), "sg")
        self.pr.run_loop("hg_silu", KD, silu)

        def logs(i):
            f = pr[:, bass.ds(i + 8, 1), :]
            if True:
                a.did(nc.scalar.activation(f, f, ACT.Ln, bias=self.lb[:, bass.ds(i, 1)],
                                           scale=self.oml[:, bass.ds(i, 1)]), "logf")
            v.wait("logf")
            v.did(nc.vector.tensor_tensor_scan(pr[:, bass.ds(i + 8, 1), :].rearrange("p a t -> p (a t)"),
                                               self.c2["restart"], f.rearrange("p a t -> p (a t)"), 0.0,
                                               ALU.mult, ALU.add), "b")
        a.wait("sf")
        v.reach(self.s_c2, self.n_c2)
        self.pr.run_loop("hg_logs", KD, logs)
        g.wait("b", "k1")
        for j in range(2):
            v.did(nc.vector.memset(scT[j][:, :], 0.0), "scT0")

        def flat(ap):
            return ap.rearrange("p a t -> p (a t)")

        def chunks(ap):
            return ap.rearrange("p (c t) -> p c t", c=TT)

        def body(i):
            heads = []
            for hh in range(2):
                h = 2 * i + hh
                heads.append(dict(j=hh, q=flat(pr[:, bass.ds(h, 1), :]), b=flat(pr[:, bass.ds(h + 8, 1), :]),
                                  v=flat(pr[:, bass.ds(h + 16, 1), :]), k=flat(kk[:, bass.ds(h, 1), :])))

            def decays(H):
                j, last = H["j"], chunks(H["b"])[:, :, P - 1:P]
                v.wait("kd_scaled")
                v.did(nc.vector.tensor_tensor(chunks(kdiff[:, :]), last.to_broadcast([P, TT, P]), chunks(H["b"]),
                                              ALU.subtract), "kd_diff")
                a.wait("v_turned")
                a.did(nc.scalar.activation(vs[:, :], H["v"], ACT.Copy), "vs")
                a.wait("kd_diff", "kd_turned")
                a.did(nc.scalar.activation(kd[:, :], kdiff[:, :], ACT.Exp), "kd_exp")
                self.pr.events["kd_scaled"] = self.pr.events["kd_exp"]
                a.wait(f"state_done{j}")
                a.did(nc.scalar.activation(ebl[j][:, :], last.rearrange("p c t -> p (c t)"), ACT.Exp), f"ebl{j}")
                a.wait(f"o{j}")
                a.did(nc.scalar.activation(qe[j][:, :], H["b"], ACT.Exp), f"qe_exp{j}")

            def scale(H):
                g.wait("kd_exp")
                g.did(nc.gpsimd.tensor_tensor(kd[:, :], kd[:, :], H["k"], ALU.mult), "kd")

            def scale_q(H):
                j = H["j"]
                g.wait(f"qe_exp{j}")
                g.did(nc.gpsimd.tensor_tensor(qe[j][:, :], qe[j][:, :], H["q"], ALU.mult), f"qe{j}")

            def turn(H):
                j = H["j"]
                for src, ready, bank, dst, done in ((vs, "vs", 3, vT, "v_turned"), (kd, "kd", 4, kdT, "kd_turned")):
                    p.wait(ready, f"bank{bank}")
                    for c in range(TT):
                        w = slice(c * P, (c + 1) * P)
                        ins = nc.tensor.transpose(self.ps[:, bank, w], src[:, w], self.c("ident"))
                    p.did(ins, done)
                    a.wait(done, f"o{j}", f"st{j}")
                    a.did(nc.scalar.activation(dst[j][:, :], self.ps[:, bank, :], ACT.Copy), f"bank{bank}")

            def carry(H, c):
                j = H["j"]
                w = slice(c * P, (c + 1) * P)
                p.wait("bank3", "bank4", "bank5")
                p.did(nc.tensor.matmul(self.ps[:, 5, 0:P], kdT[j][:, w], vT[j][:, w], start=True, stop=True), f"st{j}")
                v.wait(f"st{j}", f"o{j}", f"ebl{j}")
                if c == 0:
                    ins = nc.vector.tensor_copy(state[j][:, 0, :], self.ps[:, 5, 0:P])
                else:
                    v.wait(f"state_done{j}")
                    ins = nc.vector.scalar_tensor_tensor(state[j][:, c, :], state[j][:, c - 1, :], ebl[j][:, c:c + 1],
                                                         self.ps[:, 5, 0:P], ALU.mult, ALU.add)
                v.did(ins, f"state_done{j}")
                self.pr.events["bank5"] = self.pr.events[f"state_done{j}"]

            def output(H):
                j = H["j"]
                p.wait(f"scT{j}", f"state_done{j}", f"qe{j}", f"bank{6 + j}")
                for c in range(TT):
                    w = slice(c * P, (c + 1) * P)
                    ins = nc.tensor.matmul(self.ps[:, 6 + j, w], vT[j][:, w], scT[j][:, w], start=True, stop=c == 0)
                    if c:
                        ins = nc.tensor.matmul(self.ps[:, 6 + j, w], state[j][:, c - 1, :], qe[j][:, w],
                                               start=False, stop=True)
                p.did(ins, f"o{j}")
                a.wait(f"o{j}")
                a.did(nc.scalar.activation(H["q"], self.ps[:, 6 + j, :], ACT.Copy), f"bank{6 + j}")

            def level(n, H, m):
                r = n % 3
                if m < 7:
                    hs = 1 << m

                    def halves(ap):
                        return ap.rearrange("p (n a t) -> p n a t", a=2, t=hs)
                    bb, dd, gg = halves(H["b"]), halves(diff[r][:, :]), halves(G[r][:, :])
                    ref = bb[:, :, 0, hs - 1:hs].to_broadcast([P, S // (2 * hs), hs])
                    v.wait(f"G{r}")
                    v.did(nc.vector.tensor_tensor(dd[:, :, 1, :], bb[:, :, 1, :], ref, ALU.subtract))
                    v.did(nc.vector.tensor_tensor(dd[:, :, 0, :], ref, bb[:, :, 0, :], ALU.subtract), f"d{r}")
                    a.wait(f"d{r}")
                    a.did(nc.scalar.activation(diff[r][:, :], diff[r][:, :], ACT.Exp), f"e{r}")
                    g.wait(f"e{r}", f"S{r}")
                    g.did(nc.gpsimd.tensor_tensor(gg[:, :, 1, :], halves(H["q"])[:, :, 1, :], dd[:, :, 1, :], ALU.mult))
                    g.did(nc.gpsimd.tensor_tensor(gg[:, :, 0, :], halves(H["k"])[:, :, 0, :], dd[:, :, 0, :], ALU.mult),
                          f"G{r}")
                else:
                    v.wait(f"S{r}", f"G{r}")
                    v.did(nc.vector.tensor_tensor(G[r][:, :], H["q"], H["k"], ALU.mult), f"G{r}")
                p.wait(f"G{r}", f"bank{r}")
                for c in range(TT):
                    gc = G[r][:, c * P:(c + 1) * P]
                    ins = nc.tensor.matmul(self.ps[:, r, c * P:(c + 1) * P], gc,
                                           gc if m < 7 else self.c("ones"), start=True, stop=True)
                p.did(ins, f"S{r}")

            def place_scores(n, H, m):
                r, j = n % 3, H["j"]
                mask = self.c2[f"level{m}"].bitcast(I32).unsqueeze(1).broadcast_to([P, TT, P])
                v.wait(f"S{r}", f"o{j}", f"scT{j}")
                v.settle(True)
                v.did(nc.vector.copy_predicated(chunks(scT[j][:, :]), mask, chunks(self.ps[:, r, :])), f"scT{j}")
                self.pr.events[f"bank{r}"] = self.pr.events[f"scT{j}"]

            for n in range(16 + 3):
                if n < 16:
                    H, m = heads[n // 8], n % 8
                    if m == 0:
                        decays(H)
                    level(n, H, m)
                    if m == 1:
                        scale(H)
                    elif m == 2:
                        scale_q(H)
                    elif m == 3:
                        turn(H)
                    elif m >= 5:
                        carry(H, m - 5)
                if 0 <= n - 2 < 16:
                    place_scores(n - 2, heads[(n - 2) // 8], (n - 2) % 8)
                if n in (10, 18):
                    output(heads[n // 9 - 1])
        self.forget("S0", "S1", "S2", "G0", "G1", "G2", "o0", "o1", "st0", "st1", "scT0", "scT1", "kd_scaled", "v_turned",
                    "kd_turned", "state_done0", "state_done1")
        v.did(nc.vector.memset(self.small[:, 3:4], 0.0), "ready")
        for e in (a, v, p, g):
            e.wait("ready", *[f"bank{n}" for n in range(8)])
        g.wait("sg")
        a.wait("b")
        self.pr.run_loop("hg_heads", KD // 2, body)
        self.warm_ln()
        sq, rst = diff[0:2], [self.proj[:, 8 + kt, :] for kt in range(KD)]
        a.wait("scT0", "scT1", "G0", "G1", "G2", "bank5", "S0", "S1", "S2")
        for kt in range(KD):
            a.wait(f"hn_used{kt % 2}", "bank6", "bank7")
            a.did(nc.scalar.activation(sq[kt % 2][:, :], self.proj[:, kt, :], ACT.Square), f"hn_sq{kt % 2}")
            p.wait(f"hn_sq{kt % 2}", f"bank{kt}")
            p.did(nc.tensor.matmul(self.ps[:, kt, :], self.c("ones"), sq[kt % 2][:, :], start=True, stop=True),
                  f"hn_used{kt % 2}")
            if kt:
                a.wait(f"hn_used{(kt - 1) % 2}")
                a.did(nc.scalar.activation(rst[kt - 1], self.ps[:, kt - 1, :], ACT.Ln, bias=self.eps, scale=1.0 / P),
                      f"bank{kt - 1}")
        a.wait(f"hn_used{(KD - 1) % 2}")
        a.did(nc.scalar.activation(rst[KD - 1], self.ps[:, KD - 1, :], ACT.Ln, bias=self.eps, scale=1.0 / P), "bank7")
        a.wait("bank7")
        for kt in range(KD):
            a.did(nc.scalar.activation(rst[kt], rst[kt], ACT.Exp, scale=-0.5), f"hn_rst{kt}")
        v.wait("bank6", "scT0", "scT1")
        for kt in range(KD + 1):
            if kt < KD:
                o, gt = self.proj[:, kt, :], self.proj[:, 24 + kt, :]
                v.wait(f"hn_rst{kt}")
                v.did(nc.vector.scalar_tensor_tensor(o, o, self.gn, rst[kt], ALU.mult, ALU.mult), "hn_o")
                e, ee = (g, nc.gpsimd) if kt % 2 else (v, nc.vector)
                e.wait("hn_o")
                e.did(ee.tensor_tensor(o, o, gt, ALU.mult), f"hn_g{kt}")
                a.wait(f"hn_g{kt}")
                a.did(nc.scalar.activation(self.h_hi[:, kt, :], o, ACT.Copy), f"hh{kt % 2}")
            if kt:
                o = self.proj[:, kt - 1, :]
                v.wait(f"hh{(kt - 1) % 2}")
                v.did(nc.vector.tensor_tensor(self.h_lo[:, kt - 1, :], o, self.h_hi[:, kt - 1, :].bitcast(F32),
                                              ALU.subtract), f"h{kt - 1}")

    def split_h(self, src, need):
        nc = self.nc
        self.a.wait(*need)
        self.v.wait(*need)
        for kt in range(KD):
            self.a.did(nc.scalar.activation(self.h_hi[:, kt, :], src(kt), ACT.Copy), f"hh{kt % 2}")
            self.v.wait(f"hh{kt % 2}")
            self.v.did(nc.vector.tensor_tensor(self.h_lo[:, kt, :], src(kt), self.h_hi[:, kt, :].bitcast(F32),
                                               ALU.subtract), f"h{kt}")

    def out_proj(self, w, gain, need, extra=None):
        nc = self.nc
        for gi in range(2):
            banks = range(4 * gi, 4 * gi + 4)
            self.group(0, 0, banks, lambda u: self.k_tiles(w, u, slice(gi * 512, (gi + 1) * 512)),
                       extra=(lambda u, gi=gi: extra(4 * gi + u)) if extra else None)
            self.group_done(self.v, 3)
            self.v.wait(*need)
            for n in range(4):
                kt = gi * 4 + n
                self.add_to_x(kt, banks[n], gain)
            self.U += 4

    def add_to_x(self, kt, bank, gain):
        x = self.xT[:, kt, :]
        self.v.did(self.nc.vector.scalar_tensor_tensor(x, self.ps[:, bank, :], gain(kt), x, ALU.mult, ALU.add),
                   f"bank{bank}")
        self.pr.events[f"x{kt}"] = self.pr.events[f"bank{bank}"]

    def ffn(self, name, gate_w, up_w, down_w, gain, conv=None, need=(), extra=None, after_up=None):
        nc, v, a, p = self.nc, self.v, self.a, self.p
        hid_hi = self.sb(f"hid_hi_{name}", [P, KF, S], F32R, at=self.arena)
        hid_lo = self.sb(f"hid_lo_{name}", [P, KF, S], F32R, at=self.arena + KF * 2048)
        cb = [self.sb(f"cb{j}_{name}", [P, S], at=self.arena + (2 * KF + j) * 2048) for j in range(2)]

        def up_group(f0, k, step, banks, ex=None):
            def pieces(u):
                cols = bass.ds(f0 * P, 256) if not isinstance(f0, int) else slice(f0 * P, f0 * P + 256)
                for half, w in enumerate((gate_w, up_w)):
                    yield (slice(0, 2), slice(half * 256, half * 256 + 256)), \
                        w[2 * u * P:(2 * u + 2) * P, cols].rearrange("(kk p) c -> p kk c", p=P)
            self.group(k, step, banks, pieces, extra=ex)
            self.group_done(a, k + 3, step)
            self.group_done(v, k + 3, step)
            def col(tb, f):
                return tb[:, bass.ds(f, 1)] if not isinstance(f, int) else tb[:, f:f + 1]

            def tile(tb, f):
                return tb[:, bass.ds(f, 1), :] if not isinstance(f, int) else tb[:, f:f + 1, :]
            gates = [self.ps[:, banks[j], :] for j in range(2)]
            if conv:
                wt, bias = conv
                for j in range(2):
                    v.wait(f"hid{j}")
                    v.did(nc.vector.tensor_scalar(cb[j][:, :], gates[j], col(wt[:, 2, :], f0 + j),
                                                  col(bias, f0 + j), ALU.mult, ALU.add), f"cv{j}")
                for sh in (1, 2):
                    for j in range(2):
                        v.wait(f"cv{j}")
                        v.did(nc.vector.scalar_tensor_tensor(
                            cb[j][:, sh:S], gates[j][:, 0:S - sh], col(wt[:, 2 - sh, :], f0 + j),
                            cb[j][:, sh:S], ALU.mult, ALU.add), f"cv{j}")
                        self.pr.events[f"bank{banks[j]}"] = self.pr.events[f"cv{j}"]
            for j in range(2):
                if conv:
                    a.wait(f"cv{j}")
                    a.did(nc.scalar.activation(cb[j][:, :], cb[j][:, :], ACT.Silu), f"silu{j}")
                else:
                    a.wait(f"hid{j}")
                    a.did(nc.scalar.activation(cb[j][:, :], gates[j], ACT.Silu), f"silu{j}")
                    self.pr.events[f"bank{banks[j]}"] = self.pr.events[f"silu{j}"]
            for j in range(2):
                v.wait(f"silu{j}")
                v.did(nc.vector.tensor_tensor(cb[j][:, :], cb[j][:, :], self.ps[:, banks[2 + j], :], ALU.mult),
                      f"bank{banks[2 + j]}")
                a.wait(f"bank{banks[2 + j]}")
                a.did(nc.scalar.activation(tile(hid_hi, f0 + j), cb[j][:, :].unsqueeze(1), ACT.Copy), f"hid_hi{j}")
            for j in range(2):
                v.wait(f"hid_hi{j}")
                v.did(nc.vector.tensor_tensor(tile(hid_lo, f0 + j), cb[j][:, :].unsqueeze(1),
                                              tile(hid_hi, f0 + j).bitcast(F32), ALU.subtract), f"hid{j}")

        def body(i):
            for gi in range(2):
                up_group(4 * i + 2 * gi, 4 * gi, 8, range(4 * gi, 4 * gi + 4),
                         (lambda u, gi=gi: extra(i, 4 * gi + u)) if extra else None)
        self.forget("hid0", "hid1")
        self.pr.run_loop(name, KF // 4, body)
        self.U += 8 * (KF // 4)
        if extra:
            self.M += 8 * (KF // 4)
        up_group(KF - 2, 0, 0, range(0, 4))
        self.U += 4

        def down_unit(kt, k, step, start, stop):
            rows = bass.ds(kt * P, P) if not isinstance(kt, int) else slice(kt * P, (kt + 1) * P)

            def halves(raw):
                for c in range(2):
                    yield raw[:, c * 512:(c + 1) * 512], down_w[rows, c * 512:(c + 1) * 512]

            def products(hi, lo):
                for n in range(KD):
                    out = self.ps[:, n, :]
                    ht = hid_hi[:, bass.ds(kt, 1), :] if not isinstance(kt, int) else hid_hi[:, kt, :]
                    lt = hid_lo[:, bass.ds(kt, 1), :] if not isinstance(kt, int) else hid_lo[:, kt, :]
                    yield out, hi[:, n * P:(n + 1) * P], ht, start, False
                    yield out, hi[:, n * P:(n + 1) * P], lt, False, False
                    yield out, lo[:, n * P:(n + 1) * P], ht, False, stop
            self.load_unit(halves, k, step)
            self.multiply_unit(products, k, step, mark=[] if stop else None)
            self.split_unit(k=k + 2, step=step)
        if after_up:
            after_up()
        p.wait("hid0", "hid1", *[f"bank{b}" for b in range(8)])
        for kt in range(2):
            down_unit(kt, 0, 0, kt == 0, False)
            self.U += 1

        def down_body(i):
            for j in range(4):
                down_unit(4 * i + 2 + j, j, 4, False, False)
        n = (KF - 2) // 4 - 1
        self.pr.run_loop(name + "_down", n, down_body)
        self.U += 4 * n
        for kt in range(4 * n + 2, KF):
            down_unit(kt, 0, 0, False, kt == KF - 1)
            self.U += 1
        self.warm_ln()
        self.v.wait(*need)
        for n in range(KD):
            if n < KD - 1:
                self.v.wait(f"sum{n}")
            else:
                self.group_done(self.v, -1)
            self.add_to_x(n, n, gain)

    def finish_early(self):
        self.store_x()
        self.pr.learned["units"] = self.U
        return self.pr.learned

    def attention_scratch(self, tag, at):
        self.at_s = [self.sb(f"at_s{j}{tag}", [P, S], at=at + j * 2048) for j in range(4)]
        self.at_t = [self.sb(f"at_t{j}{tag}", [P, S], at=at + (4 + j) * 2048) for j in range(2)]
        return at + 6 * 2048

    def attend(self, blocks, mx):
        nc, v, a, p = self.nc, self.v, self.a, self.p

        def scores(m, B):
            j, jp, w = m % 4, m % 2, B["n"] * P
            sc, mxc = self.at_s[j][:, 0:w], mx[:, j:j + 1]
            p.wait(f"sc_read{jp}", *B["ready"])
            p.settle(True)
            p.did(nc.tensor.matmul(self.ps[:, jp, 0:w], B["q"], B["k"], start=True, stop=True), f"qk{jp}")
            B["after_q"]()
            v.wait(f"qk{jp}", f"pt{j}", *B["bias_ready"])
            v.settle(True)
            v.did(nc.vector.tensor_tensor_reduce(sc, self.ps[:, jp, 0:w], B["bias"], 1.0, -3e38,
                                                 ALU.add, ALU.max, mxc), f"sc_read{jp}")
            v.wait(f"sc_read{jp}")
            v.did(nc.vector.tensor_scalar(mxc, mxc, -1.0, None, ALU.mult), f"mx{j}")
            a.wait(f"mx{j}")
            a.did(nc.scalar.activation(sc, sc, ACT.Exp, bias=mxc, accum_out=B["rs"]), f"exp{j}")

        def turn(m, B):
            j, jp, w = m % 4, m % 2, B["n"] * P
            p.wait(f"exp{j}", f"pt_read{jp}")
            for s in range(B["n"]):
                ins = nc.tensor.transpose(self.ps[:, 2 + jp, s * P:(s + 1) * P], self.at_s[j][:, s * P:(s + 1) * P],
                                          self.c("ident"))
            p.did(ins, f"pt{j}")
            self.pr.events[f"ptb{jp}"] = self.pr.events[f"pt{j}"]
            e = v if m % 3 == 0 else a
            e.wait(f"pt{j}", f"pv{jp}")
            dst, src = self.at_t[jp][:, 0:w], self.ps[:, 2 + jp, 0:w]
            e.did(nc.vector.tensor_copy(dst, src) if e is v else nc.scalar.activation(dst, src, ACT.Copy),
                  f"pt_read{jp}")

        def values(m, B):
            jp = m % 2
            p.wait(f"pt_read{jp}", *B["out_ready"])
            for s in range(B["n"]):
                ins = nc.tensor.matmul(B["out"], self.at_t[jp][:, s * P:(s + 1) * P], B["v"](s),
                                       start=s == 0, stop=s == B["n"] - 1)
            p.did(ins, f"pv{jp}")
            self.pr.events["pv"] = self.pr.events[f"pv{jp}"]
            B["done"]()
        for m in range(len(blocks) + 3):
            if m < len(blocks):
                blocks[m]["before"]()
                scores(m, blocks[m])
            if 0 <= m - 2 < len(blocks):
                turn(m - 2, blocks[m - 2])
            if m >= 3:
                values(m - 3, blocks[m - 3])

    ATTEND_EVENTS = [n + str(j) for n in ("pt", "ptb", "pt_read", "sc_read", "pv", "exp", "qk", "mx") for j in range(4)]

    def forget(self, *names):
        for n in names:
            self.pr.events.pop(n, None)

    def nsa_weights(self):
        nc, io = self.nc, self.io
        self.w1 = self.sb("nsa_w1", [64, 2, 32, 64], at=self.arena + 74752)
        self.w2 = self.small[0:64, 64:192].rearrange("p (a b) -> p a b", a=2)
        self.pe_rows = self.small[0:64, 192:256]
        for kv in range(2):
            nc.scalar.dma_start(self.w1[:, kv, :, :], io["nsa_cmp_w1"][0, kv].rearrange("(l d) h -> d l h", d=64)) \
                .then_inc(self.s_c2, 16)
            nc.scalar.dma_start(self.w2[:, kv, :], io["nsa_cmp_w2"][0, kv]).then_inc(self.s_c2, 16)
        nc.scalar.dma_start(self.pe_rows, io["nsa_cmp_pe"][0].rearrange("a l d -> (a l) d")).then_inc(self.s_c2, 16)
        self.n_c2 += 5 * 16

    def nsa_in(self):
        nc, v, a, w = self.nc, self.v, self.a, self.io["nsa_w_in"][0]
        ar = self.arena
        self.nq = self.sb("nsa_q", [64, 16, S], at=ar)
        self.nk = self.sb("nsa_k", [64, 8, S], at=ar + 32768)
        self.nc_kv = self.sb("nsa_ckv", [64, 8, S], at=ar + 49152)
        self.nv = self.sb("nsa_v", [P, TT, S], at=ar + 65536)
        self.gate = self.sb("nsa_gate", [P, TT, 48], at=ar + 73728)

        def cols(a0, n=512):
            return slice(a0, a0 + n)

        def strided(off):
            def pieces(u):
                for kk in range(2):
                    kt = 2 * u + kk
                    src = w[kt * P:(kt + 1) * P, 1536:2560].rearrange("p (b c) -> p b c", b=2)[:, :, off:off + 256]
                    yield (kk, slice(0, 512)), src
            return pieces

        groups = [("feature", lambda u: self.k_tiles(w, u, cols(0)), [(self.nq, n) for n in range(4)]),
                  ("feature", lambda u: self.k_tiles(w, u, cols(512)), [(self.nq, n) for n in range(4, 8)]),
                  ("feature", lambda u: self.k_tiles(w, u, cols(1024)), [(self.nc_kv, n) for n in range(4)]),
                  ("feature", strided(0), [(self.nk, n) for n in range(4)]),
                  ("token", strided(256), None),
                  ("token", lambda u: self.k_tiles(w, u, cols(2560, 48)), None)]
        for gi, (kind, pieces, dsts) in enumerate(groups):
            banks = range(4 * (gi % 2), 4 * (gi % 2) + 4)
            self.group(0, 0, banks, pieces, kind=kind, width=48 if gi == 5 else 512)
            self.group_done(a, 3)
            self.group_done(v, 3)
            for n, b in enumerate(banks):
                if kind == "feature":
                    dst, tile = dsts[n]
                    s = 0.125 if dst is self.nq else 1.0
                    a.did(nc.scalar.activation(dst[:, 2 * tile, :], self.ps[0:64, b, :], ACT.Copy, scale=s), f"half{b}")
                    v.wait(f"half{b}")
                    v.did(nc.vector.tensor_scalar(dst[:, 2 * tile + 1, :], self.ps[64:128, b, :], s, None,
                                                  ALU.mult), f"bank{b}")
                elif gi == 4:
                    v.did(nc.vector.tensor_copy(self.nv[:, n, :], self.ps[:, b, :]), f"bank{b}")
                else:
                    a.did(nc.scalar.activation(self.gate[:, n, :], self.ps[:, b, 0:48], ACT.Sigmoid), f"bank{b}")
            self.U += 4

    def nsa_compress(self):
        nc, v, a, p, g = self.nc, self.v, self.a, self.p, self.g
        hs = self.tmp("c_hs", [64, 2, 4, 31])
        self.kc = self.tmp("c_kc", [64, 4, 32])
        self.vbd = self.tmp("c_vbd", [P, 4, 4, 64])
        peT, bias = self.tmp("c_peT", [64, 64]), self.tmp("c_bias", [64, 2])
        v.did(nc.vector.memset(self.kc[:, :, :], 0.0), "kc0")
        v.did(nc.vector.memset(self.vbd[:, :, :, :], 0.0), "vbd0")
        for e in (p, v, a):
            e.reach(self.s_c2, self.n_c2)
        p.wait("bank0")
        p.did(nc.tensor.transpose(self.ps[0:64, 0, 0:64], self.pe_rows[:, :], self.c("ident")[0:64, 0:64]), "peT")
        v.wait("peT")
        v.did(nc.vector.tensor_copy(peT[:, :], self.ps[0:64, 0, 0:64]), "bank0")
        for kv in range(2):
            p.wait(f"bank{1 + kv}", "bank0", f"bank{3 + kv}")
            for l in range(32):
                nc.tensor.matmul(self.ps[0:64, 1 + kv, 0:124], self.w1[:, kv, l, :],
                                 self.nc_kv[:, 4 * kv:4 * kv + 4, l:l + 16 * 30 + 1:16],
                                 start=l == 0, stop=l == 31)
            for l in range(32):
                ins = nc.tensor.matmul(self.ps[0:64, 3 + kv, 0:1], self.w1[:, kv, l, :],
                                       peT[:, kv * 32 + l:kv * 32 + l + 1], start=l == 0, stop=l == 31)
            p.did(ins, f"hid_c{kv}")
            v.wait(f"hid_c{kv}")
            v.did(nc.vector.tensor_copy(bias[:, kv:kv + 1], self.ps[0:64, 3 + kv, 0:1]), f"bank{3 + kv}")
            a.wait(f"bank{3 + kv}")
            a.did(nc.scalar.activation(hs[:, kv, :, :], self.ps[0:64, 1 + kv, 0:124].rearrange("p (a b) -> p a b", a=4),
                                       ACT.Silu, bias=bias[:, kv:kv + 1]), f"bank{1 + kv}")
        p.wait("bank1", "bank2", "bank5", "bank6")
        ins = nc.tensor.matmul(self.ps[0:64, 5, 0:124], self.w2[:, 0, :], hs[:, 0, :, :], start=True, stop=True)
        p.did(ins, "kc_p")
        v.wait("kc_p", "kc0")
        v.did(nc.vector.tensor_copy(self.kc[:, :, 0:31], self.ps[0:64, 5, 0:124].rearrange("p (a b) -> p a b", a=4)), "bank5")
        for j in range(4):
            for gr in range(4):
                ins = nc.tensor.matmul(self.ps[32 * j:32 * j + 31, 6, gr * 64:(gr + 1) * 64], hs[:, 1, gr, :],
                                       self.w2[:, 1, :], start=True, stop=True)
        p.did(ins, "vc_p")
        v.wait("vc_p", "vbd0")
        for j in range(4):
            v.did(nc.vector.tensor_copy(self.vbd[32 * j:32 * j + 31, :, j, :],
                                        self.ps[32 * j:32 * j + 31, 6, 0:256].rearrange("p (g d) -> p g d", g=4)), "bank6")

    def nsa_mix(self):
        nc, v, a, p, g = self.nc, self.v, self.a, self.p, self.g
        at = [self.h_at]

        def tmp(name, shape, dt=F32):
            t = self.sb(name, shape, dt, at=at[0])
            at[0] += (int(np.prod(shape[1:])) * 4 + 31) // 32 * 32
            assert at[0] <= self.h_at + 32768
            return t
        self.tmp = tmp
        for e in (a, v):
            e.wait("bank0", "bank4", "bank5", "bank6", "bank7")
        self.nsa_compress()
        at[0] = self.attention_scratch("n", at[0])
        qst = tmp("n_q", [64, 4, S])
        bs = [tmp(f"n_b{j}", [P, S]) for j in range(2)]
        o_tok = self.sb("o_tok", [P, TT, D], at=self.arena + 74752)
        base = self.arena + 49152
        spc, self_bc, pT, ot1 = (self.sb(f"n_x{i}", [P, S], at=base + i * 2048) for i in range(4))
        st = self.sb("n_stat", [P, 8, 16], at=base + 8192)
        cm, rc, fc = st[:, 0, :], st[:, 1, :], st[:, 2, :]
        mxs = self.sb("n_mx", [P, 8], at=base + 8192 + 512)
        rs = self.sb("n_rs", [P, 2, 4, 2], at=base + 8192 + 576)
        fac = self.sb("n_fac", [P, 2, 4, 2], at=base + 8192 + 640)
        C, Cc, slope, ok = self.c2["dist"], self.c2["dist_c"], self.c2["slope"], self.c2["seen"]
        O = [4, 5]
        self.forget("qst", "b_used0", "b_used1", "osum", *self.ATTEND_EVENTS)
        for e in (a, v, p, g):
            for n in range(8):
                e.wait(f"bank{n}")

        def body(i):
            a.wait("qk0", "qk1", "cs")
            a.did(nc.scalar.activation(qst[:, :, :], self.nq[:, bass.ds(4 * i, 4), :], ACT.Copy), "qst")
            p.wait("qst", "bank6")
            p.settle(True)
            for t in range(TT):
                for j in range(4):
                    c0 = (t * 4 + j) * 32
                    ins = nc.tensor.matmul(self.ps[:, 6, c0:c0 + 32], qst[:, j, t * P:(t + 1) * P],
                                           self.kc[:, bass.ds(i, 1), :], start=True, stop=True)
            p.did(ins, "cs")
            v.wait("cT")
            for j in range(4):
                dst = self_bc[:, :].rearrange("p (t j n) -> p t j n", t=TT, j=4)[:, :, j, :]
                v.did(nc.vector.tensor_scalar(dst, Cc.rearrange("p (t n) -> p t n", t=TT),
                                              slope[:, bass.ds(4 * i + j, 1)], None, ALU.mult), "bc")
            v.wait("bc", "cs")
            v.did(nc.vector.tensor_tensor(spc[:, :], self.ps[:, 6, :], self_bc[:, :], ALU.add), "bank6")
            v.wait("bank6")
            s3 = spc[:, :].rearrange("p (r n) -> p r n", n=32)
            v.did(nc.vector.tensor_reduce(cm, s3, AX.X, ALU.max), "cm")
            v.wait("cm")
            v.did(nc.vector.tensor_tensor(s3, s3, cm.unsqueeze(2).broadcast_to([P, 16, 32]), ALU.subtract), "cm")
            a.wait("cm")
            a.did(nc.scalar.activation(spc[:, :], spc[:, :], ACT.Exp), "ce")
            v.wait("ce")
            v.did(nc.vector.tensor_reduce(rc, s3, AX.X, ALU.add), "cm")
            v.wait("cm")
            v.did(nc.vector.reciprocal(rc, rc), "cm")
            v.wait("cm")
            v.did(nc.vector.tensor_tensor(rc, rc, ok, ALU.mult), "cm")
            v.wait("cm")
            gt = self.gate[:, :, bass.ds(12 * i, 12)].rearrange("p t (j b) -> p t j b", b=3)
            v.did(nc.vector.tensor_tensor(fc.rearrange("p (t j) -> p t j", t=TT), rc.rearrange("p (t j) -> p t j", t=TT),
                                          gt[:, :, :, 0], ALU.mult), "fc")
            p.wait("ce", "bank7")
            for t in range(TT):
                ins = nc.tensor.transpose(self.ps[:, 7, t * P:(t + 1) * P], spc[:, t * P:(t + 1) * P], self.c("ident"))
            p.did(ins, "cT")
            a.wait("cT", "cv")
            a.did(nc.scalar.activation(pT[:, :], self.ps[:, 7, :], ACT.Copy), "bank7")
            p.wait("bank7", "bank6")
            for t in range(TT):
                b = 7 if t < 2 else 6
                ins = nc.tensor.matmul(self.ps[:, b, (t % 2) * 256:(t % 2) * 256 + 256], pT[:, t * P:(t + 1) * P],
                                       self.vbd[:, bass.ds(i, 1), :, :], start=True, stop=True)
            p.did(ins, "cv")
            v.wait("cv", "fc")
            for half in range(2):
                dst = o_tok[:, 2 * half:2 * half + 2, bass.ds(256 * i, 256)].rearrange("p t (j d) -> p t j d", j=4)
                src = self.ps[:, 7 - half, :].rearrange("p (t j d) -> p t j d", t=2, j=4)
                f = fc.rearrange("p (t j) -> p t j", t=TT)[:, 2 * half:2 * half + 2, :].unsqueeze(3).broadcast_to([P, 2, 4, 64])
                v.did(nc.vector.tensor_tensor(dst, src, f, ALU.mult), f"bank{7 - half}")
            nothing = lambda: None
            blocks = []
            for j in range(4):
                jb = j % 2

                def make_bias(j=j, jb=jb):
                    v.wait(f"b_used{jb}")
                    v.did(nc.vector.tensor_scalar(bs[jb][:, :], C, slope[:, bass.ds(4 * i + j, 1)], None,
                                                  ALU.mult), f"bias{jb}")

                def combine(j=j, jb=jb):
                    v.wait("exp0", "exp1", "exp2", "exp3")
                    v.did(nc.vector.reciprocal(fac[:, jb, :, :], rs[:, jb, :, :]), "fac")
                    v.wait("fac")
                    gj = self.gate[:, :, bass.ds(12 * i + 3 * j + 1, 2)]
                    v.did(nc.vector.tensor_tensor(fac[:, jb, :, :], fac[:, jb, :, :], gj, ALU.mult), "fac")
                    v.wait("fac", "pv")
                    for br in range(2):
                        src = self.ps[:, O[jb], :].rearrange("p (t b d) -> p t b d", t=TT, b=2)[:, :, br, :]
                        f = fac[:, jb, :, br:br + 1].broadcast_to([P, TT, 64])
                        t3 = ot1[:, br * 256:(br + 1) * 256].rearrange("p (t d) -> p t d", t=TT)
                        v.did(nc.vector.tensor_tensor(t3, src, f, ALU.mult), f"ot{br}")
                    self.pr.events[f"bank{O[jb]}"] = self.pr.events["ot1"]
                    for br in range(2):
                        t3 = ot1[:, br * 256:(br + 1) * 256].rearrange("p (t d) -> p t d", t=TT)
                        o = o_tok[:, :, bass.ds(256 * i + 64 * j, 64)]
                        v.wait(f"ot{br}", "bank6", "osum")
                        v.did(nc.vector.tensor_tensor(o, o, t3, ALU.add), "osum")
                for br in range(2):
                    for t in range(TT):
                        first, last = br == 0 and t == 0, br == 1 and t == TT - 1
                        blocks.append(dict(
                            n=t + 1, q=qst[:, j, t * P:(t + 1) * P],
                            k=self.nk[:, bass.ds(i + 4 * br, 1), 0:(t + 1) * P],
                            bias=bs[jb][:, (3 - t) * P:S], bias_ready=(f"bias{jb}",), ready=("qst",),
                            v=lambda s, br=br: self.nv[:, s, bass.ds(64 * i + 256 * br, 64)],
                            out=self.ps[:, O[jb], (t * 2 + br) * 64:(t * 2 + br) * 64 + 64],
                            out_ready=(f"bank{O[jb]}",), rs=rs[:, jb, t, br:br + 1],
                            before=make_bias if first else nothing,
                            after_q=nothing,
                            done=combine if last else nothing))
            self.attend(blocks, mxs)
            for jb in range(2):
                self.pr.events[f"b_used{jb}"] = self.pr.events["osum"]
        self.pr.run_loop("nsa_heads", 4, body)
        for e in (a, v, p):
            e.wait("osum", "qst", "pv")
        self.token_to_h(o_tok, 0, KD)

    def token_to_h(self, src, first, count):
        nc = self.nc
        for n in range(count):
            kt, b = first + n, n % 4
            self.p.wait(f"bank{b}")
            for t in range(TT):
                ins = nc.tensor.transpose(self.ps[:, b, t * P:(t + 1) * P], src[:, t, n * P:(n + 1) * P], self.c("ident"))
            self.p.did(ins, f"oT{b}")
            self.a.wait(f"oT{b}")
            self.a.did(nc.scalar.activation(self.h_hi[:, kt, :], self.ps[:, b, :], ACT.Copy), f"hh{b}")
            self.v.wait(f"hh{b}")
            self.v.did(nc.vector.tensor_tensor(self.h_lo[:, kt, :], self.ps[:, b, :], self.h_hi[:, kt, :].bitcast(F32),
                                               ALU.subtract), f"h{kt}")
            self.pr.events[f"bank{b}"] = self.pr.events[f"h{kt}"]

    def dsa_weights(self):
        nc, io, at = self.nc, self.io, self.arena + 89344
        self.pool_w = self.sb("pool_w", [P, 4, P], at=at)
        self.qk_gain = self.sb("qk_gain", [P, 2, 64], at=at + 2048)
        nc.scalar.dma_start(self.pool_w[:, :, :], io["pool_w_2"][0].rearrange("g c d -> c g d")).then_inc(self.s_c2, 16)
        for n, name in enumerate(("q_norm_2", "k_norm_2")):
            nc.scalar.dma_start(self.qk_gain[:, n, :], io[name].partition_broadcast(P)
                                if len(io[name].shape) == 1 else io[name][0].partition_broadcast(P)) \
                .then_inc(self.s_c2, 16)
        self.n_c2 += 48

    def dsa_in(self):
        nc, v, a, w, ar = self.nc, self.v, self.a, self.io["w_in_2"][0], self.arena
        self.tq = self.sb("dsa_q", [P, TT, S], at=ar)
        self.tk = self.sb("dsa_k", [P, TT, S], at=ar + 8192)
        self.tv = self.sb("dsa_v", [P, TT, S], at=ar + 16384)
        self.ti = self.sb("dsa_i", [P, TT, 324], at=ar + 24576)
        self.mask = self.sb("dsa_mask", [P, 10 * P], at=ar + 29760)
        self.qT = self.sb("dsa_qT", [64, 8, S], at=ar + 34880)
        self.kT = self.sb("dsa_kT", [64, 8, S], at=ar + 51264)
        self.iT = self.sb("dsa_iT", [64, 5, S], at=ar + 67648)
        self.u = self.sb("dsa_u", [P, 4, S], at=ar + 77888)
        groups = [("token", 1536, 324, self.ti), ("token", 0, 512, self.tq), ("token", 512, 512, self.tk),
                  ("token", 1024, 512, self.tv), ("feature", 1860, 512, self.u)]
        for gi, (kind, c0, width, dst) in enumerate(groups):
            banks = range(4 * (gi % 2), 4 * (gi % 2) + 4)
            self.group(0, 0, banks, lambda u: self.k_tiles(w, u, slice(c0, c0 + width)), kind=kind, width=width)
            for n, b in enumerate(banks):
                e = (a, v)[n % 2]
                if n < 2:
                    self.group_done(e, 3)
                src = self.ps[:, b, 0:width]
                e.did(nc.scalar.activation(dst[:, n, :], src, ACT.Copy) if e is a
                      else nc.vector.tensor_copy(dst[:, n, :], src), f"bank{b}")
                self.pr.events[f"g{gi}_{n}"] = self.pr.events[f"bank{b}"]
            self.U += 4

    def rotate(self, x, heads, half, cs, sn, tables=None):
        nc, v = self.nc, self.v
        x1, x2 = x[:, :, :, 0:half], x[:, :, :, half:2 * half]
        t = [b[:, 0:TT * heads * half].rearrange("p (t h d) -> p t h d", t=TT, h=heads) for b in self.rt]
        c1, s2, c2, s1 = tables or (cs, sn, cs, sn)

        def wide(tb):
            return tb.rearrange("p (t d) -> p t d", t=TT).unsqueeze(2).broadcast_to([P, TT, heads, half])
        v.wait("rot")
        v.did(nc.vector.tensor_tensor(t[0], x1, wide(c1), ALU.mult))
        v.did(nc.vector.tensor_tensor(t[1], x2, wide(s2), ALU.mult))
        v.did(nc.vector.tensor_tensor(t[2], x2, wide(c2), ALU.mult))
        v.did(nc.vector.tensor_tensor(t[3], x1, wide(s1), ALU.mult), "rot")
        v.wait("rot")
        v.did(nc.vector.tensor_tensor(x1, t[0], t[1], ALU.subtract))
        v.did(nc.vector.tensor_tensor(x2, t[2], t[3], ALU.add), "rot")

    def heads_out(self, x, heads, dst, scale, base):
        for h in range(heads):
            b = base + h % 2
            self.p.wait(f"bank{b}", "rot")
            for t in range(TT):
                ins = self.nc.tensor.transpose(self.ps[0:64, b, t * P:(t + 1) * P], x[:, t, h * 64:(h + 1) * 64],
                                               self.c("ident"))
            self.p.did(ins, f"ho{b}")
            self.a.wait(f"ho{b}")
            self.a.did(self.nc.scalar.activation(dst[:, h, :], self.ps[0:64, b, :], ACT.Copy, scale=scale), f"bank{b}")
            self.pr.events["heads"] = self.pr.events[f"bank{b}"]

    def dsa_mix(self):
        nc, v, a, p, g = self.nc, self.v, self.a, self.p, self.g
        hb = self.h_at
        self.rt = [self.sb(f"rt{j}", [P, 1024], at=hb + j * 4096) for j in range(4)]
        sm = self.sb("dsa_small", [P, 256], at=hb + 16384 - 1024)
        cs, sn, ci, si = (self.c2[n] for n in ("cos", "sin", "cos_i", "sin_i"))
        for e in (v, p, a, g):
            e.reach(self.s_c2, self.n_c2)
            e.wait(*[f"bank{n}" for n in range(8)])
        v.did(nc.vector.tensor_scalar(self.ti[:, :, 320:324], self.ti[:, :, 320:324], (4 ** -0.5) * (64 ** -0.5),
                                      None, ALU.mult), "wi")
        i4 = self.ti[:, :, 0:320].rearrange("p t (h d) -> p t h d", d=64)
        self.rotate(i4, 5, 16, ci, si)
        self.heads_out(self.ti, 5, self.iT, 1.0, 0)
        off = [0, P, 3 * P, 6 * P]
        rl = [self.sb(f"relu{j}", [P, S], at=hb + 16384 + j * 2048) for j in range(2)]
        n = 0
        v.did(nc.vector.tensor_copy(self.mask[:, 0:P], self.c2["tri"]), "sc0")
        for t in range(1, TT):
            w = (t + 1) * P
            m = self.mask[:, off[t]:off[t] + w]
            for h in range(4):
                j = n % 2
                n += 1
                p.wait("heads", f"bank{2 + j}")
                p.did(nc.tensor.matmul(self.ps[:, 2 + j, 0:w], self.iT[:, h, t * P:(t + 1) * P], self.iT[:, 4, 0:w],
                                       start=True, stop=True), f"is{j}")
                a.wait(f"is{j}", f"relu_used{j}")
                a.did(nc.scalar.activation(rl[j][:, 0:w], self.ps[:, 2 + j, 0:w], ACT.Relu), f"bank{2 + j}")
                v.wait(f"bank{2 + j}", "wi")
                wc = self.ti[:, t, 320 + h:321 + h]
                if h == 0:
                    v.did(nc.vector.tensor_scalar(m, rl[j][:, 0:w], wc, None, ALU.mult), "acc")
                else:
                    v.wait("acc")
                    v.did(nc.vector.scalar_tensor_tensor(m, rl[j][:, 0:w], wc, m, ALU.mult, ALU.add), "acc")
                self.pr.events[f"relu_used{j}"] = self.pr.events["acc"]
            v.wait("acc")
            v.did(nc.vector.tensor_tensor(m[:, t * P:w], m[:, t * P:w], self.c2["tri"], ALU.add), f"sc{t}")
        sq = self.sb("dsa_sq", [P, TT, S], at=self.arena + 51264)
        ss, tabs = self.sb("dsa_ss", [P, 32], at=hb + 24576), self.sb("dsa_tab", [P, 4, P], at=hb + 24576 + 128)
        for n, (x, dst, scale) in enumerate(((self.tq, self.qT, 0.125), (self.tk, self.kT, 1.0))):
            gain = self.qk_gain[:, n, :]
            x4 = x[:, :, :].rearrange("p t (h d) -> p (t h) d", d=64)
            a.wait("ssum", f"g{n + 1}_0", f"g{n + 1}_1", f"g{n + 1}_3")
            v.wait(f"g{n + 1}_0", f"g{n + 1}_2", "rot")
            a.did(nc.scalar.activation(sq[:, :, :], x[:, :, :], ACT.Square), "qsq")
            v.wait("qsq")
            v.did(nc.vector.tensor_reduce(ss[:, :], sq[:, :, :].rearrange("p t (h d) -> p (t h) d", d=64), AX.X, ALU.add), "ssum")
            a.wait("ssum")
            a.did(nc.scalar.activation(ss[:, :], ss[:, :], ACT.Ln, bias=self.eps, scale=1.0 / 64), "sln")
            a.wait("sln")
            a.did(nc.scalar.activation(ss[:, :], ss[:, :], ACT.Exp, scale=-0.5), "sln")
            for k, (tb, off_g) in enumerate(((cs, 0), (sn, 32), (cs, 32), (sn, 0))):
                v.did(nc.vector.tensor_tensor(tabs[:, k, :].rearrange("p (t d) -> p t d", t=TT),
                                              tb.rearrange("p (t d) -> p t d", t=TT),
                                              gain[:, off_g:off_g + 32].unsqueeze(1).broadcast_to([P, TT, 32]),
                                              ALU.mult), "tab")
            v.wait("sln", "tab")
            v.did(nc.vector.tensor_tensor(x4, x4, ss[:, :].unsqueeze(2).broadcast_to([P, 32, 64]), ALU.mult), "rot")
            self.rotate(x[:, :, :].rearrange("p t (h d) -> p t h d", d=64), 8, 32, None, None,
                        tables=[tabs[:, k, :] for k in range(4)])
            if n == 0:
                self.heads_out(x, 8, dst, scale, 0)
        bufs = [self.sb(f"pool{j}", [P, 4, S], at=hb + 16384 + j * 8192) for j in range(2)]
        mx8 = self.small[:, 192:200]
        for t in range(1, TT):
            w = (t + 1) * P
            m = self.mask[:, off[t]:off[t] + w]

            def rounds(i, m=m, t=t):
                v.wait("mr", f"sc{t}")
                v.did(nc.vector.max(mx8, m), "m8")
                v.wait("m8")
                v.settle(True)
                v.did(nc.vector.match_replace(m, mx8, m, -3.3e38), "mr")
            for i in range(P // 8):
                rounds(i)
            v.wait("mr")
            v.did(nc.vector.tensor_scalar(m, m, -3.2e38, NEG, ALU.is_gt, ALU.mult), "mask")
        self.heads_out(self.tk, 8, self.kT, 1.0, 0)
        a.wait("heads")
        g.wait("acc", "rot", "heads")
        src = self.u
        for step in range(4):
            sh, dst = 1 << step, bufs[step % 2]
            g.wait("pl")
            g.did(nc.gpsimd.tensor_tensor(dst[:, step:4, sh:S], src[:, step:4, sh:S], src[:, step:4, 0:S - sh], ALU.add))
            g.did(nc.gpsimd.tensor_copy(dst[:, step:4, 0:sh], src[:, step:4, 0:sh]), "pl")
            d, uu = dst[:, step, :], self.u[:, step, :]
            v.wait("pl")
            corr = self.c2["corr"][:, step * 16:(step + 1) * 16]
            v.did(nc.vector.tensor_tensor(d[:, 0:16], d[:, 0:16], corr, ALU.mult), "pc")
            v.wait("pc")
            v.did(nc.vector.scalar_tensor_tensor(uu, d, 1.0 / (2 * sh), uu, ALU.mult, ALU.subtract), f"pooled{step}")
            self.pr.events["pooled"] = self.pr.events[f"pooled{step}"]
            g.wait(f"pooled{step}")
            src = dst
        self.attention_scratch("d", hb)
        qst = [self.sb(f"d_q{j}", [64, S], at=hb + 12288 + j * 2048) for j in range(2)]
        o_tok = self.sb("d_o", [P, TT, S], at=self.arena)
        st = self.sb("d_st", [P, 32], at=self.arena + 8192)
        mxs, rs, fac = st[:, 0:4], st[:, 8:16].rearrange("p (j t) -> p j t", j=2), \
            st[:, 16:24].rearrange("p (j t) -> p j t", j=2)
        self.forget("q_used0", "q_used1", *self.ATTEND_EVENTS)
        for e in (a, v, p):
            e.wait("mask", "rot", "heads", "pooled", "relu_used0", "relu_used1", *[f"bank{n}" for n in range(8)])

        def body(i):
            nothing = lambda: None
            blocks = []
            for j in range(2):
                a.wait(f"q_used{j}")
                a.did(nc.scalar.activation(qst[j][:, :].unsqueeze(1), self.qT[:, bass.ds(2 * i + j, 1), :], ACT.Copy), f"qst{j}")

                def combine(j=j):
                    v.wait("exp0", "exp1", "exp2", "exp3")
                    v.did(nc.vector.reciprocal(fac[:, j, :], rs[:, j, :]), "fac")
                    v.wait("fac", "pv")
                    v.did(nc.vector.tensor_tensor(o_tok[:, :, bass.ds(128 * i + 64 * j, 64)],
                                                  self.ps[:, 4 + j, 0:256].rearrange("p (t d) -> p t d", t=TT),
                                                  fac[:, j, :].unsqueeze(2).broadcast_to([P, TT, 64]), ALU.mult),
                          f"bank{4 + j}")

                def used(j=j):
                    self.pr.events[f"q_used{j}"] = p.prog.events[f"qk{1}"]
                for t in range(TT):
                    blocks.append(dict(
                        n=t + 1, q=qst[j][:, t * P:(t + 1) * P],
                        k=self.kT[:, bass.ds(2 * i + j, 1), 0:(t + 1) * P],
                        bias=self.mask[:, off[t]:off[t] + (t + 1) * P], bias_ready=(), ready=(f"qst{j}",),
                        v=lambda s, j=j: self.tv[:, s, bass.ds(128 * i + 64 * j, 64)],
                        out=self.ps[:, 4 + j, t * 64:t * 64 + 64], out_ready=(f"bank{4 + j}",),
                        rs=rs[:, j, t:t + 1], before=nothing,
                        after_q=used if t == TT - 1 else nothing,
                        done=combine if t == TT - 1 else nothing))
            self.attend(blocks, mxs)
        self.pr.run_loop("dsa_heads", 4, body)
        for e in (a, v, p):
            e.wait("bank4", "bank5", "qst0", "qst1", "pv")
        self.token_to_h(o_tok, 0, 4)
        for n in range(4):
            b = 4 + n
            p.wait(f"bank{b}")
            p.did(nc.tensor.matmul(self.ps[:, b, :], self.pool_w[:, n, :], self.u[:, n, :], start=True, stop=True), f"pw{n}")
            v.wait(f"pw{n}")
            v.did(nc.vector.tensor_scalar(self.u[:, n, :], self.ps[:, b, :], self.pool_scale[:, n:n + 1], None,
                                          ALU.mult), f"bank{b}")
            a.wait(f"bank{b}")
            a.did(nc.scalar.activation(self.h_hi[:, 4 + n, :], self.u[:, n, :], ACT.Copy), f"hh{n}")
            v.wait(f"hh{n}")
            v.did(nc.vector.tensor_tensor(self.h_lo[:, 4 + n, :], self.u[:, n, :], self.h_hi[:, 4 + n, :].bitcast(F32),
                                          ALU.subtract), f"h{4 + n}")

    def store_x(self):
        nc = self.nc
        ot = self.sb("out_tok", [P, TT, D], at=self.arena)
        out = self.io["out"].rearrange("b (t p) d -> p (b t) d", p=P)
        for t in range(TT):
            for half in range(2):
                b = (2 * t + half) % 8
                self.p.wait(f"bank{b}", *[f"x{n}" for n in range(KD)])
                for j in range(4):
                    kt = half * 4 + j
                    ins = nc.tensor.transpose(self.ps[:, b, j * P:(j + 1) * P], self.xT[:, kt, t * P:(t + 1) * P],
                                              self.c("ident"))
                self.p.did(ins, "xo")
                self.v.wait("xo")
                self.v.did(nc.vector.tensor_copy(ot[:, t, half * 512:(half + 1) * 512], self.ps[:, b, :]), "ot")
            self.s.wait("ot")
            nc.sync.dma_start(out[:, t:t + 1, :], ot[:, t:t + 1, :]).then_inc(self.s_out, 16)
        nc.sync.wait_ge(self.s_out, 16 * TT)


def bass_part(i):
    return i



def program(nc, io, const_at, per_loop):
    K = Kernel(nc, io, const_at, per_loop)
    K.names = iter(range(100))
    K.s_c2 = nc.alloc_semaphore("phase_constants_landed")
    K.n_c2 = 0

    def phase_constants(base, names):
        K.c2 = {}
        for n in names:
            o, w = K.const_at[n]
            t = K.sb(f"c2_{n}", [P, w], at=base)
            base += w * 4
            nc.scalar.dma_start(t[:, :], K.io["const2"][:, o:o + w]).then_inc(K.s_c2, 16)
            K.n_c2 += 16
            K.c2[n] = t[:, :]
    K.phase_constants = phase_constants
    K.start()
    K.lower_bounds()
    K.norm_scratch(K.arena)
    phase_constants(K.arena + 81920, [f"level{m}" for m in range(8)] + ["restart"])
    K.prologue()
    K.modulation_scales(0)
    K.norm(lambda kt: K.mod[:, 0, 1, kt:kt + 1], lambda kt: K.mod[:, 0, 0, kt:kt + 1], ("ms01", "mod00"))
    K.hgrn_in()
    for j, part in enumerate(range(2, 6)):
        K.mod_finish(0, part, j, j)
    K.modulation_scales(0)
    K.hgrn_mix()
    K.v.wait("mod_sum")
    K.out_proj(K.io["hg_w_out"][0], lambda kt: K.mod[:, 0, 2, kt:kt + 1], ("mod02",),
               extra=lambda u: K.mod_unit(1, 5, u, K.m_acc[:, 0, :], u))
    if STOP < 2:
        return K.finish_early()
    K.M += 8
    K.norm_scratch(K.arena)
    K.norm(lambda kt: K.mod[:, 0, 4, kt:kt + 1], lambda kt: K.mod[:, 0, 3, kt:kt + 1], ("ms04", "mod03"))
    K.mod_finish(1, 5, 0, 0)
    K.v.wait("mod_sum")
    K.ffn("ffn_a", K.io["ffn_w_up"][0][:, 0:FF], K.io["ffn_w_up"][0][:, FF:2 * FF], K.io["ffn_w_down"][0],
          lambda kt: K.mod[:, 0, 5, kt:kt + 1], conv=K.conv[0], need=("mod05",),
          extra=lambda i, m: K.mod_unit(1, i, m, K.m_acc[:, bass.ds(i, 1), :], m, 8))
    for part in range(5):
        K.mod_finish(1, part, part, part)
    K.modulation_scales(1)
    if STOP < 3:
        return K.finish_early()
    K.norm_scratch(K.arena)
    K.a.wait("x7")
    phase_constants(K.arena + 91136, ["dist", "dist_c", "slope", "seen"])
    K.nsa_weights()
    K.norm(lambda kt: K.mod[:, 1, 1, kt:kt + 1], lambda kt: K.mod[:, 1, 0, kt:kt + 1], ("ms11", "mod10"))
    K.nsa_in()
    K.nsa_mix()
    K.out_proj(K.io["nsa_w_out"][0], lambda kt: K.mod[:, 1, 2, kt:kt + 1], ("mod12",))
    if STOP < 4:
        return K.finish_early()
    K.norm_scratch(K.arena)
    K.norm(lambda kt: K.mod[:, 1, 4, kt:kt + 1], lambda kt: K.mod[:, 1, 3, kt:kt + 1], ("ms14", "mod13"))
    K.ffn("ffn_b", K.io["ffn_w_up"][1][:, 0:FF], K.io["ffn_w_up"][1][:, FF:2 * FF], K.io["ffn_w_down"][1],
          lambda kt: K.mod[:, 1, 5, kt:kt + 1], conv=K.conv[1], need=("mod15",))
    if STOP < 5:
        return K.finish_early()
    K.norm_scratch(K.arena)
    K.norm(lambda kt: K.norms["final_norm"][:, kt:kt + 1], None, (), into_x=True)
    K.norm(lambda kt: K.norms["ffn1_norm_2"][:, kt:kt + 1], None, ())
    K.ffn("ffn_c", K.io["ffn1_w_gate_2"][0], K.io["ffn1_w_up_2"][0], K.io["ffn1_w_down_2"][0], lambda kt: 0.5)
    if STOP < 6:
        return K.finish_early()
    K.norm_scratch(K.arena)
    K.a.wait("x7")
    phase_constants(K.arena + 91904, ["cos", "sin", "cos_i", "sin_i", "tri", "corr"])
    K.dsa_weights()
    K.norm(lambda kt: K.norms["mix_norm_2"][:, kt:kt + 1], None, ())
    K.dsa_in()
    K.dsa_mix()
    K.out_proj(K.io["w_out_2"][0], lambda kt: 1.0, ())
    K.norm_scratch(K.arena)
    K.norm(lambda kt: K.norms["ffn2_norm_2"][:, kt:kt + 1], None, ())
    K.ffn("ffn_d", K.io["ffn2_w_gate_2"][0], K.io["ffn2_w_up_2"][0], K.io["ffn2_w_down_2"][0], lambda kt: 0.5)
    return K.finish_early()


_OUT = (1, S, D)


def kernel(**inputs):
    import concourse.bacc as bacc
    from concourse.bass_utils import run_bass_kernel_spmd
    table, const_at = constants()
    small = const_at["ones"][0] + P
    arrays = {"const": np.ascontiguousarray(table[:, :small]), "const2": table}
    arrays.update({n: np.ascontiguousarray(a) for n, a in inputs.items()})

    def build(per_loop):
        nc = bacc.Bacc("TRN2", target_bir_lowering=False, num_devices=1)
        io = {}
        for n, a in arrays.items():
            io[n] = nc.dram_tensor("in_" + n, a.shape, mybir.dt.from_np(a.dtype), kind="ExternalInput").ap()
        io["out"] = nc.dram_tensor("out", _OUT, F32, kind="ExternalOutput").ap()
        return nc, program(nc, io, const_at, per_loop)
    _, counts = build({})
    nc, _ = build(counts)
    r = run_bass_kernel_spmd(nc, [{"in_" + n: a for n, a in arrays.items()}], core_ids=[0])
    return r.results[0]["out"]
```

```python
import numpy as np

import concourse.bass as bass
import concourse.mybir as mybir

F32 = mybir.dt.float32
F32R = mybir.dt.float32r
I32 = mybir.dt.int32
ALU = mybir.AluOpType
ACT = mybir.ActivationFunctionType
AX = mybir.AxisListType

P = 128
S = 512
D = 1024
KD = D // P
TT = S // P
FF = 2816
KF = FF // P
EPS = 1e-6
NEG = -1e30
RAW = 4
SPL = 2


class Event:
    def __init__(self, eng, const, loop=None):
        self.eng, self.const, self.loop = eng, const, loop


class Engine:
    def __init__(self, prog, name, raw):
        self.prog, self.name, self.e = prog, name, raw
        self.sem = prog.nc.alloc_semaphore("done_" + name)
        self.n = 0
        self.seen = {}

    def did(self, instruction, name=None):
        instruction.then_inc(self.sem, 1)
        self.n += 1
        if name is not None:
            self.prog.events[name] = Event(self, self.n, self.prog.loop)
        return instruction

    def wait(self, *names):
        for name in names:
            self.prog.wait(self, name)

    def reach(self, sem, const, step=0):
        loop = self.prog.loop
        if loop is None or step == 0:
            if const > 0:
                self.e.wait_ge(sem, const)
        else:
            assert const > 0, const
            self.e.wait_ge(sem, loop["i"] * step + const)
            self.settle()

    def settle(self, always=False):
        if (always or self.name in ("scalar", "gpsimd")) and self.prog.loop is not None:
            self.e.sem_inc(self.prog.settled[self.name], 1)


class Program:
    def __init__(self, nc, per_loop):
        self.nc = nc
        self.per_loop = per_loop
        self.learned = {}
        self.events = {}
        self.loop = None
        self.v = Engine(self, "vector", nc.vector)
        self.a = Engine(self, "scalar", nc.scalar)
        self.g = Engine(self, "gpsimd", nc.gpsimd)
        self.p = Engine(self, "tensor", nc.tensor)
        self.s = Engine(self, "sync", nc.sync)
        self.settled = {n: nc.alloc_semaphore("settled_" + n) for n in ("scalar", "gpsimd", "vector", "tensor")}
        self.engines = [self.v, self.a, self.g, self.p, self.s]

    def wait(self, eng, name):
        loop = self.loop
        ev = self.events.get(name)
        here = ev is not None and loop is not None and ev.loop is loop
        if not here:
            if ev is not None:
                const = ev.const
                if ev.loop is not None:
                    L = ev.loop
                    const += (L["count"] - 1) * L["per"][ev.eng.name]
                key = (ev.eng.name, None)
                if eng.seen.get(key, 0) < const:
                    eng.e.wait_ge(ev.eng.sem, const)
                    eng.seen[key] = const
            if loop is not None and name in loop["last"]:
                producer, k = loop["last"][name]
                src = next(x for x in self.engines if x.name == producer)
                self.wait_iter(eng, src, loop["base"][producer] + k - loop["per"][producer])
            return
        self.wait_iter(eng, ev.eng, ev.const)

    def wait_iter(self, eng, src, const):
        loop = self.loop
        key = (src.name, loop["name"])
        if eng.seen.get(key, -10**9) >= const:
            return
        eng.seen[key] = const
        per = loop["per"][src.name]
        if per:
            assert const > 0, (loop["name"], const)
            eng.e.wait_ge(src.sem, loop["i"] * per + const)
            eng.settle()
        elif const > 0:
            eng.e.wait_ge(src.sem, const)

    def run_loop(self, name, count, body):
        base = {e.name: e.n for e in self.engines}
        per, last = self.per_loop.get(name, ({e.name: 0 for e in self.engines}, {}))
        with self.nc.Fori(0, count) as i:
            L = dict(name=name, i=i, count=count, base=base, per=per, last=last)
            self.loop = L
            body(i)
            self.loop = None
        made = {e.name: e.n - base[e.name] for e in self.engines}
        self.learned[name] = (made, {n: (ev.eng.name, ev.const - base[ev.eng.name])
                                     for n, ev in self.events.items() if ev.loop is L})
        L["per"] = made
        for e in self.engines:
            for src in self.engines:
                const = e.seen.pop((src.name, name), None)
                if const is not None:
                    whole = const + (count - 1) * made[src.name]
                    e.seen[(src.name, None)] = max(whole, e.seen.get((src.name, None), 0))
            e.n = base[e.name] + count * made[e.name]


def constants():
    p = np.arange(P)[:, None]
    cols, at = [], {}

    def put(name, a):
        a = np.asarray(a, np.float32).reshape(P, -1)
        at[name] = (sum(c.shape[1] for c in cols), a.shape[1])
        cols.append(a)

    put("ident", np.eye(P))
    put("ones", np.ones((P, P)))
    f = np.arange(P)[None, :]
    for m in range(7):
        hs = 1 << m
        own = (p // (2 * hs) == f // (2 * hs)) & (p // hs % 2 == 0) & (f // hs % 2 == 1)
        put(f"level{m}", own.astype(np.int32).view(np.float32))
    put("level7", (p == f).astype(np.int32).view(np.float32))
    t = np.arange(S)[None, :]
    put("restart", np.broadcast_to((t % P != 0), (P, S)))
    u = np.arange(S)[None, :]
    put("dist", np.where(u <= p + 3 * P, -(p + 3 * P - u).astype(np.float64), NEG))
    n = np.arange(32)[None, None, :]
    tok = (np.arange(TT)[None, :, None] * P + p[:, :, None])
    put("dist_c", np.where((n < 31) & (n * 16 + 31 <= tok), -(tok - (n * 16 + 15.5)), NEG))
    put("slope", np.broadcast_to(2.0 ** (-8.0 * (np.arange(16)[None, :] + 1) / 16), (P, 16)))
    put("seen", np.broadcast_to(tok >= 31, (P, TT, 4)))
    for tag, half in (("", 32), ("_i", 16)):
        inv = np.float32(10000.0) ** (-np.arange(half, dtype=np.float32) / np.float32(half))
        ang = tok[:, :, 0:1].astype(np.float32) * inv[None, None, :].astype(np.float32)
        put("cos" + tag, np.cos(ang))
        put("sin" + tag, np.sin(ang))
    put("tri", np.where(f <= p, 0.0, NEG))
    t16 = np.arange(16) + 1.0
    put("corr", np.broadcast_to(np.stack([w / np.minimum(t16, w) for w in (2, 4, 8, 16)]), (P, 4, 16)))
    return np.concatenate(cols, 1), at


class Kernel:
    def __init__(self, nc, io, const_at, per_loop):
        self.nc, self.io, self.const_at = nc, io, const_at
        self.pr = Program(nc, per_loop)
        self.v, self.a, self.g, self.p, self.s = self.pr.engines
        nc_alloc = nc.alloc_sbuf_tensor_at
        self.at = (nc.sbuf_base + 31) // 32 * 32
        self.used = 0

        def sb(name, shape, dt=F32, at=None):
            size = int(np.prod(shape[1:])) * 4
            if at is None:
                at = self.at
                self.at += (size + 31) // 32 * 32
            assert at + size <= nc.sbuf_usable_end, (name, at + size)
            return nc_alloc(name, shape, dt, offset=at)
        self.sb = sb
        width = const_at['ones'][0] + P
        self.const = sb("const", [P, width])
        self.xT = sb("xT", [P, KD, S])
        self.h_at = self.at
        self.h_hi = sb("h_hi", [P, KD, S], F32R)
        self.h_lo = sb("h_lo", [P, KD, S], F32R)
        self.w_raw = [sb(f"w_raw{i}", [P, 1024]) for i in range(RAW)]
        self.w_hi = [sb(f"w_hi{i}", [P, 1024], F32R) for i in range(SPL)]
        self.w_lo = [sb(f"w_lo{i}", [P, 1024], F32R) for i in range(SPL)]
        self.m_at = self.at
        self.m_raw = [sb(f"m_raw{i}", [P, 1024]) for i in range(2)]
        self.m_acc = sb("m_acc", [P, 5, 1024])
        self.mod = sb("mod", [P, 2, 6, KD])
        self.cvec = sb("cvec", [P, KD])
        self.vecs = sb("vecs", [P, 4, P])
        self.small = sb("small", [P, 256])
        self.scr_at = self.at
        self.arena = self.at
        self.ps = nc.alloc_psum_tensor("ps", [P, 8, S], F32)
        sem = nc.alloc_semaphore
        self.s_raw = [sem(f"raw_landed{i}") for i in range(RAW)]
        self.s_hi = sem("weights_high")
        self.s_lo = sem("weights_low")
        self.s_mm = sem("unit_multiplied")
        self.s_m = [sem(f"mod_landed{i}") for i in range(2)]
        self.s_mac = sem("mod_unit_added")
        self.s_const = sem("constants_landed")
        self.s_out = sem("output_stored")
        self.n_const = 0
        self.U = 0
        self.US = 0
        self.M = 0

    def c(self, name):
        o, w = self.const_at[name]
        return self.const[:, o:o + w]

    def load_const(self, dst, src):
        self.nc.scalar.dma_start(dst, src).then_inc(self.s_const, 16)
        self.n_const += 16

    def load_unit(self, halves, k=0, step=0):
        u = self.U + k
        slot = u % RAW
        assert step % RAW == 0
        self.s.reach(self.s_lo, u + 1, step)
        for dst, src in halves(self.w_raw[slot]):
            self.nc.sync.dma_start(dst, src).then_inc(self.s_raw[slot], 16)

    def split_unit(self, cols=1024, k=0, step=0, view=None):
        u = self.U + k
        if u >= self.pr.per_loop.get("units", 10**9):
            return
        raw, hi, lo = self.w_raw[u % RAW], self.w_hi[u % SPL], self.w_lo[u % SPL]
        pick = view or (lambda t: t[:, 0:cols])
        for e in (self.a, self.v):
            e.reach(self.s_raw[u % RAW], 32 * (u // RAW + 1), 32 * step // RAW)
            e.reach(self.s_mm, u + 1, step)
        self.nc.scalar.activation(pick(hi), pick(raw), ACT.Copy).then_inc(self.s_hi, 1)
        self.v.reach(self.s_hi, u + 1, step)
        self.nc.vector.tensor_tensor(pick(lo), pick(raw), pick(hi).bitcast(F32),
                                     ALU.subtract).then_inc(self.s_lo, 1)

    def multiply_unit(self, products, k=0, step=0, each_sum=None):
        u = self.U + k
        self.p.reach(self.s_lo, u + 1 + RAW, step)
        items = list(products(self.w_hi[u % SPL], self.w_lo[u % SPL]))
        n = 0
        for at, (out, lhsT, rhs, start, stop) in enumerate(items):
            ins = self.nc.tensor.matmul(out, lhsT, rhs, start=start, stop=stop)
            if at == len(items) - 1:
                ins.then_inc(self.s_mm, 1)
            if each_sum and stop:
                if at == len(items) - 1:
                    each_sum(n, lambda e: self.group_done(e, k, step))
                else:
                    self.p.did(ins, f"sum{n}")
                    each_sum(n, lambda e, n=n: e.wait(f"sum{n}"))
                n += 1

    def group_done(self, eng, k, step=0):
        eng.reach(self.s_mm, self.U + k + 1 + SPL, step)

    def mod_unit(self, layer, part, kt, acc, k, step=0):
        m = self.M + k
        raw = self.m_raw[m % 2]
        if m >= 2:
            self.g.reach(self.s_mac, m - 1, step)
        cols = bass.ds(part * D, D) if not isinstance(part, int) else slice(part * D, (part + 1) * D)
        self.nc.gpsimd.dma_start(raw[:, :], self.io["ada_w"][layer, kt * P:(kt + 1) * P, cols]) \
            .then_inc(self.s_m[m % 2], 16)
        self.v.reach(self.s_m[m % 2], 16 * (m // 2 + 1), 8 * step)
        if m >= 1:
            self.v.reach(self.s_mac, m, step)
        if kt == 0:
            ins = self.nc.vector.tensor_scalar(acc, raw[:, :], self.cvec[:, kt:kt + 1], None, ALU.mult)
        else:
            ins = self.nc.vector.scalar_tensor_tensor(acc, raw[:, :], self.cvec[:, kt:kt + 1], acc,
                                                      ALU.mult, ALU.add)
        ins.then_inc(self.s_mac, 1)

    def mod_sums(self, slots, bank):
        self.p.reach(self.s_mac, self.M)
        self.p.wait(f"bank{bank}")
        for j, slot in enumerate(slots):
            for n in range(KD):
                ins = self.nc.tensor.matmul(self.ps[:, bank, j * KD + n:j * KD + n + 1],
                                            self.m_acc[:, slot, n * P:(n + 1) * P],
                                            self.c("ones")[:, 0:1], start=True, stop=True)
        self.p.did(ins, "mod_sum")

    def mod_add(self, layer, parts, bank):
        self.v.wait("mod_sum")
        for j, part in enumerate(parts):
            self.v.did(self.nc.vector.tensor_tensor(self.mod[:, layer, part, :], self.ps[:, bank, j * KD:(j + 1) * KD],
                                                    self.mod_b[:, layer, part, :], ALU.add), f"bank{bank}")
            self.pr.events[f"mod{layer}{part}"] = self.pr.events[f"bank{bank}"]

    def mod_finish(self, layer, part, slot, bank):
        self.mod_sums([slot], bank)
        self.mod_add(layer, [part], bank)

    def group_load(self, k, step, pieces):
        for u in range(4):
            def halves(raw, u=u):
                two = raw[:, :].rearrange("p (kk c) -> p kk c", kk=2)
                for (kk, cols), src in pieces(u):
                    yield two[:, kk, cols], src
            self.load_unit(halves, k + u, step)

    @staticmethod
    def k_tiles(w, u, cols):
        for kk in range(2):
            kt = 2 * u + kk
            width = cols.stop - cols.start if isinstance(cols, slice) else 512
            yield (kk, slice(0, width)), w[kt * P:(kt + 1) * P, cols]

    def feature_products(self, u, banks):
        def products(hi, lo):
            for kk in range(2):
                kt = 2 * u + kk
                for n, b in enumerate(banks):
                    c = kk * 512 + n * P
                    out = self.ps[:, b, :]
                    yield out, hi[:, c:c + P], self.h_hi[:, kt, :], kt == 0, False
                    yield out, hi[:, c:c + P], self.h_lo[:, kt, :], False, False
                    yield out, lo[:, c:c + P], self.h_hi[:, kt, :], False, kt == KD - 1
        return products

    def token_products(self, u, banks, width=512):
        def products(hi, lo):
            for kk in range(2):
                kt = 2 * u + kk
                for t, b in enumerate(banks):
                    out = self.ps[:, b, 0:width]
                    w = slice(kk * 512, kk * 512 + width)
                    tok = slice(t * P, (t + 1) * P)
                    yield out, self.h_hi[:, kt, tok], hi[:, w], kt == 0, False
                    yield out, self.h_lo[:, kt, tok], hi[:, w], False, False
                    yield out, self.h_hi[:, kt, tok], lo[:, w], False, kt == KD - 1
        return products

    def group(self, k, step, banks, pieces, kind="feature", width=512, extra=None,
              each_sum=None):
        self.group_load(k, step, pieces)
        for u in range(4):
            self.p.wait(*([f"h{2 * u}", f"h{2 * u + 1}"]))
            if u == 0:
                self.p.wait(*[f"bank{b}" for b in banks])
            if kind == "feature":
                self.multiply_unit(self.feature_products(u, banks), k + u, step, each_sum if u == 3 else None)
            else:
                self.multiply_unit(self.token_products(u, banks, width), k + u, step)
            w = width if u < 2 else 512
            view = None if w == 512 else (lambda t, w=w: t[:, :].rearrange("p (a b) -> p a b", a=2)[:, :, 0:w])
            self.split_unit(k=k + u + 2, step=step, view=view)
            if extra:
                extra(u)

    def square(self, kt):
        self.a.wait(f"x{kt}", f"sq_used{kt % 2}")
        self.a.did(self.nc.scalar.activation(self.sq[kt % 2][:, :], self.xT[:, kt, :], ACT.Square), f"sq{kt % 2}")

    def square_sum(self, kt):
        self.p.wait(f"sq{kt % 2}")
        if kt == 0:
            self.p.wait("bank0")
        ins = self.nc.tensor.matmul(self.ps[:, 0, :], self.c("ones"), self.sq[kt % 2][:, :],
                                    start=kt == 0, stop=kt == KD - 1)
        self.p.did(ins, f"sq_used{kt % 2}")
        self.summed = kt + 1

    def add_and_square(self, kt, bank, gain, wait):
        wait(self.v)
        self.add_to_x(kt, bank, gain)
        if kt == KD - 1:
            self.warm_ln()
        self.square_next(kt)

    def square_next(self, kt):
        for n in range(self.squared, min(kt + 1, self.summed + 2)):
            self.square(n)
            self.squared = n + 1
        if self.summed <= kt - 3 and self.summed < self.squared:
            self.square_sum(self.summed)

    def warm_ln(self):
        self.a.did(self.nc.scalar.activation(self.small[:, 2:3], self.eps, ACT.Ln))

    def norm(self, scale, bias, need, into_x=False):
        self.norm_sums()
        self.norm_apply(scale, bias, need, into_x)

    def norm_sums(self):
        nc, bank = self.nc, 0
        for kt in range(self.summed, KD):
            if kt >= self.squared:
                self.square(kt)
                self.squared = kt + 1
            if kt + 1 == self.squared < KD:
                self.square(kt + 1)
                self.squared = kt + 2
            self.square_sum(kt)
        self.squared = self.summed = 0
        self.a.wait(f"sq_used{(KD - 1) % 2}")
        self.a.did(nc.scalar.activation(self.rstd[:, :], self.ps[:, bank, :], ACT.Ln, bias=self.eps,
                                        scale=1.0 / D), f"bank{bank}")
        self.a.wait(f"bank{bank}")
        self.a.did(nc.scalar.activation(self.rstd[:, :], self.rstd[:, :], ACT.Exp, scale=-0.5), "rstd")

    def norm_apply(self, scale, bias, need, into_x=False):
        nc = self.nc
        self.a.wait(*need)
        self.v.wait("rstd", *need)
        for kt in range(KD):
            t = self.nt[kt % 4]
            if into_x:
                self.v.did(nc.vector.scalar_tensor_tensor(self.xT[:, kt, :], self.xT[:, kt, :], scale(kt),
                                                          self.rstd[:, :], ALU.mult, ALU.mult), f"x{kt}")
                continue
            self.v.did(nc.vector.scalar_tensor_tensor(t[:, :], self.xT[:, kt, :], scale(kt),
                                                      self.rstd[:, :], ALU.mult, ALU.mult), f"nt{kt % 4}")
            self.a.wait(f"nt{kt % 4}")
            hi = self.h_hi[:, kt, :]
            self.a.did(nc.scalar.activation(hi, t[:, :], ACT.Identity, bias=bias(kt)) if bias else
                       nc.scalar.activation(hi, t[:, :], ACT.Copy), f"hh{kt % 2}")
            if kt:
                self.low_part(kt - 1, bias)
        if not into_x:
            self.low_part(KD - 1, bias)

    def low_part(self, kt, bias):
        nc, t, hi, lo = self.nc, self.nt[kt % 4], self.h_hi[:, kt, :].bitcast(F32), self.h_lo[:, kt, :]
        self.v.wait(f"hh{kt % 2}")
        self.v.did(nc.vector.scalar_tensor_tensor(lo, t[:, :], bias(kt), hi, ALU.add, ALU.subtract) if bias else
                   nc.vector.tensor_tensor(lo, t[:, :], hi, ALU.subtract), f"h{kt}")

    def norm_scratch(self, base, sq=None):
        n = next(self.names)
        self.sq = [self.sb(f"sq{n}_{i}", [P, S], at=(base if sq is None else sq) + i * 2048) for i in range(2)]
        self.nt = [self.sb(f"nt{n}_{i}", [P, S], at=base + (2 + i) * 2048) for i in range(4)]
        self.rstd = self.sb(f"rstd{n}", [P, S], at=base + 6 * 2048)

    def start(self):
        nc, io = self.nc, self.io
        nc.vector.sem_inc(self.s_lo, RAW)
        nc.tensor.sem_inc(self.s_mm, SPL)
        nc.vector.sem_inc(self.v.sem, 8); self.v.n = 8
        nc.scalar.sem_inc(self.a.sem, 8); self.a.n = 8
        nc.gpsimd.sem_inc(self.g.sem, 8); self.g.n = 8
        nc.tensor.sem_inc(self.p.sem, 8); self.p.n = 8
        first = [self.m_raw[0][:, :], self.m_raw[1][:, :]] + [self.m_acc[:, k, :] for k in (2, 3, 4)]
        self.s_first = [nc.alloc_semaphore(f"first_mod_landed{k}") for k in range(len(first))]

        def load_first(u):
            self.s.wait(f"first{u % len(first)}")
            nc.sync.dma_start(first[u % len(first)], io["ada_w"][0, u % KD * P:(u % KD + 1) * P,
                                                                 u // KD * D:(u // KD + 1) * D]) \
                .then_inc(self.s_first[u % len(first)], 16)
        for u in range(len(first)):
            load_first(u)
        xin = self.sb("xin", [P, TT, D], at=self.arena)
        self.load_const(self.const[:, :], io["const"])
        self.load_const(xin[:, :, :], io["x"].rearrange("b (t p) d -> p (b t) d", p=P))
        rows = self.sb("vec_rows", [P, 4, P], at=self.arena + 16384)
        at = {}

        def vec(tile, name, src, n):
            lo = sum(k for (t, k) in at.values() if t == tile)
            at[name] = (tile, n)
            self.load_const(rows[lo:lo + n, tile, :], src)
            return self.vecs[:, tile, lo:lo + n]
        self.mod_b = vec(0, "ada_b", io["ada_b"].rearrange("l (r p) -> (l r) p", p=P), 96) \
            .rearrange("p (l a k) -> p l a k", l=2, a=6)
        self.c_in = vec(0, "c", io["c"].rearrange("b (k p) -> (b k) p", p=P), KD)
        self.lbp = vec(0, "hg_lb", io["hg_lb"].rearrange("a (k p) -> (a k) p", p=P), 16) \
            .rearrange("p (a k) -> p a k", a=2)
        self.gn = vec(0, "hg_gnorm", io["hg_gnorm"], 1)
        self.norms = {}
        for name in ("norm_mix", "norm_ffn", "final_norm", "ffn1_norm_2", "mix_norm_2", "ffn2_norm_2"):
            src = io[name]
            src = src.rearrange("(k p) -> k p", p=P) if name == "final_norm" else \
                src.rearrange("l (k p) -> (l k) p", p=P)
            self.norms[name] = vec(1, name, src, src.shape[0])
        self.pool_scale = vec(1, "pool_scale", io["pool_scale_2"].rearrange("l (k p) -> (l k) p", p=P), 4)
        self.conv = []
        for layer in range(2):
            w = vec(2 + layer, f"conv_w{layer}", io["ffn_conv_w"][layer].rearrange("w (k p) -> (w k) p", p=P), 3 * KF)
            bias = vec(2 + layer, f"conv_b{layer}", io["ffn_conv_b"][layer].rearrange("(k p) -> k p", p=P), KF)
            self.conv.append((w.rearrange("p (w k) -> p w k", w=3), bias))
        n_rows = [sum(k for (t, k) in at.values() if t == tile) for tile in range(4)]
        small = self.small
        self.eps, self.lb, self.oml = small[:, 0:1], small[:, 8:16], small[:, 16:24]
        for e in (self.v, self.a, self.p, self.g):
            e.reach(self.s_const, self.n_const)
        self.v.did(nc.vector.memset(self.eps, EPS), "eps")
        self.a.wait("eps")
        for tile, n in enumerate(n_rows):
            ins = nc.tensor.transpose(self.ps[:, 4 + tile, 0:n], rows[0:n, tile, :], self.c("ident")[0:n, 0:n])
            self.p.did(ins, "vec_t")
            self.v.wait("vec_t")
            self.v.did(nc.vector.tensor_copy(self.vecs[:, tile, 0:n], self.ps[:, 4 + tile, 0:n]), f"bank{4 + tile}")
        self.a.wait("bank7")
        self.a.did(nc.scalar.activation(self.cvec[:, :], self.c_in, ACT.Silu), "c_act")
        self.v.wait("c_act")
        for kt in range(KD):
            b = kt % 4
            if kt >= 4:
                self.p.wait(f"bank{b}")
            for t in range(TT):
                ins = nc.tensor.transpose(self.ps[:, b, t * P:(t + 1) * P], xin[:, t, kt * P:(kt + 1) * P],
                                          self.c("ident"))
            self.p.did(ins, "xt")
            self.a.wait("xt")
            self.a.did(nc.scalar.activation(self.xT[:, kt, :], self.ps[:, b, :], ACT.Copy), f"bank{b}")
            self.pr.events[f"x{kt}"] = self.pr.events[f"bank{b}"]
        self.norm_scratch(self.arena + 18432)
        self.squared = self.summed = 0
        self.norm_sums()
        for u in range(2 * KD):
            part, kt, slot = u // KD, u % KD, u % len(first)
            if u >= len(first):
                load_first(u)
            acc = self.m_acc[:, part, :]
            self.v.reach(self.s_first[slot], 16 * (u // len(first) + 1))
            if kt == 0:
                ins = nc.vector.tensor_scalar(acc, first[slot], self.cvec[:, kt:kt + 1], None, ALU.mult)
            else:
                self.v.wait("mac")
                ins = nc.vector.scalar_tensor_tensor(acc, first[slot], self.cvec[:, kt:kt + 1], acc, ALU.mult, ALU.add)
            self.v.did(ins, "mac")
            self.pr.events[f"first{slot}"] = self.pr.events["mac"]
            if kt == KD - 1:
                self.p.wait("mac")
                self.mod_finish(0, part, part, 4 + part)
        self.g.wait("mac")
        self.v.wait("mod_sum")

    def lower_bounds(self):
        nc, v, a = self.nc, self.v, self.a
        sc = self.small
        mx, e0, e1 = sc[:, 40:48], sc[:, 48:56], sc[:, 56:64]
        l0, l1 = self.lbp[:, 0, :], self.lbp[:, 1, :]
        v.did(nc.vector.tensor_tensor(mx, l0, l1, ALU.max), "lb_t"); v.wait("lb_t")
        v.did(nc.vector.tensor_tensor(e0, l0, mx, ALU.subtract), "lb_t")
        v.did(nc.vector.tensor_tensor(e1, l1, mx, ALU.subtract), "lb_t")
        a.wait("lb_t")
        a.did(nc.scalar.activation(sc[:, 48:64], sc[:, 48:64], ACT.Exp), "lb_e")
        v.wait("lb_e")
        v.did(nc.vector.tensor_tensor(mx, e0, e1, ALU.add), "lb_t"); v.wait("lb_t")
        v.did(nc.vector.reciprocal(mx, mx), "lb_t"); v.wait("lb_t")
        v.did(nc.vector.tensor_tensor(self.lb, e0, mx, ALU.mult), "lb_t")
        v.did(nc.vector.tensor_tensor(self.oml, e1, mx, ALU.mult), "lb")

    def modulation_scales(self, layer):
        nc, v = self.nc, self.v
        for part, gain in ((1, "norm_mix"), (4, "norm_ffn")):
            if f"mod{layer}{part}" not in self.pr.events or f"ms{layer}{part}" in self.pr.events:
                continue
            dst = self.mod[:, layer, part, :]
            v.wait(f"mod{layer}{part}")
            v.did(nc.vector.scalar_tensor_tensor(dst, dst, 1.0, self.norms[gain][:, layer * KD:(layer + 1) * KD],
                                                         ALU.add, ALU.mult),
                  f"ms{layer}{part}")

    def prologue(self):
        for k in range(2):
            self.split_unit(k=k)

    def hgrn_in(self):
        nc, w, v, a = self.nc, self.io["hg_w_in"], self.v, self.a
        self.proj = self.sb("proj", [P, 4 * KD, S], at=self.arena)
        self.hg_kk = self.sb("hg_k", [P, KD, S], at=self.arena + 65536)
        F, GT = KD, 3 * KD

        def half(gi, k, step, cols, part, acc, more=None):
            banks = range(4 * gi, 4 * gi + 4)

            def extra(u):
                self.mod_unit(0, part, 4 * gi + u, acc, k + u, step)
                if more:
                    more(4 * gi + u)
            self.group(k, step, banks, lambda u: self.k_tiles(w[0], u, cols), extra=extra)
            self.group_done(a, k + 3, step)
            self.group_done(v, k + 3, step)
            return banks

        for gi in range(2):
            banks = half(gi, 0, 0, slice(D + gi * 512, D + gi * 512 + 512), 2, self.m_acc[:, 0, :])
            for n, b in enumerate(banks):
                kt = 4 * gi + n
                k = self.hg_kk[:, kt, :]
                a.did(nc.scalar.activation(k, self.ps[:, b, :], ACT.Sigmoid, scale=-1.0), f"k_{kt}")
                a.did(nc.scalar.activation(self.proj[:, F + kt, :], self.ps[:, b, :], ACT.Sigmoid), f"bank{b}")
                v.wait(f"k_{kt}")
                v.did(nc.vector.tensor_scalar(k, k, self.oml[:, kt:kt + 1], None, ALU.mult), "k1")
            self.U += 4
            self.M += 4

        def body(i):
            for gi in range(2):
                banks = half(gi, 4 * gi, 8, bass.ds(i * 2048 + gi * 512, 512), i + 3, self.m_acc[:, bass.ds(i + 1, 1), :])
                for n, e in enumerate((a, v, a, v)):
                    dst = self.proj[:, bass.ds(i * 16 + gi * 4 + n, 1), :]
                    src = self.ps[:, banks[n]:banks[n] + 1, :]
                    e.did(nc.scalar.activation(dst, src, ACT.Copy) if e is a
                          else nc.vector.tensor_copy(dst, src), f"bank{banks[n]}")
        self.pr.run_loop("hgrn_in", 2, body)
        self.U += 16
        self.M += 16
        v.reach(self.s_c2, self.n_c2)

        def log_gate(kt):
            f = self.proj[:, F + kt, :]
            a.did(nc.scalar.activation(f, f, ACT.Ln, bias=self.lb[:, kt:kt + 1], scale=self.oml[:, kt:kt + 1]), "logf")
            v.wait("logf")
            v.did(nc.vector.tensor_tensor_scan(f, self.c2["restart"], f, 0.0, ALU.mult, ALU.add), "b")
        a.wait("bank3", "bank7")
        for gi in range(2):
            banks = half(gi, 0, 0, slice(3 * D + gi * 512, 3 * D + gi * 512 + 512), 5, self.m_acc[:, 3, :], log_gate)
            for n, b in enumerate(banks):
                a.did(nc.scalar.activation(self.proj[:, GT + 4 * gi + n, :], self.ps[:, b, :], ACT.Silu), f"bank{b}")
                self.pr.events["sg"] = self.pr.events[f"bank{b}"]
            self.U += 4
            self.M += 4

    def hgrn_mix(self):
        nc, v, a, g, p = self.nc, self.v, self.a, self.g, self.p
        pr = self.proj
        def place(base, end):
            at = [base]

            def tmp(name, shape, dt=F32):
                t = self.sb(name, shape, dt, at=at[0])
                at[0] += (int(np.prod(shape[1:])) * 4 + 31) // 32 * 32
                assert at[0] <= end
                return t
            return tmp
        tmp = place(self.h_at, self.h_at + 32768)
        kk = self.hg_kk
        diff = [tmp(f"hg_d{j}", [P, S]) for j in range(3)]
        G = [tmp(f"hg_g{j}", [P, S]) for j in range(3)]
        scT, qe, kdT, vT = ([tmp(f"hg_{n}{j}", [P, S]) for j in range(2)] for n in ("scT", "qe", "kdT", "vT"))
        kd, vs = tmp("hg_kd", [P, S]), tmp("hg_vs", [P, S])
        tmp = place(self.arena + 88064, self.arena + 94208)
        state = [tmp(f"hg_state{j}", [P, 3, P]) for j in range(2)]
        ebl = [tmp(f"hg_ebl{j}", [P, TT]) for j in range(2)]
        kdiff = tmp("hg_kdiff", [P, S])
        v.wait("bank3")
        g.wait("b", "k1")
        for j in range(2):
            v.did(nc.vector.memset(scT[j][:, :], 0.0), "scT0")

        HEADS = 4

        def flat(ap):
            return ap.rearrange("p a t -> p (a t)")

        def chunks(ap):
            return ap.rearrange("p (c t) -> p c t", c=TT)

        def body(i):
            heads = []
            for hh in range(HEADS):
                h = HEADS * i + hh
                heads.append(dict(j=hh % 2, q=flat(pr[:, bass.ds(h, 1), :]), b=flat(pr[:, bass.ds(h + 8, 1), :]),
                                  v=flat(pr[:, bass.ds(h + 16, 1), :]), k=flat(kk[:, bass.ds(h, 1), :])))

            def key_decay(H):
                last = chunks(H["b"])[:, :, P - 1:P]
                v.wait("kd_exp")
                v.did(nc.vector.tensor_tensor(chunks(kdiff[:, :]), last.to_broadcast([P, TT, P]), chunks(H["b"]),
                                              ALU.subtract), "kd_diff")

            def key_exp(H):
                j, last = H["j"], chunks(H["b"])[:, :, P - 1:P]
                a.wait("kd_diff", "kd_turned")
                a.did(nc.scalar.activation(kd[:, :], kdiff[:, :], ACT.Exp), "kd_exp")
                a.wait(f"state_done{j}")
                a.did(nc.scalar.activation(ebl[j][:, :], last.rearrange("p c t -> p (c t)"), ACT.Exp), f"ebl{j}")

            def values(H):
                a.wait("v_turned")
                a.did(nc.scalar.activation(vs[:, :], H["v"], ACT.Copy), "vs")

            def key_scale(H):
                g.wait("kd_exp")
                g.did(nc.gpsimd.tensor_tensor(kd[:, :], kd[:, :], H["k"], ALU.mult), "kd")

            def query_exp(H):
                j = H["j"]
                a.wait(f"o{j}")
                a.did(nc.scalar.activation(qe[j][:, :], H["b"], ACT.Exp), f"qe_exp{j}")

            def query_scale(H):
                j = H["j"]
                g.wait(f"qe_exp{j}")
                g.did(nc.gpsimd.tensor_tensor(qe[j][:, :], qe[j][:, :], H["q"], ALU.mult), f"qe{j}")

            def turn(H):
                for src, ready, bank, done in ((vs, "vs", 3, "v_turned"), (kd, "kd", 4, "kd_turned")):
                    p.wait(ready, f"bank{bank}")
                    for c in range(TT):
                        w = slice(c * P, (c + 1) * P)
                        ins = nc.tensor.transpose(self.ps[:, bank, w], src[:, w], self.c("ident"))
                    p.did(ins, done)

            def keep_turned(H):
                j = H["j"]
                for bank, dst, done in ((3, vT, "v_turned"), (4, kdT, "kd_turned")):
                    a.wait(done, f"o{j}", f"st{j}")
                    a.did(nc.scalar.activation(dst[j][:, :], self.ps[:, bank, :], ACT.Copy), f"bank{bank}")

            def carry(H):
                j = H["j"]
                p.wait("bank3", "bank4", "bank5")
                for c in range(TT - 1):
                    w = slice(c * P, (c + 1) * P)
                    ins = nc.tensor.matmul(self.ps[:, 5, w], kdT[j][:, w], vT[j][:, w], start=True, stop=True)
                p.did(ins, f"st{j}")

            def states(H):
                j = H["j"]
                v.wait(f"st{j}", f"o{j}", f"ebl{j}")
                for c in range(TT - 1):
                    add = self.ps[:, 5, c * P:(c + 1) * P]
                    if c == 0:
                        ins = nc.vector.tensor_copy(state[j][:, 0, :], add)
                    else:
                        v.wait(f"state_done{j}")
                        ins = nc.vector.scalar_tensor_tensor(state[j][:, c, :], state[j][:, c - 1, :],
                                                             ebl[j][:, c:c + 1], add, ALU.mult, ALU.add)
                    v.did(ins, f"state_done{j}")
                self.pr.events["bank5"] = self.pr.events[f"state_done{j}"]

            def output(H):
                j = H["j"]
                p.wait(f"scT{j}", f"state_done{j}", f"qe{j}", f"bank{6 + j}")
                for c in range(TT):
                    w = slice(c * P, (c + 1) * P)
                    ins = nc.tensor.matmul(self.ps[:, 6 + j, w], vT[j][:, w], scT[j][:, w], start=True, stop=c == 0)
                    if c:
                        ins = nc.tensor.matmul(self.ps[:, 6 + j, w], state[j][:, c - 1, :], qe[j][:, w],
                                               start=False, stop=True)
                p.did(ins, f"o{j}")

            def keep_output(H):
                j = H["j"]
                a.wait(f"o{j}")
                a.did(nc.scalar.activation(H["q"], self.ps[:, 6 + j, :], ACT.Copy), f"bank{6 + j}")

            def factors(n, H, m):
                r = n % 3
                if m == 7:
                    v.wait(f"S{r}", f"G{r}")
                    v.did(nc.vector.tensor_tensor(G[r][:, :], H["q"], H["k"], ALU.mult), f"G{r}")
                    return
                hs = 1 << m

                def halves(ap):
                    return ap.rearrange("p (n a t) -> p n a t", a=2, t=hs)
                bb, dd, gg = halves(H["b"]), halves(diff[r][:, :]), halves(G[r][:, :])
                ref = bb[:, :, 0, hs - 1:hs].to_broadcast([P, S // (2 * hs), hs])
                v.wait(f"G{r}")
                v.did(nc.vector.tensor_tensor(dd[:, :, 1, :], bb[:, :, 1, :], ref, ALU.subtract))
                v.did(nc.vector.tensor_tensor(dd[:, :, 0, :], ref, bb[:, :, 0, :], ALU.subtract), f"d{r}")
                a.wait(f"d{r}")
                a.did(nc.scalar.activation(diff[r][:, :], diff[r][:, :], ACT.Exp), f"e{r}")
                g.wait(f"e{r}", f"S{r}")
                g.did(nc.gpsimd.tensor_tensor(gg[:, :, 1, :], halves(H["q"])[:, :, 1, :], dd[:, :, 1, :], ALU.mult))
                g.did(nc.gpsimd.tensor_tensor(gg[:, :, 0, :], halves(H["k"])[:, :, 0, :], dd[:, :, 0, :], ALU.mult),
                      f"G{r}")

            def scores(n, m):
                r = n % 3
                p.wait(f"G{r}", f"bank{r}")
                for c in range(TT):
                    gc = G[r][:, c * P:(c + 1) * P]
                    ins = nc.tensor.matmul(self.ps[:, r, c * P:(c + 1) * P], gc,
                                           gc if m < 7 else self.c("ones"), start=True, stop=True)
                p.did(ins, f"S{r}")

            def place_scores(n, H, m):
                r, j = n % 3, H["j"]
                mask = self.c2[f"level{m}"].bitcast(I32).unsqueeze(1).broadcast_to([P, TT, P])
                v.wait(f"S{r}", f"o{j}", f"scT{j}")
                v.settle(True)
                v.did(nc.vector.copy_predicated(chunks(scT[j][:, :]), mask, chunks(self.ps[:, r, :])), f"scT{j}")
                self.pr.events[f"bank{r}"] = self.pr.events[f"scT{j}"]

            other = {0: [key_decay], 1: [key_exp], 2: [values, key_scale], 3: [query_exp], 4: [query_scale, turn],
                     7: [keep_turned], 9: [carry], 12: [states], 13: [output], 15: [keep_output]}
            for n in range(8 * HEADS + 8):
                H, m = (heads[n // 8], n % 8) if n < 8 * HEADS else (None, None)
                at_step = [(fn, heads[k]) for k in range(HEADS) for fn in other.get(n - 8 * k, [])]
                if H and m < 7:
                    factors(n, H, m)
                if 0 <= n - 3 < 8 * HEADS:
                    place_scores(n - 3, heads[(n - 3) // 8], (n - 3) % 8)
                if H:
                    if m == 7:
                        factors(n, H, m)
                    scores(n, m)
                for fn, head in at_step:
                    fn(head)
        self.forget("S0", "S1", "S2", "G0", "G1", "G2", "o0", "o1", "st0", "st1", "scT0", "scT1", "v_turned", "kd_exp",
                    "kd_turned", "state_done0", "state_done1")
        v.did(nc.vector.memset(self.small[:, 3:4], 0.0), "ready")
        for e in (a, v, p, g):
            e.wait("ready", *[f"bank{n}" for n in range(8)])
        g.wait("sg")
        a.wait("b")
        self.pr.run_loop("hg_heads", KD // HEADS, body)
        self.warm_ln()
        sq, rst = diff[0:2], [self.proj[:, 8 + kt, :] for kt in range(KD)]
        a.wait("scT0", "scT1", "G0", "G1", "G2", "bank5", "S0", "S1", "S2")
        for kt in range(KD):
            a.wait(f"hn_used{kt % 2}", "bank6", "bank7")
            a.did(nc.scalar.activation(sq[kt % 2][:, :], self.proj[:, kt, :], ACT.Square), f"hn_sq{kt % 2}")
            p.wait(f"hn_sq{kt % 2}", f"bank{kt}")
            p.did(nc.tensor.matmul(self.ps[:, kt, :], self.c("ones"), sq[kt % 2][:, :], start=True, stop=True),
                  f"hn_used{kt % 2}")
            if kt:
                a.wait(f"hn_used{(kt - 1) % 2}")
                a.did(nc.scalar.activation(rst[kt - 1], self.ps[:, kt - 1, :], ACT.Ln, bias=self.eps, scale=1.0 / P),
                      f"bank{kt - 1}")
        a.wait(f"hn_used{(KD - 1) % 2}")
        a.did(nc.scalar.activation(rst[KD - 1], self.ps[:, KD - 1, :], ACT.Ln, bias=self.eps, scale=1.0 / P), "bank7")
        a.wait("bank7")
        for kt in range(KD):
            a.did(nc.scalar.activation(rst[kt], rst[kt], ACT.Exp, scale=-0.5), f"hn_rst{kt}")
        self.mod_sums(range(4), 7)
        v.wait("bank6", "scT0", "scT1")
        for kt in range(KD + 1):
            if kt < KD:
                o, gt = self.proj[:, kt, :], self.proj[:, 24 + kt, :]
                v.wait(f"hn_rst{kt}")
                v.did(nc.vector.scalar_tensor_tensor(o, o, self.gn, rst[kt], ALU.mult, ALU.mult), "hn_o")
                e, ee = (g, nc.gpsimd) if kt % 2 else (v, nc.vector)
                e.wait("hn_o")
                e.did(ee.tensor_tensor(o, o, gt, ALU.mult), f"hn_g{kt}")
                a.wait(f"hn_g{kt}")
                a.did(nc.scalar.activation(self.h_hi[:, kt, :], o, ACT.Copy), f"hh{kt % 2}")
            if kt:
                o = self.proj[:, kt - 1, :]
                v.wait(f"hh{(kt - 1) % 2}")
                v.did(nc.vector.tensor_tensor(self.h_lo[:, kt - 1, :], o, self.h_hi[:, kt - 1, :].bitcast(F32),
                                              ALU.subtract), f"h{kt - 1}")

    def split_h(self, src, need):
        nc = self.nc
        self.a.wait(*need)
        self.v.wait(*need)
        for kt in range(KD):
            self.a.did(nc.scalar.activation(self.h_hi[:, kt, :], src(kt), ACT.Copy), f"hh{kt % 2}")
            self.v.wait(f"hh{kt % 2}")
            self.v.did(nc.vector.tensor_tensor(self.h_lo[:, kt, :], src(kt), self.h_hi[:, kt, :].bitcast(F32),
                                               ALU.subtract), f"h{kt}")

    def out_proj(self, w, gain, need, extra=None):
        nc = self.nc
        self.squared = self.summed = 0
        self.v.wait(*need)
        for gi in range(2):
            def beside(u):
                if extra:
                    extra(4 * gi + u)
                if gi and u < 3:
                    self.square(u)
                    self.square_sum(u)
                    self.squared = u + 1
            self.group(0, 0, range(4 * gi, 4 * gi + 4), lambda u: self.k_tiles(w, u, slice(gi * 512, (gi + 1) * 512)),
                       extra=beside,
                       each_sum=lambda n, wait: self.add_and_square(4 * gi + n, 4 * gi + n, gain, wait) if gi else
                       (wait(self.v), self.add_to_x(n, n, gain)))
            self.U += 4

    def add_to_x(self, kt, bank, gain):
        x = self.xT[:, kt, :]
        self.v.did(self.nc.vector.scalar_tensor_tensor(x, self.ps[:, bank, :], gain(kt), x, ALU.mult, ALU.add),
                   f"bank{bank}")
        self.pr.events[f"x{kt}"] = self.pr.events[f"bank{bank}"]

    def ffn(self, name, gate_w, up_w, down_w, gain, conv=None, need=(), extra=None, squares=True):
        nc, v, a, p = self.nc, self.v, self.a, self.p
        hid_hi = self.sb(f"hid_hi_{name}", [P, KF, S], F32R, at=self.arena)
        hid_lo = self.sb(f"hid_lo_{name}", [P, KF, S], F32R, at=self.arena + KF * 2048)
        cb = [self.sb(f"cb{j}_{name}", [P, S], at=self.arena + (2 * KF + j) * 2048) for j in range(2)]

        def up_group(f0, k, step, banks, ex=None):
            def pieces(u):
                cols = bass.ds(f0 * P, 256) if not isinstance(f0, int) else slice(f0 * P, f0 * P + 256)
                for half, w in enumerate((gate_w, up_w)):
                    yield (slice(0, 2), slice(half * 256, half * 256 + 256)), \
                        w[2 * u * P:(2 * u + 2) * P, cols].rearrange("(kk p) c -> p kk c", p=P)
            self.group(k, step, banks, pieces, extra=ex)
            self.group_done(a, k + 3, step)
            self.group_done(v, k + 3, step)
            def col(tb, f):
                return tb[:, bass.ds(f, 1)] if not isinstance(f, int) else tb[:, f:f + 1]

            def tile(tb, f):
                return tb[:, bass.ds(f, 1), :] if not isinstance(f, int) else tb[:, f:f + 1, :]
            gates = [self.ps[:, banks[j], :] for j in range(2)]
            if conv:
                wt, bias = conv
                for j in range(2):
                    v.wait(f"hid{j}")
                    v.did(nc.vector.tensor_scalar(cb[j][:, :], gates[j], col(wt[:, 2, :], f0 + j),
                                                  col(bias, f0 + j), ALU.mult, ALU.add), f"cv{j}")
                for sh in (1, 2):
                    for j in range(2):
                        v.wait(f"cv{j}")
                        v.did(nc.vector.scalar_tensor_tensor(
                            cb[j][:, sh:S], gates[j][:, 0:S - sh], col(wt[:, 2 - sh, :], f0 + j),
                            cb[j][:, sh:S], ALU.mult, ALU.add), f"cv{j}")
                        self.pr.events[f"bank{banks[j]}"] = self.pr.events[f"cv{j}"]
            for j in range(2):
                if conv:
                    a.wait(f"cv{j}")
                    a.did(nc.scalar.activation(cb[j][:, :], cb[j][:, :], ACT.Silu), f"silu{j}")
                else:
                    a.wait(f"hid{j}")
                    a.did(nc.scalar.activation(cb[j][:, :], gates[j], ACT.Silu), f"silu{j}")
                    self.pr.events[f"bank{banks[j]}"] = self.pr.events[f"silu{j}"]
            for j in range(2):
                v.wait(f"silu{j}")
                v.did(nc.vector.tensor_tensor(cb[j][:, :], cb[j][:, :], self.ps[:, banks[2 + j], :], ALU.mult),
                      f"bank{banks[2 + j]}")
                a.wait(f"bank{banks[2 + j]}")
                a.did(nc.scalar.activation(tile(hid_hi, f0 + j), cb[j][:, :].unsqueeze(1), ACT.Copy), f"hid_hi{j}")
            for j in range(2):
                v.wait(f"hid_hi{j}")
                v.did(nc.vector.tensor_tensor(tile(hid_lo, f0 + j), cb[j][:, :].unsqueeze(1),
                                              tile(hid_hi, f0 + j).bitcast(F32), ALU.subtract), f"hid{j}")

        def body(i):
            for gi in range(2):
                up_group(4 * i + 2 * gi, 4 * gi, 8, range(4 * gi, 4 * gi + 4),
                         (lambda u, gi=gi: extra(i, 4 * gi + u)) if extra else None)
        self.forget("hid0", "hid1")
        self.pr.run_loop(name, KF // 4, body)
        self.U += 8 * (KF // 4)
        if extra:
            self.M += 8 * (KF // 4)
        up_group(KF - 2, 0, 0, range(0, 4))
        self.U += 4

        def down_unit(kt, k, step, start, stop, each_sum=None):
            rows = bass.ds(kt * P, P) if not isinstance(kt, int) else slice(kt * P, (kt + 1) * P)

            def halves(raw):
                for c in range(2):
                    yield raw[:, c * 512:(c + 1) * 512], down_w[rows, c * 512:(c + 1) * 512]

            def products(hi, lo):
                for n in range(KD):
                    out = self.ps[:, n, :]
                    ht = hid_hi[:, bass.ds(kt, 1), :] if not isinstance(kt, int) else hid_hi[:, kt, :]
                    lt = hid_lo[:, bass.ds(kt, 1), :] if not isinstance(kt, int) else hid_lo[:, kt, :]
                    yield out, hi[:, n * P:(n + 1) * P], ht, start, False
                    yield out, hi[:, n * P:(n + 1) * P], lt, False, False
                    yield out, lo[:, n * P:(n + 1) * P], ht, False, stop
            self.load_unit(halves, k, step)
            self.multiply_unit(products, k, step, each_sum)
            self.split_unit(k=k + 2, step=step)
        p.wait("hid0", "hid1", *[f"bank{b}" for b in range(8)])
        for kt in range(2):
            down_unit(kt, 0, 0, kt == 0, False)
            self.U += 1

        def down_body(i):
            for j in range(4):
                down_unit(4 * i + 2 + j, j, 4, False, False)
        n = (KF - 2) // 4 - 1
        self.pr.run_loop(name + "_down", n, down_body)
        self.U += 4 * n
        self.v.wait(*need)
        self.norm_scratch(self.arena, sq=self.arena + 2 * KF * 2048)
        self.squared = self.summed = 0
        for kt in range(4 * n + 2, KF):
            down_unit(kt, 0, 0, False, kt == KF - 1,
                      None if kt < KF - 1 else lambda n, wait: self.add_and_square(n, n, gain, wait)
                      if squares else (wait(self.v), self.add_to_x(n, n, gain)))
            self.U += 1

    def finish(self):
        self.store_x()
        self.pr.learned["units"] = self.U
        return self.pr.learned

    def attention_scratch(self, tag, at, more):
        self.at_s = [self.sb(f"at_s{j}{tag}", [P, S], at=at + j * 2048 if j < 4 else more + (j - 4) * 2048)
                     for j in range(6)]
        self.at_t = [self.sb(f"at_t{j}{tag}", [P, S], at=at + (4 + j) * 2048) for j in range(2)]
        return at + 6 * 2048

    def attend(self, blocks, mx):
        TURN = 3
        nc, v, a, p = self.nc, self.v, self.a, self.p

        def scores(m, B):
            j, jp, w = m % 6, m % 2, B["n"] * P
            sc, mxc = self.at_s[j][:, 0:w], mx[:, j:j + 1]
            p.wait(f"sc_read{jp}", *B["ready"])
            p.settle(True)
            for n, (qq, kk) in enumerate(B["qk"]):
                ins = nc.tensor.matmul(self.ps[:, jp, 0:w], qq, kk, start=n == 0, stop=n == len(B["qk"]) - 1)
            p.did(ins, f"qk{jp}")
            B["after_q"]()
            v.wait(f"qk{jp}", f"pt{j}", *B["bias_ready"])
            v.settle(True)
            v.did(nc.vector.tensor_tensor_reduce(sc, self.ps[:, jp, 0:w], B["bias"], 1.0, -3e38,
                                                 ALU.add, ALU.max, mxc), f"sc_read{jp}")
            v.wait(f"sc_read{jp}")
            v.did(nc.vector.tensor_scalar(mxc, mxc, -1.0, None, ALU.mult), f"mx{j}")
            a.wait(f"mx{j}")
            a.did(nc.scalar.activation(sc, sc, ACT.Exp, bias=mxc, accum_out=B["rs"]), f"exp{j}")
            B["exp"] = self.pr.events[f"exp{j}"]

        def turn(m, B):
            j, jp, w = m % 6, m % 2, B["n"] * P
            p.wait(f"exp{j}", f"pt_read{jp}")
            for s in range(B["n"]):
                ins = nc.tensor.transpose(self.ps[:, 2 + jp, s * P:(s + 1) * P], self.at_s[j][:, s * P:(s + 1) * P],
                                          self.c("ident"))
            p.did(ins, f"pt{j}")
            self.pr.events[f"ptb{jp}"] = self.pr.events[f"pt{j}"]
            e = v if m % 3 == 0 else a
            e.wait(f"pt{j}", f"pv{jp}")
            dst, src = self.at_t[jp][:, 0:w], self.ps[:, 2 + jp, 0:w]
            e.did(nc.vector.tensor_copy(dst, src) if e is v else nc.scalar.activation(dst, src, ACT.Copy),
                  f"pt_read{jp}")

        def values(m, B):
            jp = m % 2
            p.wait(f"pt_read{jp}", *B["out_ready"])
            for s in range(B["n"]):
                ins = nc.tensor.matmul(B["out"], self.at_t[jp][:, s * P:(s + 1) * P], B["v"](s),
                                       start=s == 0, stop=s == B["n"] - 1)
            p.did(ins, f"pv{jp}")
            self.pr.events["pv"] = self.pr.events[f"pv{jp}"]
            self.pr.events["exp_of_block"] = B["exp"]
            B["done"]()
        for m in range(len(blocks) + TURN + 1):
            if m < len(blocks):
                blocks[m]["before"]()
                scores(m, blocks[m])
            if 0 <= m - TURN < len(blocks):
                turn(m - TURN, blocks[m - TURN])
            if m > TURN:
                values(m - TURN - 1, blocks[m - TURN - 1])

    ATTEND_EVENTS = [n + str(j) for n in ("pt", "ptb", "pt_read", "sc_read", "pv", "exp", "qk", "mx") for j in range(6)]

    def forget(self, *names):
        for n in names:
            self.pr.events.pop(n, None)

    def nsa_weights(self):
        nc, io = self.nc, self.io
        self.w1 = self.sb("nsa_w1", [64, 2, 32, 64], at=self.arena + 74752)
        self.w2 = self.small[0:64, 64:192].rearrange("p (a b) -> p a b", a=2)
        self.pe_rows = self.small[0:64, 192:256]
        for kv in range(2):
            nc.scalar.dma_start(self.w1[:, kv, :, :], io["nsa_cmp_w1"][0, kv].rearrange("(l d) h -> d l h", d=64)) \
                .then_inc(self.s_c2, 16)
            nc.scalar.dma_start(self.w2[:, kv, :], io["nsa_cmp_w2"][0, kv]).then_inc(self.s_c2, 16)
        nc.scalar.dma_start(self.pe_rows, io["nsa_cmp_pe"][0].rearrange("a l d -> (a l) d")).then_inc(self.s_c2, 16)
        self.n_c2 += 5 * 16

    def nsa_in(self):
        nc, v, a, w = self.nc, self.v, self.a, self.io["nsa_w_in"][0]
        ar = self.arena
        self.nq = self.sb("nsa_q", [64, 16, S], at=ar)
        self.nk = self.sb("nsa_k", [P, 8, S], F32R, at=ar + 32768)
        self.nk_lo = self.sb("nsa_k_lo", [64, 8, S], F32R, at=self.m_at + 12288)
        self.nc_kv = self.sb("nsa_ckv", [64, 8, S], at=ar + 49152)
        self.nv = self.sb("nsa_v", [P, TT, S], at=ar + 65536)
        self.gate = self.sb("nsa_gate", [P, TT, 48], at=ar + 73728)

        def cols(a0, n=512):
            return slice(a0, a0 + n)

        def strided(off):
            def pieces(u):
                for kk in range(2):
                    kt = 2 * u + kk
                    src = w[kt * P:(kt + 1) * P, 1536:2560].rearrange("p (b c) -> p b c", b=2)[:, :, off:off + 256]
                    yield (kk, slice(0, 512)), src
            return pieces

        groups = [("feature", lambda u: self.k_tiles(w, u, cols(1024)), [(self.nc_kv, n) for n in range(4)]),
                  ("feature", lambda u: self.k_tiles(w, u, cols(0)), [(self.nq, n) for n in range(4)]),
                  ("feature", lambda u: self.k_tiles(w, u, cols(512)), [(self.nq, n) for n in range(4, 8)]),
                  ("feature", strided(0), [(self.nk, n) for n in range(4)]),
                  ("token", strided(256), None),
                  ("token", lambda u: self.k_tiles(w, u, cols(2560, 48)), None)]
        self.compress_scratch()
        nothing = lambda: None
        beside = {2: [lambda: self.compress_pe(0), lambda: self.compress_pe(1), nothing, nothing],
                  5: [self.compress_bias, lambda: self.compress_hidden(0), lambda: self.compress_hidden(1),
                      self.compress_out]}
        for gi, (kind, pieces, dsts) in enumerate(groups):
            banks = range(4 * (gi % 2), 4 * (gi % 2) + 4)
            self.group(0, 0, banks, pieces, kind=kind, width=48 if gi == 5 else 512,
                       extra=(lambda u, gi=gi: beside[gi][u]()) if gi in beside else None)
            self.group_done(a, 3)
            self.group_done(v, 3)
            for n, b in enumerate(banks):
                if gi == 3:
                    for half in range(2):
                        own, other = (slice(0, 64), slice(64, P))[::1 - 2 * half]
                        a.did(nc.scalar.activation(self.nk[own, 2 * n + half, :], self.ps[own, b, :], ACT.Copy), "k_hi")
                    v.wait("k_hi", "c_part")
                    for half in range(2):
                        own, other = (slice(0, 64), slice(64, P))[::1 - 2 * half]
                        v.did(nc.vector.tensor_tensor(self.nk_lo[:, 2 * n + half, :], self.ps[own, b, :],
                                                      self.nk[own, 2 * n + half, :].bitcast(F32), ALU.subtract), f"bank{b}")
                    for half in range(2):
                        own, other = (slice(0, 64), slice(64, P))[::1 - 2 * half]
                        v.did(nc.vector.tensor_copy(self.nk[other, 2 * n + half, :],
                                                    self.nk[own, 2 * n + half, :].bitcast(F32)), "nk")
                elif kind == "feature":
                    dst, tile = dsts[n]
                    s = 0.125 if dst is self.nq else 1.0
                    a.did(nc.scalar.activation(dst[:, 2 * tile, :], self.ps[0:64, b, :], ACT.Copy, scale=s), f"half{b}")
                    v.wait(f"half{b}")
                    v.did(nc.vector.tensor_scalar(dst[:, 2 * tile + 1, :], self.ps[64:128, b, :], s, None,
                                                  ALU.mult), f"bank{b}")
                    if dst is self.nc_kv:
                        self.pr.events["ckv"] = self.pr.events[f"bank{b}"]
                elif gi == 4:
                    v.did(nc.vector.tensor_copy(self.nv[:, n, :], self.ps[:, b, :]), f"bank{b}")
                else:
                    a.did(nc.scalar.activation(self.gate[:, n, :], self.ps[:, b, 0:48], ACT.Sigmoid), f"bank{b}")
            self.U += 4

    def compress_scratch(self):
        nc, v, a = self.nc, self.v, self.a
        at = [self.m_at]

        def tmp(name, shape, dt=F32):
            t = self.sb(name, shape, dt, at=at[0])
            at[0] += (int(np.prod(shape[1:])) * 4 + 31) // 32 * 32
            return t
        self.vbd = tmp("c_vbd", [P, 4, 4, 64])
        self.kc, self.kc_lo = tmp("c_kc", [P, 4, 32], F32R), tmp("c_kc_lo", [64, 4, 32], F32R)
        self.c_hs = tmp("c_hs", [64, 2, 4, 32])
        self.c_peT, self.c_bias = tmp("c_peT", [64, 64]), tmp("c_bias", [64, 2])
        self.c_part = tmp("c_part", [64, 2, 64])
        self.c_prod = tmp("c_prod", [64, 32, 64])
        assert at[0] <= self.m_at + 28672
        v.wait("mod_sum"); a.wait("mod_sum")
        v.did(nc.vector.memset(self.c_hs[:, :, :, :], 0.0), "c_hs0")
        v.did(nc.vector.memset(self.vbd[:, :, :, :], 0.0), "vbd0")

    def compress_pe(self, kv):
        nc, v, p = self.nc, self.v, self.p
        if kv == 0:
            for e in (p, v, self.a):
                e.reach(self.s_c2, self.n_c2)
            p.wait("bank4")
            p.did(nc.tensor.transpose(self.ps[0:64, 4, 0:64], self.pe_rows[:, :], self.c("ident")[0:64, 0:64]), "peT")
            v.wait("peT")
            v.did(nc.vector.tensor_copy(self.c_peT[:, :], self.ps[0:64, 4, 0:64]), "bank4")
            v.wait("bank4")
        else:
            v.wait("c_part")
        v.did(nc.vector.tensor_tensor(self.c_prod[:, :, :], self.w1[:, kv, :, :],
                                      self.c_peT[:, kv * 32:(kv + 1) * 32].unsqueeze(2).broadcast_to([64, 32, 64]),
                                      ALU.mult), "c_prod")
        v.wait("c_prod")
        v.did(nc.vector.tensor_reduce(self.c_part[:, kv, :], self.c_prod[:, :, :].rearrange("p l h -> p h l"),
                                      AX.X, ALU.add), "c_part")

    def compress_bias(self):
        nc, v, p = self.nc, self.v, self.p
        p.wait("c_part", "bank0")
        for kv in range(2):
            ins = nc.tensor.matmul(self.ps[0:64, 0, kv:kv + 1], self.c_part[:, kv, :], self.c("ones")[0:64, 0:1],
                                   start=True, stop=True)
        p.did(ins, "c_bias_p")
        v.wait("c_bias_p")
        v.did(nc.vector.tensor_copy(self.c_bias[:, :], self.ps[0:64, 0, 0:2]), "bank0")
        self.pr.events["c_bias"] = self.pr.events["bank0"]

    def compress_hidden(self, kv):
        nc, a, p = self.nc, self.a, self.p
        p.wait(f"bank{1 + kv}", "ckv")
        for l in range(32):
            ins = nc.tensor.matmul(self.ps[0:64, 1 + kv, 0:124], self.w1[:, kv, l, :],
                                   self.nc_kv[:, 4 * kv:4 * kv + 4, l:l + 16 * 30 + 1:16],
                                   start=l == 0, stop=l == 31)
        p.did(ins, f"hid_c{kv}")
        a.wait(f"hid_c{kv}", "c_bias", "c_hs0")
        a.did(nc.scalar.activation(self.c_hs[:, kv, :, 0:31], self.ps[0:64, 1 + kv, 0:124].rearrange("p (a b) -> p a b", a=4),
                                   ACT.Silu, bias=self.c_bias[:, kv:kv + 1]), f"bank{1 + kv}")

    def compress_out(self):
        nc, v, p, hs = self.nc, self.v, self.p, self.c_hs
        p.wait("bank0", "bank1", "bank2", "bank3")
        ins = nc.tensor.matmul(self.ps[0:64, 0, 0:128], self.w2[:, 0, :], hs[:, 0, :, :], start=True, stop=True)
        p.did(ins, "kc_p")
        for j in range(4):
            for gr in range(4):
                ins = nc.tensor.matmul(self.ps[32 * j:32 * j + 31, 3, gr * 64:(gr + 1) * 64], hs[:, 1, gr, 0:31],
                                       self.w2[:, 1, :], start=True, stop=True)
        p.did(ins, "vc_p")
        kc_p = self.ps[0:64, 0, 0:128].rearrange("p (a b) -> p a b", a=4)
        self.a.wait("kc_p")
        self.a.did(nc.scalar.activation(self.kc[0:64, :, :], kc_p, ACT.Copy), "kc_hi")
        v.wait("kc_hi")
        v.did(nc.vector.tensor_tensor(self.kc_lo[:, :, :], kc_p, self.kc[0:64, :, :].bitcast(F32), ALU.subtract), "bank0")
        v.did(nc.vector.tensor_copy(self.kc[64:P, :, :], self.kc[0:64, :, :].bitcast(F32)), "kc")
        v.wait("vc_p", "vbd0")
        for j in range(4):
            v.did(nc.vector.tensor_copy(self.vbd[32 * j:32 * j + 31, :, j, :],
                                        self.ps[32 * j:32 * j + 31, 3, 0:256].rearrange("p (g d) -> p g d", g=4)), "bank3")

    def nsa_mix(self):
        nc, v, a, p, g = self.nc, self.v, self.a, self.p, self.g
        at = [self.h_at]

        def tmp(name, shape, dt=F32):
            t = self.sb(name, shape, dt, at=at[0])
            at[0] += (int(np.prod(shape[1:])) * 4 + 31) // 32 * 32
            assert at[0] <= self.h_at + 32768
            return t
        at[0] = self.attention_scratch("n", at[0], self.arena + 49152 + 9216)
        qst = [tmp(f"n_q{j}", [P, 4, S], F32R) for j in range(2)]
        bs = [tmp(f"n_b{j}", [P, S]) for j in range(2)]
        o_tok = self.sb("o_tok", [P, TT, D], at=self.arena + 74752)
        base = self.arena + 49152
        spc, self_bc, pT, ot1 = (self.sb(f"n_x{i}", [P, S], at=base + i * 2048) for i in range(4))
        st = self.sb("n_stat", [P, 8, 16], at=base + 8192)
        cm, rc, fc = st[:, 0, :], st[:, 1, :], st[:, 2, :]
        mxs = self.sb("n_mx", [P, 8], at=base + 8192 + 512)
        rs = self.sb("n_rs", [P, 2, 4, 2], at=base + 8192 + 576)
        fac = self.sb("n_fac", [P, 2, 4, 2], at=base + 8192 + 640)
        C, Cc, slope, ok = self.c2["dist"], self.c2["dist_c"], self.c2["slope"], self.c2["seen"]
        O = [4, 5]
        s3 = spc[:, :].rearrange("p (r n) -> p r n", n=32)
        self.forget("qst0", "qst1", "q_hi0", "q_hi1", "q_used0", "q_used1", "b_used0", "b_used1", "osum", *self.ATTEND_EVENTS)
        for e in (a, v, p, g):
            for n in range(8):
                e.wait(f"bank{n}")
        p.wait("nk", "kc")

        def body(ii):
            blocks = []
            for gg in range(2):
                group_blocks(ii * 2 + gg, gg, blocks)
            self.attend(blocks, mxs)
            for jb in range(2):
                self.pr.events[f"b_used{jb}"] = self.pr.events["osum"]

        def group_blocks(i, gg, blocks):
            qs = qst[gg]

            def queries():
                q4 = self.nq[:, bass.ds(4 * i, 4), :]
                a.wait(f"q_used{gg}", f"cs{gg}")
                a.did(nc.scalar.activation(qs[0:64, :, :], q4, ACT.Copy), f"q_hi{gg}")
                v.wait(f"q_hi{gg}")
                v.did(nc.vector.tensor_tensor(qs[64:P, :, :], q4, qs[0:64, :, :].bitcast(F32), ALU.subtract), f"qst{gg}")

            def compressed_scores():
                p.wait(f"qst{gg}", "bank6")
                p.settle(True)
                for t in range(TT):
                    for j in range(4):
                        c0 = (t * 4 + j) * 32
                        tok = slice(t * P, (t + 1) * P)
                        nc.tensor.matmul(self.ps[:, 6, c0:c0 + 32], qs[:, j, tok], self.kc[:, bass.ds(i, 1), :],
                                         start=True, stop=False)
                        ins = nc.tensor.matmul(self.ps[:, 6, c0:c0 + 32], qs[0:64, j, tok],
                                               self.kc_lo[:, bass.ds(i, 1), :], start=False, stop=True)
                p.did(ins, f"cs{gg}")
                v.wait("cT")
                for j in range(4):
                    dst = self_bc[:, :].rearrange("p (t j n) -> p t j n", t=TT, j=4)[:, :, j, :]
                    v.did(nc.vector.tensor_scalar(dst, Cc.rearrange("p (t n) -> p t n", t=TT),
                                                  slope[:, bass.ds(4 * i + j, 1)], None, ALU.mult), "bc")
                v.wait("bc", f"cs{gg}")
                v.did(nc.vector.tensor_tensor(spc[:, :], self.ps[:, 6, :], self_bc[:, :], ALU.add), "bank6")
                v.wait("bank6")
                v.did(nc.vector.tensor_reduce(cm, s3, AX.X, ALU.max), "cm")
                v.wait("cm")
                v.did(nc.vector.tensor_tensor(s3, s3, cm.unsqueeze(2).broadcast_to([P, 16, 32]), ALU.subtract), "cm")
                a.wait("cm")
                a.did(nc.scalar.activation(spc[:, :], spc[:, :], ACT.Exp), "ce")

            def compressed_turn():
                v.wait("ce")
                v.did(nc.vector.tensor_reduce(rc, s3, AX.X, ALU.add), "cm")
                v.wait("cm")
                v.did(nc.vector.reciprocal(rc, rc), "cm")
                v.wait("cm")
                v.did(nc.vector.tensor_tensor(rc, rc, ok, ALU.mult), "cm")
                v.wait("cm")
                gt = self.gate[:, :, bass.ds(12 * i, 12)].rearrange("p t (j b) -> p t j b", b=3)
                v.did(nc.vector.tensor_tensor(fc.rearrange("p (t j) -> p t j", t=TT), rc.rearrange("p (t j) -> p t j", t=TT),
                                              gt[:, :, :, 0], ALU.mult), "fc")
                p.wait("ce", "bank7")
                for t in range(TT):
                    ins = nc.tensor.transpose(self.ps[:, 7, t * P:(t + 1) * P], spc[:, t * P:(t + 1) * P], self.c("ident"))
                p.did(ins, "cT")
                a.wait("cT", "cv")
                a.did(nc.scalar.activation(pT[:, :], self.ps[:, 7, :], ACT.Copy), "bank7")

            def compressed_values():
                p.wait("bank7", "bank6")
                for t in range(TT):
                    b = 7 if t < 2 else 6
                    ins = nc.tensor.matmul(self.ps[:, b, (t % 2) * 256:(t % 2) * 256 + 256], pT[:, t * P:(t + 1) * P],
                                           self.vbd[:, bass.ds(i, 1), :, :], start=True, stop=True)
                p.did(ins, "cv")
                v.wait("cv", "fc")
                for half in range(2):
                    dst = o_tok[:, 2 * half:2 * half + 2, bass.ds(256 * i, 256)].rearrange("p t (j d) -> p t j d", j=4)
                    src = self.ps[:, 7 - half, :].rearrange("p (t j d) -> p t j d", t=2, j=4)
                    f = fc.rearrange("p (t j) -> p t j", t=TT)[:, 2 * half:2 * half + 2, :].unsqueeze(3).broadcast_to([P, 2, 4, 64])
                    v.did(nc.vector.tensor_tensor(dst, src, f, ALU.mult), f"bank{7 - half}")

            nothing = lambda: None
            n0 = len(blocks)
            hooks = {2: compressed_scores, 4: compressed_turn, 7: compressed_values}
            if gg:
                blocks[n0 - 3]["before"] = queries
            else:
                queries()

            def used():
                self.pr.events[f"q_used{gg}"] = self.pr.events["qk1"]
            for j in range(4):
                jb = j % 2

                def make_bias(j=j, jb=jb):
                    v.wait(f"b_used{jb}")
                    v.did(nc.vector.tensor_scalar(bs[jb][:, :], C, slope[:, bass.ds(4 * i + j, 1)], None,
                                                  ALU.mult), f"bias{jb}")

                def combine(j=j, jb=jb):
                    v.wait("exp_of_block")
                    v.did(nc.vector.reciprocal(fac[:, jb, :, :], rs[:, jb, :, :]), "fac")
                    v.wait("fac")
                    gj = self.gate[:, :, bass.ds(12 * i + 3 * j + 1, 2)]
                    v.did(nc.vector.tensor_tensor(fac[:, jb, :, :], fac[:, jb, :, :], gj, ALU.mult), "fac")
                    v.wait("fac", "pv")
                    for br in range(2):
                        src = self.ps[:, O[jb], :].rearrange("p (t b d) -> p t b d", t=TT, b=2)[:, :, br, :]
                        f = fac[:, jb, :, br:br + 1].broadcast_to([P, TT, 64])
                        t3 = ot1[:, br * 256:(br + 1) * 256].rearrange("p (t d) -> p t d", t=TT)
                        v.did(nc.vector.tensor_tensor(t3, src, f, ALU.mult), f"ot{br}")
                    self.pr.events[f"bank{O[jb]}"] = self.pr.events["ot1"]
                    for br in range(2):
                        t3 = ot1[:, br * 256:(br + 1) * 256].rearrange("p (t d) -> p t d", t=TT)
                        o = o_tok[:, :, bass.ds(256 * i + 64 * j, 64)]
                        v.wait(f"ot{br}", "bank6", "osum")
                        v.did(nc.vector.tensor_tensor(o, o, t3, ALU.add), "osum")
                for br in range(2):
                    for t in range(TT):
                        first, last = br == 0 and t == 0, br == 1 and t == TT - 1
                        blocks.append(dict(
                            n=t + 1, qk=[(qs[:, j, t * P:(t + 1) * P], self.nk[:, bass.ds(i + 4 * br, 1), 0:(t + 1) * P]),
                                         (qs[0:64, j, t * P:(t + 1) * P],
                                          self.nk_lo[:, bass.ds(i + 4 * br, 1), 0:(t + 1) * P])],
                            bias=bs[jb][:, (3 - t) * P:S], bias_ready=(f"bias{jb}",), ready=(f"qst{gg}",),
                            v=lambda s, br=br: self.nv[:, s, bass.ds(64 * i + 256 * br, 64)],
                            out=self.ps[:, O[jb], (t * 2 + br) * 64:(t * 2 + br) * 64 + 64],
                            out_ready=(f"bank{O[jb]}",), rs=rs[:, jb, t, br:br + 1],
                            before=make_bias if first else hooks.get(len(blocks) - n0, nothing),
                            after_q=used if j == 3 and last else nothing,
                            done=combine if last else nothing))
        self.pr.run_loop("nsa_heads", 2, body)
        for e in (a, v, p):
            e.wait("osum", "qst0", "qst1", "pv")
        self.token_to_h(o_tok, 0, KD)

    def token_to_h(self, src, first, count):
        nc = self.nc
        for n in range(count):
            kt, b = first + n, n % 4
            self.p.wait(f"bank{b}")
            for t in range(TT):
                ins = nc.tensor.transpose(self.ps[:, b, t * P:(t + 1) * P], src[:, t, n * P:(n + 1) * P], self.c("ident"))
            self.p.did(ins, f"oT{b}")
            self.a.wait(f"oT{b}")
            self.a.did(nc.scalar.activation(self.h_hi[:, kt, :], self.ps[:, b, :], ACT.Copy), f"hh{b}")
            self.v.wait(f"hh{b}")
            self.v.did(nc.vector.tensor_tensor(self.h_lo[:, kt, :], self.ps[:, b, :], self.h_hi[:, kt, :].bitcast(F32),
                                               ALU.subtract), f"h{kt}")
            self.pr.events[f"bank{b}"] = self.pr.events[f"h{kt}"]

    def dsa_weights(self):
        nc, io, at = self.nc, self.io, self.arena + 89344
        self.pool_w = self.sb("pool_w", [P, 4, P], at=at)
        self.qk_gain = self.sb("qk_gain", [P, 2, 64], at=at + 2048)
        nc.scalar.dma_start(self.pool_w[:, :, :], io["pool_w_2"][0].rearrange("g c d -> c g d")).then_inc(self.s_c2, 16)
        for n, name in enumerate(("q_norm_2", "k_norm_2")):
            nc.scalar.dma_start(self.qk_gain[:, n, :], io[name].partition_broadcast(P)
                                if len(io[name].shape) == 1 else io[name][0].partition_broadcast(P)) \
                .then_inc(self.s_c2, 16)
        self.n_c2 += 48

    def dsa_in(self):
        nc, v, a, w, ar = self.nc, self.v, self.a, self.io["w_in_2"][0], self.arena
        self.tq = self.sb("dsa_q", [P, TT, S], at=ar)
        self.tk = self.sb("dsa_k", [P, TT, S], at=ar + 8192)
        self.tv = self.sb("dsa_v", [P, TT, S], at=ar + 16384)
        self.ti = self.sb("dsa_i", [P, TT, 324], at=ar + 24576)
        self.mask = self.sb("dsa_mask", [P, 10 * P], at=ar + 29760)
        self.qT = self.sb("dsa_qT", [64, 8, S], at=ar + 34880)
        self.kT = self.sb("dsa_kT", [P, 8, S], F32R, at=ar + 51264)
        self.kT_lo = self.sb("dsa_kT_lo", [64, 8, S], F32R, at=self.m_at)
        self.iT = self.sb("dsa_iT", [64, 5, S], at=ar + 67648)
        self.u = self.sb("dsa_u", [P, 4, S], at=ar + 77888)
        groups = [("token", 1536, 324, self.ti), ("token", 0, 512, self.tq), ("token", 512, 512, self.tk),
                  ("token", 1024, 512, self.tv), ("feature", 1860, 512, self.u)]
        self.dsa_scratch()
        rounds = iter([(t, n) for t in range(1, TT) for n in range(P // 8)])

        def top_k_rounds(count):
            for _ in range(count):
                self.top_k_round(*next(rounds))
        beside = {1: [lambda: self.index_heads(), lambda: None, lambda: self.index_scores(1),
                      lambda: (self.index_scores(2), self.index_scores(3), top_k_rounds(3))],
                  2: [lambda: (self.head_norm(0), top_k_rounds(3))] + 3 * [lambda: top_k_rounds(4)],
                  3: [lambda: (self.head_norm(1), top_k_rounds(3)), lambda: top_k_rounds(4), lambda: top_k_rounds(4),
                      lambda: (self.heads_out(self.tq, 8, self.qT, 0.125, 0, "rot_q"), top_k_rounds(4))],
                  4: 3 * [lambda: top_k_rounds(4)] + [lambda: (self.heads_out(self.tk, 8, self.kT, 1.0, 6, "rot_k",
                                                                              self.kT_lo),
                                                               top_k_rounds(3))]}
        for gi, (kind, c0, width, dst) in enumerate(groups):
            banks = range(4 * (gi % 2), 4 * (gi % 2) + 4)
            self.group(0, 0, banks, lambda u: self.k_tiles(w, u, slice(c0, c0 + width)), kind=kind, width=width,
                       extra=(lambda u, gi=gi: beside[gi][u]()) if gi in beside else None)
            for n, b in enumerate(banks):
                e = (a, v)[n % 2]
                if n < 2:
                    self.group_done(e, 3)
                src = self.ps[:, b, 0:width]
                e.did(nc.scalar.activation(dst[:, n, :], src, ACT.Copy) if e is a
                      else nc.vector.tensor_copy(dst[:, n, :], src), f"bank{b}")
                self.pr.events[f"g{gi}_{n}"] = self.pr.events[f"bank{b}"]
            self.U += 4
        assert next(rounds, None) is None

    def dsa_scratch(self):
        nc, at = self.nc, self.m_at
        self.rt = [self.sb(f"rt{j}", [P, 1024], at=at + j * 4096) for j in range(4)]
        self.relu = [self.sb(f"relu{j}", [P, S], at=at + 16384 + j * 2048) for j in range(2)]
        self.sq_qk = self.sb("dsa_sq", [P, TT, S], at=self.arena + 51264)
        self.ss = self.sb("dsa_ss", [P, 2, 32], at=self.arena + 86080)
        self.tabs = self.sb("dsa_tab", [P, 4, P], at=self.arena + 86080 + 256)
        self.mask_off = [0, P, 3 * P, 6 * P]
        self.n_scores = 0
        self.v.reach(self.s_c2, self.n_c2)

    def rotate(self, e, x, heads, half, tables, name):
        x1, x2 = x[:, :, :, 0:half], x[:, :, :, half:2 * half]
        t = [b[:, 0:TT * heads * half].rearrange("p (t h d) -> p t h d", t=TT, h=heads) for b in self.rt]
        c1, s2, c2, s1 = tables

        def wide(tb):
            return tb.rearrange("p (t d) -> p t d", t=TT).unsqueeze(2).broadcast_to([P, TT, heads, half])
        e.did(e.e.tensor_tensor(t[0], x1, wide(c1), ALU.mult), name)
        e.did(e.e.tensor_tensor(t[1], x2, wide(s2), ALU.mult), name)
        e.did(e.e.tensor_tensor(t[2], x2, wide(c2), ALU.mult), name)
        e.did(e.e.tensor_tensor(t[3], x1, wide(s1), ALU.mult), name)
        e.wait(name)
        e.did(e.e.tensor_tensor(x1, t[0], t[1], ALU.subtract), name)
        e.did(e.e.tensor_tensor(x2, t[2], t[3], ALU.add), name)

    def heads_out(self, x, heads, dst, scale, base, ready, low=None):
        for h in range(heads):
            b = base + h % 2
            self.p.wait(f"bank{b}", ready)
            for t in range(TT):
                ins = self.nc.tensor.transpose(self.ps[0:64, b, t * P:(t + 1) * P], x[:, t, h * 64:(h + 1) * 64],
                                               self.c("ident"))
            self.p.did(ins, f"ho{b}")
            self.a.wait(f"ho{b}")
            self.a.did(self.nc.scalar.activation(dst[0:64, h, :], self.ps[0:64, b, :], ACT.Copy, scale=scale), f"bank{b}")
            if low is not None:
                self.v.wait(f"bank{b}")
                self.v.did(self.nc.vector.tensor_tensor(low[:, h, :], self.ps[0:64, b, :], dst[0:64, h, :].bitcast(F32),
                                                        ALU.subtract), f"bank{b}")
                self.v.did(self.nc.vector.tensor_copy(dst[64:P, h, :], dst[0:64, h, :].bitcast(F32)), "heads_split")
            self.pr.events["heads"] = self.pr.events[f"bank{b}"]

    def index_heads(self):
        v, ti = self.v, self.ti
        v.wait(*[f"g0_{n}" for n in range(TT)])
        v.did(self.nc.vector.tensor_scalar(ti[:, :, 320:324], ti[:, :, 320:324], (4 ** -0.5) * (64 ** -0.5),
                                           None, ALU.mult), "wi")
        ci, si = self.c2["cos_i"], self.c2["sin_i"]
        self.rotate(v, ti[:, :, 0:320].rearrange("p t (h d) -> p t h d", d=64), 5, 16, (ci, si, ci, si), "rot_i")
        self.heads_out(ti, 5, self.iT, 1.0, 0, "rot_i")
        v.did(self.nc.vector.tensor_copy(self.mask[:, 0:P], self.c2["tri"]), "sc0")

    def index_scores(self, t):
        nc, v, a, p = self.nc, self.v, self.a, self.p
        w = (t + 1) * P
        m = self.mask[:, self.mask_off[t]:self.mask_off[t] + w]
        for h in range(4):
            j = self.n_scores % 2
            self.n_scores += 1
            rl = self.relu[j][:, 0:w]
            p.wait("heads", f"bank{2 + j}")
            p.did(nc.tensor.matmul(self.ps[:, 2 + j, 0:w], self.iT[:, h, t * P:(t + 1) * P], self.iT[:, 4, 0:w],
                                   start=True, stop=True), f"is{j}")
            a.wait(f"is{j}", f"relu_used{j}")
            a.did(nc.scalar.activation(rl, self.ps[:, 2 + j, 0:w], ACT.Relu), f"bank{2 + j}")
            v.wait(f"bank{2 + j}", "wi")
            wc = self.ti[:, t, 320 + h:321 + h]
            if h == 0:
                v.did(nc.vector.tensor_scalar(m, rl, wc, None, ALU.mult), "acc")
            else:
                v.wait("acc")
                v.did(nc.vector.scalar_tensor_tensor(m, rl, wc, m, ALU.mult, ALU.add), "acc")
            self.pr.events[f"relu_used{j}"] = self.pr.events["acc"]
        v.wait("acc")
        v.did(nc.vector.tensor_tensor(m[:, t * P:w], m[:, t * P:w], self.c2["tri"], ALU.add), f"sc{t}")

    def top_k_round(self, t, n):
        nc, v = self.nc, self.v
        m = self.mask[:, self.mask_off[t]:self.mask_off[t] + (t + 1) * P]
        mx8 = self.small[:, 192:200]
        v.wait("mr", f"sc{t}")
        v.did(nc.vector.max(mx8, m), "m8")
        v.wait("m8")
        v.settle(True)
        v.did(nc.vector.match_replace(m, mx8, m, -3.3e38), "mr")
        if n == P // 8 - 1:
            v.wait("mr")
            v.did(nc.vector.tensor_scalar(m, m, -3.2e38, NEG, ALU.is_gt, ALU.mult), "mask")

    def head_norm(self, n):
        nc, v, a, g = self.nc, self.v, self.a, self.g
        x, name = (self.tq, self.tk)[n], ("rot_q", "rot_k")[n]
        gain, sq, ss, tabs = self.qk_gain[:, n, :], self.sq_qk, self.ss[:, n, :], self.tabs
        x4 = x[:, :, :].rearrange("p t (h d) -> p (t h) d", d=64)
        cs, sn = self.c2["cos"], self.c2["sin"]
        ready = [f"g{n + 1}_{t}" for t in range(TT)]
        a.wait("ssum", *ready)
        a.did(nc.scalar.activation(sq[:, :, :], x[:, :, :], ACT.Square), "qsq")
        v.wait("rot_q")
        for k, (tb, off_g) in enumerate(((cs, 0), (sn, 32), (cs, 32), (sn, 0))):
            v.did(nc.vector.tensor_tensor(tabs[:, k, :].rearrange("p (t d) -> p t d", t=TT),
                                          tb.rearrange("p (t d) -> p t d", t=TT),
                                          gain[:, off_g:off_g + 32].unsqueeze(1).broadcast_to([P, TT, 32]),
                                          ALU.mult), "tab")
        v.wait("qsq")
        v.did(nc.vector.tensor_reduce(ss, sq[:, :, :].rearrange("p t (h d) -> p (t h) d", d=64), AX.X, ALU.add), "ssum")
        a.wait("ssum")
        a.did(nc.scalar.activation(ss, ss, ACT.Ln, bias=self.eps, scale=1.0 / 64), "sln")
        a.wait("sln")
        a.did(nc.scalar.activation(ss, ss, ACT.Exp, scale=-0.5), "sln")
        g.wait("sln", "tab", "rot_i", *ready)
        g.did(nc.gpsimd.tensor_tensor(x4, x4, ss.unsqueeze(2).broadcast_to([P, 32, 64]), ALU.mult), name)
        g.wait(name)
        self.rotate(g, x[:, :, :].rearrange("p t (h d) -> p t h d", d=64), 8, 32,
                    [tabs[:, k, :] for k in range(4)], name)

    def dsa_mix(self):
        nc, v, a, p, g = self.nc, self.v, self.a, self.p, self.g
        hb, off = self.h_at, self.mask_off
        bufs = [self.sb(f"pool{j}", [P, 4, S], at=hb + 16384 + j * 8192) for j in range(2)]
        g.wait(*[f"g4_{n}" for n in range(TT)], "heads")
        src = self.u
        for step in range(4):
            sh, dst = 1 << step, bufs[step % 2]
            g.wait("pl")
            g.did(nc.gpsimd.tensor_tensor(dst[:, step:4, sh:S], src[:, step:4, sh:S], src[:, step:4, 0:S - sh], ALU.add))
            g.did(nc.gpsimd.tensor_copy(dst[:, step:4, 0:sh], src[:, step:4, 0:sh]), "pl")
            src = dst
        HEADS = 4
        self.attention_scratch("d", hb, self.m_at + 20480)
        qst = [self.sb(f"d_q{j}", [P, S], F32R, at=hb + 12288 + j * 2048) for j in range(2)]
        o_tok = self.sb("d_o", [P, TT, S], at=self.arena)
        st = self.sb("d_st", [P, 32], at=self.arena + 8192)
        mxs, rs, fac = st[:, 0:6], st[:, 8:16].rearrange("p (j t) -> p j t", j=2), \
            st[:, 16:24].rearrange("p (j t) -> p j t", j=2)
        self.forget("q_used0", "q_used1", *self.ATTEND_EVENTS)
        for e in (a, v, p):
            e.wait("mask", "rot_q", "rot_k", "heads", "heads_split", "relu_used0", "relu_used1", *[f"bank{n}" for n in range(8)])

        def body(i):
            nothing = lambda: None
            blocks = []

            def queries(head):
                j = head % 2
                q1 = self.qT[:, bass.ds(HEADS * i + head, 1), :]
                a.wait(f"q_used{j}")
                a.did(nc.scalar.activation(qst[j][0:64, :].unsqueeze(1), q1, ACT.Copy), f"q_hi{j}")
                v.wait(f"q_hi{j}")
                v.did(nc.vector.tensor_tensor(qst[j][64:P, :].unsqueeze(1), q1, qst[j][0:64, :].bitcast(F32).unsqueeze(1),
                                              ALU.subtract), f"qst{j}")

            for head in range(HEADS):
                j = head % 2

                def combine(j=j, head=head):
                    v.wait("exp_of_block")
                    v.did(nc.vector.reciprocal(fac[:, j, :], rs[:, j, :]), "fac")
                    v.wait("fac", "pv")
                    v.did(nc.vector.tensor_tensor(o_tok[:, :, bass.ds(64 * HEADS * i + 64 * head, 64)],
                                                  self.ps[:, 4 + j, 0:256].rearrange("p (t d) -> p t d", t=TT),
                                                  fac[:, j, :].unsqueeze(2).broadcast_to([P, TT, 64]), ALU.mult),
                          f"bank{4 + j}")

                def used(j=j):
                    self.pr.events[f"q_used{j}"] = self.pr.events["qk1"]
                for t in range(TT):
                    before = nothing
                    if t == 1 and head + 1 < HEADS:
                        before = lambda head=head: queries(head + 1)
                    elif t == 0 and head == 0:
                        before = lambda: queries(0)
                    blocks.append(dict(
                        n=t + 1, qk=[(qst[j][:, t * P:(t + 1) * P], self.kT[:, bass.ds(HEADS * i + head, 1), 0:(t + 1) * P]),
                                     (qst[j][0:64, t * P:(t + 1) * P],
                                      self.kT_lo[:, bass.ds(HEADS * i + head, 1), 0:(t + 1) * P])],
                        bias=self.mask[:, off[t]:off[t] + (t + 1) * P], bias_ready=(), ready=(f"qst{j}",),
                        v=lambda s, head=head: self.tv[:, s, bass.ds(64 * HEADS * i + 64 * head, 64)],
                        out=self.ps[:, 4 + j, t * 64:t * 64 + 64], out_ready=(f"bank{4 + j}",),
                        rs=rs[:, j, t:t + 1], before=before,
                        after_q=used if t == TT - 1 else nothing,
                        done=combine if t == TT - 1 else nothing))
            self.attend(blocks, mxs)
        self.pr.run_loop("dsa_heads", 8 // HEADS, body)
        for e in (a, v, p):
            e.wait("bank4", "bank5", "qst0", "qst1", "pv")
        v.wait("pl")
        for n in range(4):
            d, uu = bufs[n % 2][:, n, :], self.u[:, n, :]
            v.did(nc.vector.tensor_tensor(d[:, 0:16], d[:, 0:16], self.c2["corr"][:, n * 16:(n + 1) * 16],
                                          ALU.mult), f"pc{n}")
        for n in range(4):
            d, uu = bufs[n % 2][:, n, :], self.u[:, n, :]
            v.wait(f"pc{n}")
            v.did(nc.vector.scalar_tensor_tensor(uu, d, 1.0 / (2 << n), uu, ALU.mult, ALU.subtract), f"pooled{n}")
        for e in (a, v):
            e.wait("pooled3")
        self.token_to_h(o_tok, 0, 4)
        p.wait("pooled3")
        for n in range(4):
            b = 4 + n
            p.wait(f"bank{b}")
            p.did(nc.tensor.matmul(self.ps[:, b, :], self.pool_w[:, n, :], self.u[:, n, :], start=True, stop=True), f"pw{n}")
            v.wait(f"pw{n}")
            v.did(nc.vector.tensor_scalar(self.u[:, n, :], self.ps[:, b, :], self.pool_scale[:, n:n + 1], None,
                                          ALU.mult), f"bank{b}")
            a.wait(f"bank{b}")
            a.did(nc.scalar.activation(self.h_hi[:, 4 + n, :], self.u[:, n, :], ACT.Copy), f"hh{n}")
            v.wait(f"hh{n}")
            v.did(nc.vector.tensor_tensor(self.h_lo[:, 4 + n, :], self.u[:, n, :], self.h_hi[:, 4 + n, :].bitcast(F32),
                                          ALU.subtract), f"h{4 + n}")

    def store_x(self):
        nc = self.nc
        ot = self.sb("out_tok", [P, TT, D], at=self.arena)
        out = self.io["out"].rearrange("b (t p) d -> p (b t) d", p=P)
        for t in range(TT):
            for half in range(2):
                b = (2 * t + half) % 8
                self.p.wait(f"bank{b}", *[f"x{n}" for n in range(KD)])
                for j in range(4):
                    kt = half * 4 + j
                    ins = nc.tensor.transpose(self.ps[:, b, j * P:(j + 1) * P], self.xT[:, kt, t * P:(t + 1) * P],
                                              self.c("ident"))
                self.p.did(ins, "xo")
                self.v.wait("xo")
                self.v.did(nc.vector.tensor_copy(ot[:, t, half * 512:(half + 1) * 512], self.ps[:, b, :]), "ot")
            self.s.wait("ot")
            nc.sync.dma_start(out[:, t:t + 1, :], ot[:, t:t + 1, :]).then_inc(self.s_out, 16)
        nc.sync.wait_ge(self.s_out, 16 * TT)


def program(nc, io, const_at, per_loop):
    K = Kernel(nc, io, const_at, per_loop)
    K.names = iter(range(100))
    K.s_c2 = nc.alloc_semaphore("phase_constants_landed")
    K.n_c2 = 0

    def phase_constants(base, names):
        K.c2 = {}
        for n in names:
            o, w = K.const_at[n]
            t = K.sb(f"c2_{n}", [P, w], at=base)
            base += w * 4
            nc.scalar.dma_start(t[:, :], K.io["const2"][:, o:o + w]).then_inc(K.s_c2, 16)
            K.n_c2 += 16
            K.c2[n] = t[:, :]
    K.phase_constants = phase_constants
    K.start()
    K.lower_bounds()
    phase_constants(K.arena + 81920, [f"level{m}" for m in range(8)] + ["restart"])
    K.prologue()
    K.modulation_scales(0)
    K.norm_apply(lambda kt: K.mod[:, 0, 1, kt:kt + 1], lambda kt: K.mod[:, 0, 0, kt:kt + 1], ("ms01", "mod00"))
    K.hgrn_in()
    K.hgrn_mix()
    K.mod_add(0, range(2, 6), 7)
    K.modulation_scales(0)
    K.v.wait("mod_sum")
    K.norm_scratch(K.arena)
    K.out_proj(K.io["hg_w_out"][0], lambda kt: K.mod[:, 0, 2, kt:kt + 1], ("mod02",),
               extra=lambda u: K.mod_unit(1, 5, u, K.m_acc[:, 0, :], u))
    K.M += 8
    K.norm(lambda kt: K.mod[:, 0, 4, kt:kt + 1], lambda kt: K.mod[:, 0, 3, kt:kt + 1], ("ms04", "mod03"))
    K.mod_finish(1, 5, 0, 0)
    K.v.wait("mod_sum")
    K.ffn("ffn_a", K.io["ffn_w_up"][0][:, 0:FF], K.io["ffn_w_up"][0][:, FF:2 * FF], K.io["ffn_w_down"][0],
          lambda kt: K.mod[:, 0, 5, kt:kt + 1], conv=K.conv[0], need=("mod05",),
          extra=lambda i, m: K.mod_unit(1, i, m, K.m_acc[:, bass.ds(i, 1), :], m, 8))
    for part in range(2):
        K.mod_finish(1, part, part, 4 + part)
    K.modulation_scales(1)
    K.norm_sums()
    K.a.wait("rstd")
    phase_constants(K.arena + 91136, ["dist", "dist_c", "slope", "seen"])
    K.nsa_weights()
    K.norm_apply(lambda kt: K.mod[:, 1, 1, kt:kt + 1], lambda kt: K.mod[:, 1, 0, kt:kt + 1], ("ms11", "mod10"))
    K.mod_sums(range(2, 5), 6)
    K.mod_add(1, range(2, 5), 6)
    K.modulation_scales(1)
    K.nsa_in()
    K.nsa_mix()
    K.norm_scratch(K.arena)
    K.out_proj(K.io["nsa_w_out"][0], lambda kt: K.mod[:, 1, 2, kt:kt + 1], ("mod12",))
    K.norm(lambda kt: K.mod[:, 1, 4, kt:kt + 1], lambda kt: K.mod[:, 1, 3, kt:kt + 1], ("ms14", "mod13"))
    K.ffn("ffn_b", K.io["ffn_w_up"][1][:, 0:FF], K.io["ffn_w_up"][1][:, FF:2 * FF], K.io["ffn_w_down"][1],
          lambda kt: K.mod[:, 1, 5, kt:kt + 1], conv=K.conv[1], need=("mod15",))
    K.norm(lambda kt: K.norms["final_norm"][:, kt:kt + 1], None, (), into_x=True)
    K.norm(lambda kt: K.norms["ffn1_norm_2"][:, kt:kt + 1], None, ())
    K.ffn("ffn_c", K.io["ffn1_w_gate_2"][0], K.io["ffn1_w_up_2"][0], K.io["ffn1_w_down_2"][0], lambda kt: 0.5)
    K.norm_sums()
    K.a.wait("rstd")
    phase_constants(K.arena + 91904, ["cos", "sin", "cos_i", "sin_i", "tri", "corr"])
    K.dsa_weights()
    K.norm_apply(lambda kt: K.norms["mix_norm_2"][:, kt:kt + 1], None, ())
    K.dsa_in()
    K.dsa_mix()
    K.norm_scratch(K.arena)
    K.out_proj(K.io["w_out_2"][0], lambda kt: 1.0, ())
    K.norm(lambda kt: K.norms["ffn2_norm_2"][:, kt:kt + 1], None, ())
    K.ffn("ffn_d", K.io["ffn2_w_gate_2"][0], K.io["ffn2_w_up_2"][0], K.io["ffn2_w_down_2"][0], lambda kt: 0.5,
          squares=False)
    return K.finish()


_OUT = (1, S, D)


def kernel(**inputs):
    import concourse.bacc as bacc
    from concourse.bass_utils import run_bass_kernel_spmd
    table, const_at = constants()
    small = const_at["ones"][0] + P
    arrays = {"const": np.ascontiguousarray(table[:, :small]), "const2": table}
    arrays.update({n: np.ascontiguousarray(a) for n, a in inputs.items()})

    def build(per_loop):
        nc = bacc.Bacc("TRN2", target_bir_lowering=False, num_devices=1)
        io = {}
        for n, a in arrays.items():
            io[n] = nc.dram_tensor("in_" + n, a.shape, mybir.dt.from_np(a.dtype), kind="ExternalInput").ap()
        io["out"] = nc.dram_tensor("out", _OUT, F32, kind="ExternalOutput").ap()
        return nc, program(nc, io, const_at, per_loop)
    _, counts = build({})
    nc, _ = build(counts)
    r = run_bass_kernel_spmd(nc, [{"in_" + n: a for n, a in arrays.items()}], core_ids=[0])
    return r.results[0]["out"]
```
